# Optimizing a Trainium2 kernel written in Bass

```python
import functools
import jax
import jax.numpy as jnp
from jax import lax
import numpy as np

D_MODEL = 1024
BATCH = 1
SEQ = 1024
DEPTH = 1
DEC_BATCH = 8
DEC_SEQ = 1
PAST_LEN = 2048
PAGE_SIZE = 128

FFN_DIM = 2816
RWKV_HEADS = 8
RWKV_HEAD = 64
RWKV_DIM = RWKV_HEADS * RWKV_HEAD
DECAY_LORA = 64
ICLR_LORA = 64
GATE_LORA = 128
RWKV_PROJ = 3 * RWKV_DIM + DECAY_LORA + ICLR_LORA + GATE_LORA
LNX_EPS = 64e-5
MLA_HEADS = 8
QK_NOPE = 64
QK_ROPE = 32
V_HEAD = 64
Q_LORA = 768
KV_LORA = 256
CACHE_W = KV_LORA + QK_ROPE
MLA_SCALE = (QK_NOPE + QK_ROPE) ** -0.5
ROPE_BASE = 10000.0
Q_BLOCK = 128
MEM_TOKENS = 256
MEM_HEADS = 4
MEM_HEAD_DIM = 128
MEM_DIM = MEM_HEADS * MEM_HEAD_DIM
N_BRANCH = 3
IN_PROJ = RWKV_PROJ + Q_LORA + KV_LORA + QK_ROPE + MEM_DIM + N_BRANCH * D_MODEL
IN_SPLITS = (RWKV_PROJ,
             RWKV_PROJ + Q_LORA,
             RWKV_PROJ + Q_LORA + KV_LORA,
             RWKV_PROJ + Q_LORA + KV_LORA + QK_ROPE,
             RWKV_PROJ + Q_LORA + KV_LORA + QK_ROPE + MEM_DIM)
RWKV_SPLITS = (RWKV_DIM, 2 * RWKV_DIM, 3 * RWKV_DIM,
               3 * RWKV_DIM + DECAY_LORA, 3 * RWKV_DIM + DECAY_LORA + ICLR_LORA)
RMS_EPS = 1e-6
PAGE_POOL_SPARE = 4

kernel_name = 'hybrid_rwkv7_mla_memory_macaron_step'

WEIGHT_NAMES = (
    'ffn1_pre', 'ffn1_post', 'ffn1_gate', 'ffn1_up', 'ffn1_down',
    'mix_pre', 'mix_post', 'w_in',
    'rwkv_mu', 'rwkv_w0', 'rwkv_w2', 'rwkv_a0', 'rwkv_a2', 'rwkv_g2',
    'rwkv_k_k', 'rwkv_k_a', 'rwkv_r_k', 'rwkv_lnx_g', 'rwkv_lnx_b', 'rwkv_w_o',
    'mla_q_norm', 'mla_w_qb', 'mla_kv_norm', 'mla_w_uk', 'mla_w_uv', 'mla_w_o',
    'mem_norm', 'mem_w_k', 'mem_w_v', 'mem_w_o',
    'w_out',
    'ffn2_pre', 'ffn2_post', 'ffn2_gate', 'ffn2_up', 'ffn2_down',
)

def rmsnorm(x, g):
    xf = x.astype(jnp.float32)
    xf = xf * lax.rsqrt(jnp.mean(xf * xf, axis=-1, keepdims=True) + RMS_EPS)
    return (xf * g.astype(jnp.float32)).astype(x.dtype)

def swiglu_half(x, pre, post, w_gate, w_up, w_down):
    h = rmsnorm(x, pre)
    y = (jax.nn.silu(h @ w_gate) * (h @ w_up)) @ w_down
    return x + 0.5 * rmsnorm(y, post)

def rope(x, pos):
    half = x.shape[-1] // 2
    freqs = ROPE_BASE ** (-jnp.arange(half, dtype=jnp.float32) / half)
    ang = pos.astype(jnp.float32)[:, None] * freqs
    ang = ang.reshape((ang.shape[0],) + (1,) * (x.ndim - 3) + (half,))
    cos, sin = jnp.cos(ang), jnp.sin(ang)
    x1 = x[..., :half].astype(jnp.float32)
    x2 = x[..., half:].astype(jnp.float32)
    return jnp.concatenate([x1 * cos - x2 * sin, x1 * sin + x2 * cos], axis=-1).astype(x.dtype)

def rwkv_scan(r, decay, k, v, a_vec, b_vec, s0):
    xs = tuple(jnp.moveaxis(t.astype(jnp.float32), 1, 0) for t in (r, decay, k, v, a_vec, b_vec))

    def step(s, inp):
        r_t, w_t, k_t, v_t, a_t, b_t = inp
        sa = jnp.einsum('bhij,bhj->bhi', s, a_t)
        s = s * w_t[:, :, None, :] + sa[..., None] * b_t[:, :, None, :] + v_t[..., None] * k_t[:, :, None, :]
        return s, jnp.einsum('bhij,bhj->bhi', s, r_t)

    s, o = lax.scan(step, s0.astype(jnp.float32), xs)
    return jnp.moveaxis(o, 0, 1), s

def rwkv_branch(p, shift0, s0, W):
    B, T, _ = p.shape
    prev = jnp.concatenate([shift0[:, None, :].astype(p.dtype), p[:, :-1]], axis=1)
    ps = p + (prev - p) * W['rwkv_mu']
    r, k, v, wl, al, gl = jnp.split(ps, RWKV_SPLITS, axis=-1)
    w_log = -jax.nn.softplus(-(W['rwkv_w0'] + jnp.tanh(wl) @ W['rwkv_w2']).astype(jnp.float32)) - 0.5
    decay = jnp.exp(-jnp.exp(w_log))
    a = jax.nn.sigmoid(W['rwkv_a0'] + al @ W['rwkv_a2'])
    g = jax.nn.sigmoid(gl) @ W['rwkv_g2']

    def heads(t):
        return t.reshape(B, T, RWKV_HEADS, RWKV_HEAD)

    kk = heads(k * W['rwkv_k_k']).astype(jnp.float32)
    kk = kk / jnp.maximum(jnp.sqrt(jnp.sum(kk * kk, axis=-1, keepdims=True)), 1e-12)
    k = k * (1.0 + (a - 1.0) * W['rwkv_k_a'])
    rh, kh, vh = heads(r), heads(k), heads(v)
    o, s = rwkv_scan(rh, heads(decay), kh, vh, -kk, kk * heads(a).astype(jnp.float32), s0)
    mean = jnp.mean(o, axis=-1, keepdims=True)
    var = jnp.mean(jnp.square(o - mean), axis=-1, keepdims=True)
    o = ((o - mean) * lax.rsqrt(var + LNX_EPS)).reshape(B, T, RWKV_DIM)
    o = o * W['rwkv_lnx_g'].astype(jnp.float32) + W['rwkv_lnx_b'].astype(jnp.float32)
    bonus = jnp.sum((rh * kh * W['rwkv_r_k']).astype(jnp.float32), axis=-1, keepdims=True) * vh.astype(jnp.float32)
    o = (o + bonus.reshape(B, T, RWKV_DIM)).astype(p.dtype)
    return (o * g) @ W['rwkv_w_o'], p[:, -1], s.astype(s0.dtype)

def mem_kv(mem, W):
    B, M, _ = mem.shape
    m = rmsnorm(mem, W['mem_norm'])
    k = (m @ W['mem_w_k']).reshape(B, M, MEM_HEADS, MEM_HEAD_DIM)
    v = (m @ W['mem_w_v']).reshape(B, M, MEM_HEADS, MEM_HEAD_DIM)
    return k, v

def mem_attend(q, mem_k, mem_v):
    B, T, _ = q.shape
    q = q.reshape(B, T, MEM_HEADS, MEM_HEAD_DIM)
    s = jnp.einsum('bqhd,bkhd->bhqk', q, mem_k).astype(jnp.float32) * (MEM_HEAD_DIM ** -0.5)
    prob = jax.nn.softmax(s, axis=-1).astype(mem_v.dtype)
    return jnp.einsum('bhqk,bkhd->bqhd', prob, mem_v).reshape(B, T, MEM_DIM)

def prompt_attend(q_lat, q_pe, c_kv, k_pe):
    B, T, H, L = q_lat.shape
    nb = T // Q_BLOCK
    ql = jnp.moveaxis(q_lat.reshape(B, nb, Q_BLOCK, H, L), 1, 0)
    qp = jnp.moveaxis(q_pe.reshape(B, nb, Q_BLOCK, H, QK_ROPE), 1, 0)
    key_pos = jnp.arange(T)

    def block(args):
        i, ql_b, qp_b = args
        q_pos = i * Q_BLOCK + jnp.arange(Q_BLOCK)
        mask = key_pos[None, :] <= q_pos[:, None]
        s = (jnp.einsum('bqhl,bkl->bhqk', ql_b, c_kv)
             + jnp.einsum('bqhr,bkr->bhqk', qp_b, k_pe)).astype(jnp.float32) * MLA_SCALE
        s = jnp.where(mask, s, -jnp.inf)
        prob = jax.nn.softmax(s, axis=-1).astype(c_kv.dtype)
        return jnp.einsum('bhqk,bkl->bqhl', prob, c_kv)

    ctx = lax.map(block, (jnp.arange(nb), ql, qp))
    return jnp.moveaxis(ctx, 0, 1).reshape(B, T, H, L)

def sample_attend(q_lat, q_pe, c_kv, k_pe, pool, page_table):
    DB, T = q_lat.shape[0], q_lat.shape[1]
    past = pool[page_table].reshape(DB, -1, CACHE_W)
    p_lat, p_pe = past[..., :KV_LORA], past[..., KV_LORA:]
    s_past = jnp.einsum('bqhl,bkl->bhqk', q_lat, p_lat) + jnp.einsum('bqhr,bkr->bhqk', q_pe, p_pe)
    s_new = jnp.einsum('bqhl,bkl->bhqk', q_lat, c_kv) + jnp.einsum('bqhr,bkr->bhqk', q_pe, k_pe)
    causal = jnp.tril(jnp.ones((T, T), dtype=bool))
    s_new = jnp.where(causal, s_new.astype(jnp.float32), -jnp.inf)
    s = jnp.concatenate([s_past.astype(jnp.float32), s_new], axis=-1) * MLA_SCALE
    prob = jax.nn.softmax(s, axis=-1).astype(c_kv.dtype)
    n_past = p_lat.shape[1]
    return (jnp.einsum('bhqk,bkl->bqhl', prob[..., :n_past], p_lat)
            + jnp.einsum('bhqk,bkl->bqhl', prob[..., n_past:], c_kv))

def layer(x, pos, shift0, wkv0, mem_k, mem_v, attend, W):
    B, T, _ = x.shape
    h = swiglu_half(x, W['ffn1_pre'], W['ffn1_post'], W['ffn1_gate'], W['ffn1_up'], W['ffn1_down'])
    u = rmsnorm(h, W['mix_pre'])
    p = u @ W['w_in']
    p_rwkv, c_q, c_kv, k_pe, q_mem, gate_logits = jnp.split(p, IN_SPLITS, axis=-1)
    o_rwkv, shift_new, wkv_new = rwkv_branch(p_rwkv, shift0, wkv0, W)
    q = (rmsnorm(c_q, W['mla_q_norm']) @ W['mla_w_qb']).reshape(B, T, MLA_HEADS, QK_NOPE + QK_ROPE)
    q_pe = rope(q[..., QK_NOPE:], pos)
    q_lat = jnp.einsum('bthn,lhn->bthl', q[..., :QK_NOPE], W['mla_w_uk'])
    c_kv = rmsnorm(c_kv, W['mla_kv_norm'])
    k_pe = rope(k_pe, pos)
    ctx_lat = attend(q_lat, q_pe, c_kv, k_pe)
    o_mla = jnp.einsum('bthl,lhv->bthv', ctx_lat, W['mla_w_uv']).reshape(B, T, MLA_HEADS * V_HEAD) @ W['mla_w_o']
    o_mem = mem_attend(q_mem, mem_k, mem_v) @ W['mem_w_o']
    g = jax.nn.sigmoid(gate_logits).reshape(B, T, N_BRANCH, D_MODEL)
    merged = g[:, :, 0] * o_rwkv + g[:, :, 1] * o_mla + g[:, :, 2] * o_mem
    h = h + rmsnorm(merged @ W['w_out'], W['mix_post'])
    y = swiglu_half(h, W['ffn2_pre'], W['ffn2_post'], W['ffn2_gate'], W['ffn2_up'], W['ffn2_down'])
    rows = jnp.concatenate([c_kv, k_pe], axis=-1)
    return y, rows, shift_new, wkv_new

def setup_inputs(seed: int = 0) -> dict:
    key = jax.random.key(seed)
    keys = iter(jax.random.split(key, 64))
    f32 = jnp.float32

    def normal(shape, scale):
        return scale * jax.random.normal(next(keys), (DEPTH,) + shape, f32)

    def gain(n):
        return 1.0 + normal((n,), 0.05)

    def uniform(shape, lo, hi):
        return jax.random.uniform(next(keys), (DEPTH,) + shape, f32, lo, hi)

    n_pages = PAST_LEN // PAGE_SIZE
    n_used = DEC_BATCH * n_pages
    n_phys = n_used + n_used // PAGE_POOL_SPARE
    page_table = jax.random.permutation(next(keys), n_phys)[:n_used].reshape(DEC_BATCH, n_pages).astype(jnp.int32)
    return {
        'x_prompt': jax.random.normal(next(keys), (BATCH, SEQ, D_MODEL), f32),
        'x_sample': jax.random.normal(next(keys), (DEC_BATCH, DEC_SEQ, D_MODEL), f32),
        'cache_mla': normal((n_phys, PAGE_SIZE, CACHE_W), 1.0),
        'state_rwkv': normal((DEC_BATCH, RWKV_HEADS, RWKV_HEAD, RWKV_HEAD), 0.5),
        'state_shift': normal((DEC_BATCH, RWKV_PROJ), 1.0),
        'cache_mem_k': normal((DEC_BATCH, MEM_TOKENS, MEM_HEADS, MEM_HEAD_DIM), 1.0),
        'cache_mem_v': normal((DEC_BATCH, MEM_TOKENS, MEM_HEADS, MEM_HEAD_DIM), 1.0),
        'page_table': page_table,
        'mem_prompt': jax.random.normal(next(keys), (BATCH, MEM_TOKENS, D_MODEL), f32),
        'ffn1_pre': gain(D_MODEL),
        'ffn1_post': gain(D_MODEL),
        'ffn1_gate': normal((D_MODEL, FFN_DIM), D_MODEL ** -0.5),
        'ffn1_up': normal((D_MODEL, FFN_DIM), D_MODEL ** -0.5),
        'ffn1_down': normal((FFN_DIM, D_MODEL), FFN_DIM ** -0.5),
        'mix_pre': gain(D_MODEL),
        'mix_post': gain(D_MODEL),
        'w_in': normal((D_MODEL, IN_PROJ), D_MODEL ** -0.5),
        'rwkv_mu': uniform((RWKV_PROJ,), 0.0, 1.0),
        'rwkv_w0': uniform((RWKV_DIM,), -5.0, -0.5),
        'rwkv_w2': normal((DECAY_LORA, RWKV_DIM), 0.1 * DECAY_LORA ** -0.5),
        'rwkv_a0': normal((RWKV_DIM,), 0.1),
        'rwkv_a2': normal((ICLR_LORA, RWKV_DIM), ICLR_LORA ** -0.5),
        'rwkv_g2': normal((GATE_LORA, RWKV_DIM), GATE_LORA ** -0.5),
        'rwkv_k_k': 0.85 + normal((RWKV_DIM,), 0.05),
        'rwkv_k_a': 1.0 + normal((RWKV_DIM,), 0.05),
        'rwkv_r_k': normal((RWKV_HEADS, RWKV_HEAD), 0.1),
        'rwkv_lnx_g': gain(RWKV_DIM),
        'rwkv_lnx_b': normal((RWKV_DIM,), 0.01),
        'rwkv_w_o': normal((RWKV_DIM, D_MODEL), RWKV_DIM ** -0.5),
        'mla_q_norm': gain(Q_LORA),
        'mla_w_qb': normal((Q_LORA, MLA_HEADS * (QK_NOPE + QK_ROPE)), Q_LORA ** -0.5),
        'mla_kv_norm': gain(KV_LORA),
        'mla_w_uk': normal((KV_LORA, MLA_HEADS, QK_NOPE), KV_LORA ** -0.5),
        'mla_w_uv': normal((KV_LORA, MLA_HEADS, V_HEAD), KV_LORA ** -0.5),
        'mla_w_o': normal((MLA_HEADS * V_HEAD, D_MODEL), (MLA_HEADS * V_HEAD) ** -0.5),
        'mem_norm': gain(D_MODEL),
        'mem_w_k': normal((D_MODEL, MEM_DIM), D_MODEL ** -0.5),
        'mem_w_v': normal((D_MODEL, MEM_DIM), D_MODEL ** -0.5),
        'mem_w_o': normal((MEM_DIM, D_MODEL), MEM_DIM ** -0.5),
        'w_out': normal((D_MODEL, D_MODEL), D_MODEL ** -0.5),
        'ffn2_pre': gain(D_MODEL),
        'ffn2_post': gain(D_MODEL),
        'ffn2_gate': normal((D_MODEL, FFN_DIM), D_MODEL ** -0.5),
        'ffn2_up': normal((D_MODEL, FFN_DIM), D_MODEL ** -0.5),
        'ffn2_down': normal((FFN_DIM, D_MODEL), FFN_DIM ** -0.5),
    }

def reference(x_prompt, x_sample, cache_mla, state_rwkv, state_shift, cache_mem_k, cache_mem_v,
              page_table, mem_prompt,
              ffn1_pre, ffn1_post, ffn1_gate, ffn1_up, ffn1_down,
              mix_pre, mix_post, w_in,
              rwkv_mu, rwkv_w0, rwkv_w2, rwkv_a0, rwkv_a2, rwkv_g2,
              rwkv_k_k, rwkv_k_a, rwkv_r_k, rwkv_lnx_g, rwkv_lnx_b, rwkv_w_o,
              mla_q_norm, mla_w_qb, mla_kv_norm, mla_w_uk, mla_w_uv, mla_w_o,
              mem_norm, mem_w_k, mem_w_v, mem_w_o,
              w_out,
              ffn2_pre, ffn2_post, ffn2_gate, ffn2_up, ffn2_down):
    stacked = (ffn1_pre, ffn1_post, ffn1_gate, ffn1_up, ffn1_down,
               mix_pre, mix_post, w_in,
               rwkv_mu, rwkv_w0, rwkv_w2, rwkv_a0, rwkv_a2, rwkv_g2,
               rwkv_k_k, rwkv_k_a, rwkv_r_k, rwkv_lnx_g, rwkv_lnx_b, rwkv_w_o,
               mla_q_norm, mla_w_qb, mla_kv_norm, mla_w_uk, mla_w_uv, mla_w_o,
               mem_norm, mem_w_k, mem_w_v, mem_w_o,
               w_out,
               ffn2_pre, ffn2_post, ffn2_gate, ffn2_up, ffn2_down)
    B, S, _ = x_prompt.shape
    DB, T, _ = x_sample.shape
    pos_p = jnp.arange(S)
    pos_s = PAST_LEN + jnp.arange(T)
    shift_zero = jnp.zeros((B, RWKV_PROJ), x_prompt.dtype)
    wkv_zero = jnp.zeros((B, RWKV_HEADS, RWKV_HEAD, RWKV_HEAD), state_rwkv.dtype)
    x_p, x_s = x_prompt, x_sample
    rows_p, rows_s, wkv_p, wkv_s, sh_p, sh_s, mk_p, mv_p = [], [], [], [], [], [], [], []
    for l in range(DEPTH):
        W = {name: w[l] for name, w in zip(WEIGHT_NAMES, stacked)}
        mk, mv = mem_kv(mem_prompt, W)
        x_p, r_p, s_p, st_p = layer(x_p, pos_p, shift_zero, wkv_zero, mk, mv, prompt_attend, W)
        attend_s = functools.partial(sample_attend, pool=cache_mla[l], page_table=page_table)
        x_s, r_s, s_s, st_s = layer(x_s, pos_s, state_shift[l], state_rwkv[l],
                                    cache_mem_k[l], cache_mem_v[l], attend_s, W)
        rows_p.append(r_p)
        rows_s.append(r_s)
        wkv_p.append(st_p)
        wkv_s.append(st_s)
        sh_p.append(s_p)
        sh_s.append(s_s)
        mk_p.append(mk)
        mv_p.append(mv)
    mla_rows_prompt = jnp.stack(rows_p)
    mla_rows_sample = jnp.stack(rows_s)
    rwkv_prompt = jnp.stack(wkv_p)
    rwkv_sample = jnp.stack(wkv_s)
    shift_prompt = jnp.stack(sh_p)
    shift_sample = jnp.stack(sh_s)
    mem_k_prompt = jnp.stack(mk_p)
    mem_v_prompt = jnp.stack(mv_p)
    return (x_p, x_s, mla_rows_prompt, mla_rows_sample, rwkv_prompt, rwkv_sample,
            shift_prompt, shift_sample, mem_k_prompt, mem_v_prompt)


_drawn_inputs = setup_inputs


def setup_inputs(seed=0):
    import zlib

    import numpy as np

    out = dict(_drawn_inputs(seed))
    spreads = {}
    factors = {'rwkv_w2': 8.0, 'rwkv_lnx_b': 8.0, 'mla_q_norm': 8.0, 'ffn2_post': 3.659}
    for name, (base, spread) in spreads.items():
        noise = np.random.default_rng([zlib.crc32(name.encode()), seed]).standard_normal(out[name].shape)
        drawn = base * np.exp(spread * noise) if base else spread * noise
        out[name] = jnp.asarray(drawn.astype(out[name].dtype))
    for name, factor in factors.items():
        out[name] = (out[name] * factor).astype(out[name].dtype)
    return out
```

```python
import numpy as np
import concourse.bass as bass
from concourse import mybir
from contextlib import ExitStack

F32 = mybir.dt.float32
ALU = mybir.AluOpType
ACT = mybir.ActivationFunctionType
AX = mybir.AxisListType

P = 128
D = 1024
DT = D // P
SEQ = 1024
DEC = 8
T = SEQ + DEC
NT = 3
TG = T // NT
FFN = 2816
FT = FFN // P
RMS_EPS = 1e-6


class Count:

    def __init__(self, k, name):
        self.sem = k.nc.alloc_semaphore(name=name)
        k.semaphores.append(self.sem)
        self.n = 0

    def up(self, instruction, by=1):
        instruction.then_inc(self.sem, by)
        self.n += by
        return self.n


class Kit:
    pass


def stage(program):
    def whole(k, *args, **kwargs):
        before, k.semaphores = k.semaphores, []
        program(k, *args, **kwargs)
        k.nc.clear_and_free_semaphores(k.semaphores)
        k.nc.all_engine_barrier()
        k.semaphores = before
    return whole


def grp(g):
    return slice(g * TG, (g + 1) * TG)



@stage
def load_constants(k):
    nc = k.nc
    landed = Count(k, "constants_landed")
    with nc.Block() as block:
        @block.sync
        def _(sp):
            for dst, src in k.const_loads:
                landed.up(sp.dma_start(dst, src), 16)
            sp.wait_ge(landed.sem, landed.n)

        @block.gpsimd
        def _(pool):
            pass


@stage
def load_x(k):
    nc = k.nc
    n_tiles = SEQ // P
    tiles_landed = [Count(k, f"x_tile_landed{s}") for s in range(2)]
    transposed = Count(k, "x_quads_transposed")
    drained = Count(k, "x_quads_drained")
    stage = k.W
    bank = [k.ps[s][:, :].rearrange("p (f t) -> p f t", f=4) for s in range(4)]

    def src(i):
        return k.io["x_prompt"][0, bass.ds(i * P, P), :]

    with nc.Block() as block:
        @block.sync
        def _(sp):
            for s in range(2):
                sp.dma_start(stage[:, s, 0:D], src(s)).then_inc(tiles_landed[s].sem, 16)
            with sp.Fori(0, (n_tiles - 2) // 2) as pair:
                i = pair * 2
                for s in range(2):
                    sp.wait_ge(transposed.sem, 2 * i + 2 * (s + 1))
                    sp.dma_start(stage[:, s, 0:D], src(i + 2 + s)).then_inc(tiles_landed[s].sem, 16)
            sp.wait_ge(transposed.sem, 2 * (n_tiles - 1))
            sp.dma_start(stage[0:DEC, 0, 0:D], k.io["x_sample"].rearrange("b o d -> (b o) d"))\
                .then_inc(tiles_landed[0].sem, 16)

        @block.tensor
        def _(pe):
            with pe.Fori(0, n_tiles // 2) as pair:
                i = pair * 2
                for s in range(2):
                    pe.wait_ge(tiles_landed[s].sem, 8 * i + 16)
                    for q in range(2):
                        pe.wait_ge(drained.sem, 2 * i + 2 * s + q + 1)
                        for f in range(4):
                            ins = nc.tensor.transpose(bank[2 * s + q][:, f, :],
                                                      stage[:, s, (4 * q + f) * P:(4 * q + f + 1) * P],
                                                      k.ident[:, :])
                        ins.then_inc(transposed.sem, 1)
            pe.wait_ge(tiles_landed[0].sem, 16 * (n_tiles // 2 + 1))
            for q in range(2):
                pe.wait_ge(drained.sem, 2 * n_tiles + q + 1)
                for f in range(4):
                    ins = nc.tensor.transpose(bank[q][:, f, 0:DEC],
                                              stage[0:DEC, 0, (4 * q + f) * P:(4 * q + f + 1) * P],
                                              k.ident[0:DEC, 0:DEC])
                ins.then_inc(transposed.sem, 1)

        @block.vector
        def _(dve):
            dve.sem_inc(drained.sem, 4)
            with dve.Fori(0, n_tiles // 2) as pair:
                i = pair * 2
                for s in range(2):
                    for q in range(2):
                        dve.wait_ge(transposed.sem, 2 * i + 2 * s + q + 1)
                        nc.vector.tensor_copy(k.A[:, 4 * q:4 * q + 4, bass.ds((i + s) * P, P)],
                                              bank[2 * s + q]).then_inc(drained.sem, 1)
            for q in range(2):
                dve.wait_ge(transposed.sem, 2 * n_tiles + q + 1)
                nc.vector.tensor_copy(k.A[:, 4 * q:4 * q + 4, SEQ:T], bank[q][:, :, 0:DEC])\
                    .then_inc(drained.sem, 1)


@stage
def store_y(k, src):
    nc = k.nc
    n_tiles = SEQ // P
    transposed = Count(k, "y_quads_transposed")
    drained = Count(k, "y_quads_drained")
    stored = [Count(k, f"y_stored{s}") for s in range(2)]
    stage = k.W
    bank = [k.ps[s][:, :].rearrange("p (f t) -> p f t", f=4) for s in range(4)]
    copied = Count(k, "y_lhs_copied")
    lhs = k.C[:, 0:2, 0:D].rearrange("p s (f t) -> p s f t", f=DT)

    with nc.Block() as block:
        @block.gpsimd
        def _(pool):
            with pool.Fori(0, n_tiles // 2) as pair:
                i = pair * 2
                for s in range(2):
                    pool.wait_ge(transposed.sem, 2 * i + 2 * s + 2)
                    nc.gpsimd.tensor_copy(lhs[:, s], src[:, :, bass.ds((i + s) * P, P)]).then_inc(copied.sem, 1)

        @block.tensor
        def _(pe):
            pe.sem_inc(transposed.sem, 4)
            with pe.Fori(0, n_tiles // 2) as pair:
                i = pair * 2
                for s in range(2):
                    pe.wait_ge(copied.sem, i + s + 1)
                    for q in range(2):
                        pe.wait_ge(drained.sem, 2 * i + 2 * s + q + 1)
                        for f in range(4):
                            ins = nc.tensor.transpose(bank[2 * s + q][:, f, :], lhs[:, s, 4 * q + f, :],
                                                      k.ident[:, :])
                        ins.then_inc(transposed.sem, 1)
            for q in range(2):
                pe.wait_ge(drained.sem, 2 * n_tiles + q + 1)
                for f in range(4):
                    ins = nc.tensor.transpose(bank[q][0:DEC, f, :], src[:, 4 * q + f, SEQ:T], k.ident[:, :])
                ins.then_inc(transposed.sem, 1)

        @block.vector
        def _(dve):
            dve.sem_inc(drained.sem, 4)
            with dve.Fori(0, n_tiles // 2) as pair:
                i = pair * 2
                for s in range(2):
                    dve.wait_ge(stored[s].sem, 8 * i + 16)
                    for q in range(2):
                        dve.wait_ge(transposed.sem, 2 * i + 2 * s + q + 1 + 4)
                        nc.vector.tensor_copy(stage[:, s, 512 * q:512 * (q + 1)],
                                              bank[2 * s + q].rearrange("p f t -> p (f t)"))\
                            .then_inc(drained.sem, 1)
            dve.wait_ge(stored[0].sem, 16 * (n_tiles // 2 + 1))
            for q in range(2):
                dve.wait_ge(transposed.sem, 2 * n_tiles + q + 1 + 4)
                nc.vector.tensor_copy(stage[0:DEC, 0, 512 * q:512 * (q + 1)],
                                      bank[q][0:DEC].rearrange("p f t -> p (f t)")).then_inc(drained.sem, 1)

        @block.sync
        def _(sp):
            for s in range(2):
                sp.sem_inc(stored[s].sem, 16)
            with sp.Fori(0, n_tiles // 2) as pair:
                i = pair * 2
                for s in range(2):
                    sp.wait_ge(drained.sem, 2 * i + 2 * (s + 1) + 4)
                    sp.dma_start(k.io["y_prompt"][0, bass.ds((i + s) * P, P), :], stage[:, s, 0:D])\
                        .then_inc(stored[s].sem, 16)
            sp.wait_ge(drained.sem, 2 * n_tiles + 2 + 4)
            sp.dma_start(k.io["y_sample"].rearrange("b o d -> (b o) d"), stage[0:DEC, 0, 0:D])\
                .then_inc(stored[0].sem, 16)
            sp.wait_ge(stored[0].sem, 16 * (n_tiles // 2 + 2))
            sp.wait_ge(stored[1].sem, 16 * (n_tiles // 2 + 1))


@stage
def rms_norm(k, name, src, n, gain, dst=None, residual=None, half=1.0, cols=T):
    nc = k.nc
    squared = Count(k, name + "_squared")
    summed = Count(k, name + "_summed")
    rooted = Count(k, name + "_rooted")
    inverted = Count(k, name + "_inverted")
    scaled = Count(k, name + "_scaled")
    groups = [(g, slice(g * TG, min((g + 1) * TG, cols))) for g in range((cols + TG - 1) // TG)]
    ng = len(groups)
    with nc.Block() as block:
        @block.scalar
        def _(act):
            for f in range(n):
                if f >= 2:
                    act.wait_ge(summed.sem, f - 1)
                nc.scalar.activation(k.sq[:, f % 2, 0:cols], src[:, f, 0:cols], ACT.Square)\
                    .then_inc(squared.sem, 1)
            act.wait_ge(summed.sem, n)
            for g, s in groups:
                w = s.stop - s.start
                nc.scalar.activation(k.rs[:, s], k.ps[g][:, 0:w], ACT.Sqrt, scale=1.0 / (n * P),
                                     bias=k.eps_col[:, 0:1]).then_inc(rooted.sem, 1)

        @block.tensor
        def _(pe):
            for f in range(n):
                pe.wait_ge(squared.sem, f + 1)
                for g, s in groups:
                    ins = nc.tensor.matmul(k.ps[g][:, 0:s.stop - s.start], k.ones[:, :], k.sq[:, f % 2, s],
                                           start=(f == 0), stop=(f == n - 1))
                ins.then_inc(summed.sem, 1)

        @block.vector
        def _(dve):
            for i, (g, s) in enumerate(groups):
                dve.wait_ge(rooted.sem, i + 1)
                nc.vector.reciprocal(k.rs[:, s], k.rs[:, s]).then_inc(inverted.sem, 1)
            dve.wait_ge(inverted.sem, ng)
            out = src if dst is None else dst
            for f in range(n):
                nc.vector.scalar_tensor_tensor(out=out[:, f, 0:cols], in0=src[:, f, 0:cols],
                                               scalar=gain[:, f:f + 1], in1=k.rs[:, 0:cols],
                                               op0=ALU.mult, op1=ALU.mult).then_inc(scaled.sem, 1)
            if residual is not None:
                for f in range(n):
                    dve.wait_ge(scaled.sem, f + 1)
                    nc.vector.scalar_tensor_tensor(out=residual[:, f, :], in0=out[:, f, :], scalar=half,
                                                   in1=residual[:, f, :], op0=ALU.mult, op1=ALU.add)\
                        .then_inc(scaled.sem, 1)


@stage
def gate_up(k, name, x, w_gate, w_up, hidden):
    nc = k.nc
    landed = [Count(k, f"{name}_weights_landed{s}") for s in range(2)]
    multiplied = Count(k, name + "_multiplied")
    gated = Count(k, name + "_gated")
    silued = Count(k, name + "_silued")
    stored = Count(k, name + "_hidden")
    n = FT
    w = k.W[:, :, 0:2 * D].rearrange("p s (m f c) -> p s m f c", m=2, f=DT)
    srcs = [t.rearrange("(f p) n -> p f n", p=P) for t in (w_gate, w_up)]

    def load(sp, s, i):
        for m in range(2):
            sp.dma_start(w[:, s, m], srcs[m][:, :, bass.ds(i * P, P)]).then_inc(landed[s].sem, 16)

    with nc.Block() as block:
        @block.sync
        def _(sp):
            load(sp, 0, 0)
            load(sp, 1, 1)
            with sp.Fori(0, (n - 2) // 2) as pair:
                i = pair * 2
                for s in range(2):
                    sp.wait_ge(multiplied.sem, NT * i + NT * (s + 1))
                    load(sp, s, i + 2 + s)

        @block.tensor
        def _(pe):
            with pe.Fori(0, n // 2) as pair:
                i = pair * 2
                for s in range(2):
                    pe.wait_ge(landed[s].sem, 16 * i + 32)
                    for g in range(NT):
                        pe.wait_ge(stored.sem, NT * i + NT * s + g + 1)
                        for m in range(2):
                            for f in range(DT):
                                ins = nc.tensor.matmul(k.ps[2 * g + m][:, 0:TG], w[:, s, m, f], x[:, f, grp(g)],
                                                       start=(f == 0), stop=(f == DT - 1))
                        ins.then_inc(multiplied.sem, 1)

        @block.scalar
        def _(act):
            with act.Fori(0, n // 2) as pair:
                i = pair * 2
                for s in range(2):
                    for g in range(NT):
                        act.wait_ge(multiplied.sem, NT * i + NT * s + g + 1)
                        act.wait_ge(stored.sem, NT * i + NT * s + g + 1)
                        nc.scalar.activation(k.t3[:, g, :], k.ps[2 * g][:, 0:TG], ACT.Sigmoid)\
                            .then_inc(gated.sem, 1)

        @block.vector
        def _(dve):
            dve.sem_inc(stored.sem, NT)
            with dve.Fori(0, n // 2) as pair:
                i = pair * 2
                for s in range(2):
                    for g in range(NT):
                        dve.wait_ge(gated.sem, NT * i + NT * s + g + 1)
                        nc.vector.tensor_tensor(k.t3[:, g, :], k.t3[:, g, :], k.ps[2 * g][:, 0:TG], ALU.mult)\
                            .then_inc(silued.sem, 1)
                        dve.wait_ge(silued.sem, NT * i + NT * s + g + 1)
                        nc.vector.tensor_tensor(hidden[:, bass.ds(i + s, 1), grp(g)],
                                                k.t3[:, g, :].rearrange("p (a t) -> p a t", a=1),
                                                k.ps[2 * g + 1][:, 0:TG].rearrange("p (a t) -> p a t", a=1),
                                                ALU.mult).then_inc(stored.sem, 1)


@stage
def project(k, name, x, kt, w_dram, col0, n, out):
    nc = k.nc
    landed = [Count(k, f"{name}_weights_landed{s}") for s in range(2)]
    multiplied = Count(k, name + "_multiplied")
    stored = Count(k, name + "_stored")
    w = k.W[:, :, 0:kt * P].rearrange("p s (f c) -> p s f c", f=kt)
    src = w_dram.rearrange("(f p) n -> p f n", p=P)

    def load(sp, s, i):
        sp.dma_start(w[:, s], src[:, :, bass.ds(col0 + i * P, P)]).then_inc(landed[s].sem, 16)

    with nc.Block() as block:
        @block.sync
        def _(sp):
            load(sp, 0, 0)
            load(sp, 1, 1)
            with sp.Fori(0, (n - 2) // 2) as pair:
                i = pair * 2
                for s in range(2):
                    sp.wait_ge(multiplied.sem, NT * i + NT * (s + 1))
                    load(sp, s, i + 2 + s)

        @block.tensor
        def _(pe):
            with pe.Fori(0, n // 2) as pair:
                i = pair * 2
                for s in range(2):
                    pe.wait_ge(landed[s].sem, 8 * i + 16)
                    for g in range(NT):
                        pe.wait_ge(stored.sem, NT * i + NT * s + g + 1)
                        for f in range(kt):
                            ins = nc.tensor.matmul(k.ps[NT * s + g][:, 0:TG], w[:, s, f], x[:, f, grp(g)],
                                                   start=(f == 0), stop=(f == kt - 1))
                        ins.then_inc(multiplied.sem, 1)

        @block.scalar
        def _(act):
            act.sem_inc(stored.sem, 2 * NT)
            with act.Fori(0, n // 2) as pair:
                i = pair * 2
                for s in range(2):
                    for g in range(NT):
                        act.wait_ge(multiplied.sem, NT * i + NT * s + g + 1)
                        nc.scalar.activation(out[:, bass.ds(i + s, 1), grp(g)],
                                             k.ps[NT * s + g][:, 0:TG].rearrange("p (a t) -> p a t", a=1),
                                             ACT.Copy).then_inc(stored.sem, 1)


def ffn(k, name, pre, post, w_gate, w_up, w_down):
    rms_norm(k, name + "_pre", k.A, DT, pre, dst=k.B)
    gate_up(k, name + "_up", k.B, w_gate, w_up, k.C)
    project(k, name + "_down", k.C, FT, w_down, 0, DT, k.B)
    rms_norm(k, name + "_post", k.B, DT, post, residual=k.A, half=0.5)


class Steps:

    def __init__(self, k, name, steps, primed=False):
        self.sem = k.nc.alloc_semaphore(name=name)
        k.semaphores.append(self.sem)
        self.steps, self.per, self.primed, self.at = list(steps), len(steps), primed, 0

    def prime(self, eng):
        eng.sem_inc(self.sem, self.per)

    def done(self, ins, step):
        assert self.steps[self.at % self.per] == step, (self.steps[self.at % self.per], step)
        self.at += 1
        ins.then_inc(self.sem, 1)

    def wait(self, eng, step, it=0, before=0):
        n = self.steps.index(step) + 1 + self.per * (int(self.primed) - before)
        eng.wait_ge(self.sem, it * self.per + n)


RH, RN = 8, 64
RD = RH * RN
RT = RD // P
RPROJ = 3 * RD + 64 + 64 + 128
RPT = RPROJ // P
CH = 64
NCH = SEQ // CH
LNX_EPS = 64e-5
DECAY = float(np.exp(-0.5))


@stage
def spill(k, name, dst, src):
    landed = Count(k, name)
    with k.nc.Block() as block:
        @block.sync
        def _(sp):
            landed.up(sp.dma_start(dst, src), 16)
            sp.wait_ge(landed.sem, landed.n)


@stage
def rwkv_project(k):
    nc = k.nc
    n = RPT
    landed = [Count(k, f"rwkv_w_landed{s}") for s in range(2)]
    shift_landed = Count(k, "rwkv_shift_landed")
    shift_ready = Count(k, "rwkv_shift_ready")
    multiplied = Count(k, "rwkv_p_multiplied")
    copied = Count(k, "rwkv_p_copied")
    mixed = Count(k, "rwkv_p_mixed")
    chain = Count(k, "rwkv_mix_chain")
    rows_ready = Count(k, "shift_rows_ready")
    rows_copied = Count(k, "shift_rows_copied")
    rows_stored = Count(k, "shift_rows_stored")
    w = k.W[:, :, 0:D].rearrange("p s (f c) -> p s f c", f=DT)
    src = k.io["w_in"][0].rearrange("(f p) n -> p f n", p=P)
    rows = k.W[0:DEC + 1, 0, D:D + RPROJ]
    before = k.sq[:, 1, 0:RPT * DEC].rearrange("p (j b) -> p j b", b=DEC)
    last = k.sq[:, 1, 256:256 + RPT * (DEC + 1)].rearrange("p (j b) -> p j b", b=DEC + 1)
    flat = k.rowbuf
    diff = k.rs

    def load(sp, s, i):
        sp.dma_start(w[:, s], src[:, :, bass.ds(i * P, P)]).then_inc(landed[s].sem, 16)

    with nc.Block() as block:
        @block.sync
        def _(sp):
            load(sp, 0, 0)
            load(sp, 1, 1)
            sp.dma_start(rows[0:DEC, :], k.io["state_shift"][0]).then_inc(shift_landed.sem, 16)
            with sp.Fori(0, (n - 2) // 2) as pair:
                i = pair * 2
                for s in range(2):
                    sp.wait_ge(multiplied.sem, NT * i + NT * (s + 1))
                    load(sp, s, i + 2 + s)
            sp.wait_ge(rows_copied.sem, 4)
            sp.dma_start(k.io["shift_prompt"][0], rows[0:1, :]).then_inc(rows_stored.sem, 16)
            sp.dma_start(k.io["shift_sample"][0], rows[1:DEC + 1, :]).then_inc(rows_stored.sem, 16)
            sp.wait_ge(rows_stored.sem, 32)

        @block.tensor
        def _(pe):
            pe.wait_ge(shift_landed.sem, 16)
            for j in range(n):
                ins = nc.tensor.transpose(k.ps[7][:, j * DEC:(j + 1) * DEC], rows[0:DEC, j * P:(j + 1) * P],
                                          k.ident[0:DEC, 0:DEC])
            ins.then_inc(shift_ready.sem, 1)
            with pe.Fori(0, n // 2) as pair:
                i = pair * 2
                for s in range(2):
                    pe.wait_ge(landed[s].sem, 8 * i + 16)
                    for g in range(NT):
                        pe.wait_ge(copied.sem, NT * i + NT * s + g + 1)
                        for f in range(DT):
                            ins = nc.tensor.matmul(k.ps[NT * s + g][:, 0:TG], w[:, s, f], k.B[:, f, grp(g)],
                                                   start=(f == 0), stop=(f == DT - 1))
                        ins.then_inc(multiplied.sem, 1)
            pe.wait_ge(mixed.sem, 1 + n)
            pe.wait_ge(copied.sem, NT * n + 2 * NT)
            for q in range(4):
                for j in range(4 * q, min(4 * q + 4, n)):
                    ins = nc.tensor.transpose(k.ps[q][0:DEC + 1, (j % 4) * P:(j % 4 + 1) * P], last[:, j, :],
                                              k.ident[:, :])
                ins.then_inc(rows_ready.sem, 1)

        @block.scalar
        def _(act):
            act.sem_inc(copied.sem, 2 * NT)
            with act.Fori(0, n // 2) as pair:
                i = pair * 2
                for s in range(2):
                    act.wait_ge(mixed.sem, i + s + 1)
                    for g in range(NT):
                        act.wait_ge(multiplied.sem, NT * i + NT * s + g + 1)
                        nc.scalar.activation(flat[:, 1 + g * TG:1 + (g + 1) * TG], k.ps[NT * s + g][:, 0:TG],
                                             ACT.Copy).then_inc(copied.sem, 1)
            for q in range(4):
                act.wait_ge(rows_ready.sem, q + 1)
                wide = min(4 * P, RPROJ - 4 * q * P)
                nc.scalar.activation(rows[:, 4 * q * P:4 * q * P + wide], k.ps[q][0:DEC + 1, 0:wide], ACT.Copy)\
                    .then_inc(rows_copied.sem, 1)

        @block.vector
        def _(dve):
            nc.vector.memset(flat[:, 0:1], 0.0).then_inc(chain.sem, 1)
            dve.wait_ge(chain.sem, 1)
            dve.wait_ge(shift_ready.sem, 1)
            nc.vector.tensor_copy(before, k.ps[7][:, 0:n * DEC].rearrange("p (j b) -> p j b", b=DEC))\
                .then_inc(mixed.sem, 1)
            dve.wait_ge(mixed.sem, 1)
            with dve.Fori(0, n) as j:
                dve.wait_ge(copied.sem, NT * j + NT + 2 * NT)
                nc.vector.tensor_tensor(diff[:, 0:SEQ], flat[:, 0:SEQ], flat[:, 1:SEQ + 1], ALU.subtract)\
                    .then_inc(chain.sem, 1)
                nc.vector.tensor_tensor(diff[:, SEQ:T].rearrange("p (a b) -> p a b", a=1),
                                        before[:, bass.ds(j, 1), :],
                                        flat[:, SEQ + 1:T + 1].rearrange("p (a b) -> p a b", a=1), ALU.subtract)\
                    .then_inc(chain.sem, 1)
                nc.vector.tensor_copy(k.mu_now[:, 0:1], k.mu[:, bass.ds(j, 1)]).then_inc(chain.sem, 1)
                nc.vector.tensor_copy(last[:, bass.ds(j, 1), :],
                                      flat[:, SEQ:T + 1].rearrange("p (a b) -> p a b", a=1)).then_inc(chain.sem, 1)
                dve.wait_ge(chain.sem, 4 * j + 5)
                nc.vector.scalar_tensor_tensor(out=k.C[:, bass.ds(j, 1), :], in0=diff[:, :].rearrange("p (a t) -> p a t", a=1),
                                               scalar=k.mu_now[:, 0:1],
                                               in1=flat[:, 1:T + 1].rearrange("p (a t) -> p a t", a=1),
                                               op0=ALU.mult, op1=ALU.add).then_inc(mixed.sem, 1)
                dve.wait_ge(mixed.sem, j + 2)


@stage
def rwkv_vectors(k):
    nc = k.nc
    r, kk_, v = k.C[:, 0:4], k.C[:, 4:8], k.C[:, 8:12]
    s_, a_, kn = k.C[:, 14:18], k.C[:, 18:22], k.A[:, 0:4]
    low, gl = k.C[:, 12], k.C[:, 13]
    w2 = k.W[0:64, 0, 0:RD]
    a2 = k.W[64:128, 0, 0:RD]
    J = range(RT)
    G = range(NT)
    pe_s = Steps(k, "vec_products", [(m, j) for j in J for m in "za"] + [("sum", j) for j in J])
    act_s = Steps(k, "vec_functions", ["tanh", "gate"] + [(m, j) for j in J for m in "sa"] +
                  [("root", j) for j in J] + [(m, j) for j in J for m in ("up", "down", "prev")])
    dve_s = Steps(k, "vec_elementwise", [(m, j) for j in J for m in ("sq",)] +
                  [("kn", j) for j in J] + [(m, j) for j in J for m in ("cum", "scaled")])
    chain = Count(k, "vec_chain")
    landed = Count(k, "vec_w_landed")
    resets = k.W[:, 1, 0:SEQ]
    up, down, prev = k.sq[:, 0, 0:SEQ], k.sq[:, 1, 0:SEQ], k.rs[:, 0:SEQ]
    tmp, cum = k.A[:, 4, :], k.A[:, 5, 0:SEQ]
    cumprev = k.A[:, 6, 0:SEQ]

    with nc.Block() as block:
        @block.sync
        def _(sp):
            landed.up(sp.dma_start(w2, k.io["rwkv_w2"][0]), 16)
            landed.up(sp.dma_start(a2, k.io["rwkv_a2"][0]), 16)
            landed.up(sp.dma_start(resets, k.io["c_resets"]), 16)

        @block.tensor
        def _(pe):
            pe.wait_ge(landed.sem, 48)
            act_s.wait(pe, "tanh")
            for j in J:
                if j >= 1:
                    act_s.wait(pe, ("s", j - 1))
                for g in G:
                    ins = nc.tensor.matmul(k.ps[g][:, 0:TG], w2[:, j * P:(j + 1) * P], low[0:64, grp(g)],
                                           start=True, stop=True)
                pe_s.done(ins, ("z", j))
                if j >= 1:
                    act_s.wait(pe, ("a", j - 1))
                for g in G:
                    ins = nc.tensor.matmul(k.ps[3 + g][:, 0:TG], a2[:, j * P:(j + 1) * P], low[64:128, grp(g)],
                                           start=True, stop=True)
                pe_s.done(ins, ("a", j))
            act_s.wait(pe, ("a", RT - 1))
            for j in J:
                dve_s.wait(pe, ("sq", j))
                if j >= 1:
                    act_s.wait(pe, ("root", j - 1))
                for g in G:
                    ins = nc.tensor.matmul(k.ps[g][:, 0:TG], k.headones[:, :], k.A[:, 4 + j, grp(g)],
                                           start=True, stop=True)
                pe_s.done(ins, ("sum", j))

        @block.scalar
        def _(act):
            act_s.done(nc.scalar.activation(low[0:64], low[0:64], ACT.Tanh), "tanh")
            act_s.done(nc.scalar.activation(gl, gl, ACT.Sigmoid), "gate")
            for j in J:
                pe_s.wait(act, ("z", j))
                for g in G:
                    ins = nc.scalar.activation(s_[:, j, grp(g)], k.ps[g][:, 0:TG], ACT.Sigmoid,
                                               bias=k.w0[:, j:j + 1])
                act_s.done(ins, ("s", j))
                pe_s.wait(act, ("a", j))
                for g in G:
                    ins = nc.scalar.activation(a_[:, j, grp(g)], k.ps[3 + g][:, 0:TG], ACT.Sigmoid,
                                               bias=k.a0[:, j:j + 1])
                act_s.done(ins, ("a", j))
            for j in J:
                pe_s.wait(act, ("sum", j))
                for g in G:
                    ins = nc.scalar.activation(k.A[:, 4 + j, grp(g)], k.ps[g][:, 0:TG], ACT.Sqrt)
                act_s.done(ins, ("root", j))
            for j in J:
                dve_s.wait(act, ("cum", j))
                act_s.done(nc.scalar.activation(up, cum, ACT.Exp, scale=-DECAY), ("up", j))
                act_s.done(nc.scalar.activation(down, cum, ACT.Exp, scale=DECAY), ("down", j))
                act_s.done(nc.scalar.activation(prev, cumprev, ACT.Exp, scale=-DECAY), ("prev", j))

        @block.vector
        def _(dve):
            def link(ins):
                chain.up(ins)
                dve.wait_ge(chain.sem, chain.n)

            dve.wait_ge(landed.sem, 48)
            for j in J:
                link(nc.vector.tensor_scalar(kn[:, j], kk_[:, j], k.k_k[:, j:j + 1], None, ALU.mult))
                dve_s.done(nc.vector.tensor_tensor(k.A[:, 4 + j], kn[:, j], kn[:, j], ALU.mult), ("sq", j))
            for j in J:
                act_s.wait(dve, ("root", j))
                norm = k.A[:, 4 + j]
                link(nc.vector.tensor_scalar(norm, norm, 1e-12, None, ALU.max))
                link(nc.vector.reciprocal(norm, norm))
                link(nc.vector.tensor_tensor(kn[:, j], kn[:, j], norm, ALU.mult))
                link(nc.vector.tensor_scalar(norm, a_[:, j], -1.0, k.k_a[:, j:j + 1], ALU.add, ALU.mult))
                link(nc.vector.scalar_tensor_tensor(out=kk_[:, j], in0=norm, scalar=1.0, in1=kk_[:, j],
                                                    op0=ALU.add, op1=ALU.mult))
                dve_s.done(nc.vector.tensor_tensor(a_[:, j], kn[:, j], a_[:, j], ALU.mult), ("kn", j))
            dve_s.wait(dve, ("kn", RT - 1))
            for j in J:
                if j >= 1:
                    act_s.wait(dve, ("prev", j - 1))
                link(nc.vector.tensor_tensor_scan(cum, resets, s_[:, j, 0:SEQ], 0.0,
                                                  ALU.mult, ALU.add))
                dve_s.done(nc.vector.tensor_tensor(cumprev, cum, s_[:, j, 0:SEQ], ALU.subtract), ("cum", j))
                act_s.wait(dve, ("up", j))
                link(nc.vector.tensor_tensor(r[:, j, 0:SEQ], r[:, j, 0:SEQ], up, ALU.mult))
                link(nc.vector.tensor_copy(k.chunk_decay[:, :, j],
                                           up.rearrange("p (c t) -> p c t", t=CH)[:, :, CH - 1]))
                act_s.wait(dve, ("down", j))
                link(nc.vector.tensor_tensor(kk_[:, j, 0:SEQ], kk_[:, j, 0:SEQ], down, ALU.mult))
                link(nc.vector.tensor_tensor(a_[:, j, 0:SEQ], a_[:, j, 0:SEQ], down, ALU.mult))
                act_s.wait(dve, ("prev", j))
                dve_s.done(nc.vector.scalar_tensor_tensor(out=kn[:, j, 0:SEQ], in0=kn[:, j, 0:SEQ], scalar=-1.0,
                                                          in1=prev, op0=ALU.mult, op1=ALU.mult), ("scaled", j))


@stage
def rwkv_scan(k):
    nc = k.nc
    nhead = [(h, q) for h in range(RT) for q in range(2)]
    R2 = range(2)
    LV = [2, 4, 8, 16, 32]
    W0, W1 = k.W[:, 0], k.W[:, 1]
    base = [W0, W1]
    def view(s, at, c):
        return base[s][:, at:at + RT * c].rearrange("p (h c) -> p h c", h=RT)
    AR = [view(s, 0, 128) for s in R2]
    Bt = [view(s, 512, 64) for s in R2]
    Kt = [view(s, 768, 64) for s in R2]
    Vt = [view(s, 1024, 64) for s in R2]
    G1 = [view(s, 1280, 128) for s in R2]
    G2 = [view(s, 1792, 128) for s in R2]
    X = k.rw
    def wide(s, i, c=64):
        return X[:, s, i * 256:i * 256 + RT * c].rearrange("p (h c) -> p h c", h=RT)
    Vm = [view(s, 2304, 64) for s in R2]
    Bm = [view(s, 2560, 64) for s in R2]
    Km = [wide(s, 0) for s in R2]
    NT_ = [wide(s, 1) for s in R2]
    Tm = [wide(s, 2) for s in R2]
    TT = [wide(s, 3) for s in R2]
    Ym = [wide(s, 4) for s in R2]
    Wm = [wide(s, 5) for s in R2]
    Um = [wide(s, 6) for s in R2]
    ST = k.ST
    bank = [[k.ps[4 * s + b][:, :] for b in range(4)] for s in R2]

    def half(b, lo, c):
        return b[:, lo:lo + RT * c].rearrange("p (h c) -> p h c", h=RT)

    pe_s = Steps(k, "scan_products",
                 [(m, s) for s in R2 for m in ("gram", "turned")] +
                 [(m, s, l) for l in LV for m in ("Y", "Z") for s in R2] +
                 [(m, s) for s in R2 for m in ("W", "U", "OS")], primed=True)
    act_s = Steps(k, "scan_copies",
                  [("turned", s) for s in R2] + [("Y", s, l) for l in LV for s in R2] +
                  [(m, s) for s in R2 for m in ("W", "U", "O")], primed=True)
    dve_s = Steps(k, "scan_masks_and_sums",
                  [("gram", s) for s in R2] + [("first", s) for s in R2] +
                  [("T", s, l) for l in LV for s in R2] + [("state", s) for s in R2], primed=True)
    pool_s = Steps(k, "scan_operands", [("load", s) for s in R2] + [("level", s, l) for l in LV for s in R2])
    load_c = Count(k, "scan_loads")
    zeroed = Count(k, "scan_zeroed")
    chain = Count(k, "scan_state_chain")
    settled_at = Count(k, "scan_products_may_start")

    with nc.Block() as block:
        @block.gpsimd
        def _(pool):
            nc.gpsimd.memset(ST[:, :, :], 0.0).then_inc(zeroed.sem, 1)
            with pool.Fori(0, NCH // 2) as it:
                for s in R2:
                    pe_s.wait(pool, ("OS", s), it, before=1)
                    dve_s.wait(pool, ("state", s), it, before=1)
                    at = bass.ds((it * 2 + s) * CH, CH)
                    for src, dst in ((k.A[:, 0:4, at], AR[s][:, :, 0:64]), (k.C[:, 0:4, at], AR[s][:, :, 64:128]),
                                     (k.C[:, 18:22, at], Bt[s]), (k.C[:, 4:8, at], Kt[s]),
                                     (k.C[:, 8:12, at], Vt[s])):
                        nc.gpsimd.tensor_copy(dst, src).then_inc(load_c.sem, 1)
                    pool.wait_ge(load_c.sem, it * 10 + 5 * s + 5)
                    pool_s.done(nc.gpsimd.tensor_copy(k.decay_now[:, s:s + 1, :],
                                                      k.chunk_decay[:, bass.ds(it * 2 + s, 1), :]), ("load", s))
                for l in LV:
                    for s in R2:
                        dve_s.wait(pool, ("gram", s), it)
                        if l > 2:
                            pe_s.wait(pool, ("Y", s, l // 2), it)
                        pool_s.done(nc.gpsimd.tensor_tensor(NT_[s], G1[s][:, :, 0:64], k.level_mask[l], ALU.mult),
                                    ("level", s, l))

        @block.tensor
        def _(pe):
            pe_s.prime(pe)
            pe.wait_ge(zeroed.sem, 1)

            def settled():
                pe.sem_inc(settled_at.sem, 1)

            def mm(out, lhsT, rhs, start=True, stop=True, q=0):
                return nc.tensor.matmul(out, lhsT, rhs, start=start, stop=stop)

            def lane(t, h, q, lo=0, c=64):
                return t[64 * q:64 * q + 64, h, lo:lo + c]

            with pe.Fori(0, NCH // 2) as it:
                for s in R2:
                    b = bank[s]
                    pool_s.wait(pe, ("load", s), it)
                    act_s.wait(pe, ("O", s), it, before=1)
                    dve_s.wait(pe, ("state", s), it, before=1)
                    settled()
                    for h, q in nhead:
                        mm(lane(half(b[0], 0, 128), h, q, 0, 128), lane(Bt[s], h, q), lane(AR[s], h, q, 0, 128))
                    for h, q in nhead:
                        mm(lane(half(b[1], 0, 128), h, q, 0, 128), lane(Kt[s], h, q), lane(AR[s], h, q, 0, 128))
                    for h, q in nhead:
                        ins = mm(lane(half(b[2], 0, 64), h, q), lane(AR[s], h, q), lane(Bt[s], h, q))
                    pe_s.done(ins, ("gram", s))
                    for src, dst in ((Vt[s], half(b[3], 0, 64)), (Bt[s], half(b[3], 256, 64)), (Kt[s], half(b[2], 256, 64))):
                        if src is Kt[s]:
                            dve_s.wait(pe, ("gram", s), it)
                            settled()
                        for h, q in nhead:
                            ins = mm(lane(dst, h, q), lane(src, h, q), k.ident[64 * q:64 * q + 64, 64 * q:64 * q + 64])
                    pe_s.done(ins, ("turned", s))
                for l in LV:
                    for s in R2:
                        b = bank[s]
                        pool_s.wait(pe, ("level", s, l), it)
                        if l == 2:
                            dve_s.wait(pe, ("first", s), it)
                        else:
                            dve_s.wait(pe, ("T", s, l // 2), it)
                        settled()
                        for h, q in nhead:
                            ins = mm(lane(half(b[0], 0, 64), h, q), lane(NT_[s], h, q), lane(Tm[s], h, q))
                        pe_s.done(ins, ("Y", s, l))
                    for s in R2:
                        b = bank[s]
                        act_s.wait(pe, ("Y", s, l), it)
                        settled()
                        for h, q in nhead:
                            mm(lane(half(b[1], 0, 64), h, q), lane(TT[s], h, q), lane(Ym[s], h, q))
                        for h, q in nhead:
                            ins = mm(lane(half(b[1], 256, 64), h, q), lane(Ym[s], h, q), lane(TT[s], h, q))
                        pe_s.done(ins, ("Z", s, l))
                for s in R2:
                    b = bank[s]
                    if s == 1:
                        dve_s.wait(pe, ("state", 0), it)
                    else:
                        dve_s.wait(pe, ("state", 1), it, before=1)
                    act_s.wait(pe, ("turned", s), it)
                    dve_s.wait(pe, ("T", s, LV[-1]), it)
                    settled()
                    for h, q in nhead:
                        mm(lane(half(b[0], 0, 64), h, q), lane(AR[s], h, q), lane(ST, h, q), stop=False)
                        ins = mm(lane(half(b[0], 0, 64), h, q), lane(G2[s], h, q), lane(Vm[s], h, q), start=False)
                    pe_s.done(ins, ("W", s))
                    act_s.wait(pe, ("W", s), it)
                    settled()
                    for h, q in nhead:
                        ins = mm(lane(half(b[1], 0, 64), h, q), lane(TT[s], h, q), lane(Wm[s], h, q))
                    pe_s.done(ins, ("U", s))
                    act_s.wait(pe, ("U", s), it)
                    settled()
                    for h, q in nhead:
                        mm(lane(half(b[3], 0, 64), h, q), lane(Bm[s], h, q), lane(Um[s], h, q), stop=False)
                        mm(lane(half(b[3], 0, 64), h, q), lane(Km[s], h, q), lane(Vm[s], h, q), start=False)
                    for h, q in nhead:
                        o = lane(half(b[2], 0, 64), h, q)
                        mm(o, lane(ST, h, q), lane(AR[s], h, q, 64), stop=False)
                        mm(o, lane(Um[s], h, q), lane(G1[s], h, q, 64), start=False, stop=False)
                        ins = mm(o, lane(Vm[s], h, q), lane(G2[s], h, q, 64), start=False)
                    pe_s.done(ins, ("OS", s))

        @block.scalar
        def _(act):
            act_s.prime(act)
            with act.Fori(0, NCH // 2) as it:
                for s in R2:
                    b = bank[s]
                    pe_s.wait(act, ("turned", s), it)
                    nc.scalar.activation(Vm[s], half(b[3], 0, 64), ACT.Copy)
                    nc.scalar.activation(Bm[s], half(b[3], 256, 64), ACT.Copy)
                    act_s.done(nc.scalar.activation(Km[s], half(b[2], 256, 64), ACT.Copy), ("turned", s))
                for l in LV:
                    for s in R2:
                        pe_s.wait(act, ("Y", s, l), it)
                        act_s.done(nc.scalar.activation(Ym[s], half(bank[s][0], 0, 64), ACT.Copy), ("Y", s, l))
                for s in R2:
                    b = bank[s]
                    pe_s.wait(act, ("W", s), it)
                    act_s.done(nc.scalar.activation(Wm[s], half(b[0], 0, 64), ACT.Copy), ("W", s))
                    pe_s.wait(act, ("U", s), it)
                    act_s.done(nc.scalar.activation(Um[s], half(b[1], 0, 64), ACT.Copy), ("U", s))
                    pe_s.wait(act, ("OS", s), it)
                    act_s.done(nc.scalar.activation(k.C[:, 14:18, bass.ds((it * 2 + s) * CH, CH)],
                                                    half(b[2], 0, 64), ACT.Copy), ("O", s))

        @block.vector
        def _(dve):
            dve_s.prime(dve)
            with dve.Fori(0, NCH // 2) as it:
                for s in R2:
                    b = bank[s]
                    pe_s.wait(dve, ("gram", s), it)
                    pool_s.wait(dve, ("load", s), it)
                    nc.vector.tensor_tensor(G1[s], half(b[0], 0, 128), k.gram_mask, ALU.mult)
                    nc.vector.tensor_tensor(G2[s], half(b[1], 0, 128), k.gram_mask, ALU.mult)
                    dve_s.done(nc.vector.tensor_tensor(Tm[s], half(b[2], 0, 64), k.first_mask, ALU.mult),
                               ("gram", s))
                for s in R2:
                    dve_s.wait(dve, ("gram", s), it)
                    nc.vector.tensor_tensor(TT[s], G1[s][:, :, 0:64], k.first_mask_t, ALU.mult).then_inc(chain.sem, 1)
                    dve.wait_ge(chain.sem, it * 6 + 2 * s + 1)
                    nc.vector.tensor_tensor(Tm[s], Tm[s], k.ident4, ALU.add).then_inc(chain.sem, 1)
                    dve.wait_ge(chain.sem, it * 6 + 2 * s + 2)
                    dve_s.done(nc.vector.tensor_tensor(TT[s], TT[s], k.ident4, ALU.add), ("first", s))
                for l in LV:
                    for s in R2:
                        pe_s.wait(dve, ("Z", s, l), it)
                        if l == 2:
                            dve_s.wait(dve, ("first", s), it)
                        else:
                            dve_s.wait(dve, ("T", s, l // 2), it)
                        nc.vector.tensor_tensor(Tm[s], Tm[s], half(bank[s][1], 0, 64), ALU.add)
                        dve_s.done(nc.vector.tensor_tensor(TT[s], TT[s], half(bank[s][1], 256, 64), ALU.add),
                                   ("T", s, l))
                for s in R2:
                    pe_s.wait(dve, ("OS", s), it)
                    nc.vector.tensor_tensor(ST[:, :, :], ST[:, :, :], half(bank[s][3], 0, 64), ALU.add)\
                        .then_inc(chain.sem, 1)
                    dve.wait_ge(chain.sem, it * 6 + s + 5)
                    dve_s.done(nc.vector.tensor_tensor(ST[:, :, :], ST[:, :, :],
                                                       k.decay_now[:, s, :].unsqueeze(2).to_broadcast([P, RT, RN]),
                                                       ALU.mult), ("state", s))
                    dve_s.wait(dve, ("state", s), it)


@stage
def rwkv_sample_step(k):
    nc = k.nc
    names = "rwkvab"
    srcs = [k.C[:, 0:4], k.C[:, 14:18], k.C[:, 4:8], k.C[:, 8:12], k.A[:, 0:4], k.C[:, 18:22]]
    W = k.W[:, :, :].rearrange("p s c -> p (s c)")
    S = W[:, 0:2048].rearrange("p (i j) -> p i j", j=RN)
    tmp = W[:, 2048:4096].rearrange("p (i j) -> p i j", j=RN)
    rows = k.rwflat[0:DEC, 0:6 * RD].rearrange("p (m c) -> p m c", m=6)
    vec = W[:, 4096:4096 + 6 * 64].rearrange("p (m c) -> p m c", m=6)
    sa = W[:, 4480:4512]
    o = W[:, 4512:4544]
    vrow = W[:, 4544:4576]
    orow = k.rwflat[0:DEC, 0:RD]
    state_landed = Count(k, "state_landed")
    turned = Count(k, "vectors_turned")
    copied = Count(k, "vectors_copied")
    put = Count(k, "vectors_put")
    got = Count(k, "vectors_got")
    decayed = Count(k, "decay_ready")
    chain = Count(k, "step_chain")
    stepped = Count(k, "step_done")
    stored = Count(k, "step_stored")
    o_put = Count(k, "o_put")
    o_got = Count(k, "o_got")
    o_turned = Count(k, "o_turned")
    st_turned = Count(k, "prompt_state_turned")
    st_copied = Count(k, "prompt_state_copied")
    rows2 = k.t_scratch.rearrange("m b c -> b m c")
    state = k.io["state_rwkv"][0].rearrange("b h (x i) j -> (b h x) i j", x=2)
    state_out = k.io["wkv_sample"][0].rearrange("b h (x i) j -> (b h x) i j", x=2)

    with nc.Block() as block:
        @block.sync
        def _(sp):
            sp.dma_start(S, state).then_inc(state_landed.sem, 16)
            sp.wait_ge(copied.sem, 6)
            sp.dma_start(rows2, rows).then_inc(put.sem, 16)
            sp.wait_ge(put.sem, 16)
            for m in range(6):
                src = k.t_scratch[m].rearrange("b (h c) -> (b h) c", c=RN).unsqueeze(1).to_broadcast([64, 2, RN])
                sp.dma_start(vec[:, m], src).then_inc(got.sem, 16)
            sp.dma_start(vrow, k.t_scratch[3].rearrange("b (x c) -> (b x) c", c=32)).then_inc(got.sem, 16)
            sp.wait_ge(st_copied.sem, 1)
            for q in range(2):
                sp.dma_start(k.io["wkv_prompt"][0, 0].rearrange("(h q) i j -> q i h j", q=2)[q],
                             k.st_rows[64 * q:64 * q + 64]).then_inc(stored.sem, 16)
            sp.wait_ge(stepped.sem, 1)
            sp.dma_start(state_out, S).then_inc(stored.sem, 16)
            sp.wait_ge(stepped.sem, 2)
            sp.dma_start(k.o_scratch.rearrange("b (x c) -> (b x) c", c=32), o).then_inc(o_put.sem, 16)
            sp.wait_ge(o_put.sem, 16)
            sp.dma_start(orow, k.o_scratch).then_inc(o_got.sem, 16)
            sp.wait_ge(stored.sem, 48)

        @block.tensor
        def _(pe):
            for m in range(6):
                if m == 1:
                    pe.wait_ge(decayed.sem, 1)
                for j in range(RT):
                    ins = nc.tensor.transpose(k.ps[m][0:DEC, j * P:(j + 1) * P], srcs[m][:, j, SEQ:T], k.ident[:, :])
                ins.then_inc(turned.sem, 1)
            for h in range(RT):
                for q in range(2):
                    l = slice(64 * q, 64 * q + 64)
                    ins = nc.tensor.matmul(k.ps[6][l, h * RN:(h + 1) * RN], k.ST[l, h, :], k.ident[l, l],
                                           start=True, stop=True)
            ins.then_inc(st_turned.sem, 1)
            pe.wait_ge(o_got.sem, 16)
            for j in range(RT):
                ins = nc.tensor.transpose(k.ps[7][:, j * DEC:(j + 1) * DEC], orow[:, j * P:(j + 1) * P],
                                          k.ident[0:DEC, 0:DEC])
            ins.then_inc(o_turned.sem, 1)

        @block.scalar
        def _(act):
            nc.scalar.activation(srcs[1][:, :, SEQ:T], srcs[1][:, :, SEQ:T], ACT.Exp, scale=-DECAY)\
                .then_inc(decayed.sem, 1)
            for m in range(6):
                act.wait_ge(turned.sem, m + 1)
                nc.scalar.activation(rows[:, m], k.ps[m][0:DEC, :], ACT.Copy).then_inc(copied.sem, 1)
            act.wait_ge(st_turned.sem, 1)
            nc.scalar.activation(k.st_rows[:, :, :], k.ps[6][:, 0:RT * RN].rearrange("p (h c) -> p h c", h=RT),
                                 ACT.Copy).then_inc(st_copied.sem, 1)
            act.wait_ge(o_turned.sem, 1)
            nc.scalar.activation(k.C[:, 14:18, SEQ:T], k.ps[7][:, 0:RT * DEC].rearrange("p (j b) -> p j b", b=DEC),
                                 ACT.Copy)

        @block.vector
        def _(dve):
            def link(ins):
                chain.up(ins)
                dve.wait_ge(chain.sem, chain.n)

            def over_rows(m):
                return vec[:, m].unsqueeze(1).to_broadcast([P, 32, RN])

            def over_cols(x):
                return x.unsqueeze(2).to_broadcast([P, 32, RN])

            dve.wait_ge(state_landed.sem, 16)
            dve.wait_ge(got.sem, 7 * 16)
            link(nc.vector.tensor_tensor(tmp, S, over_rows(4), ALU.mult))
            link(nc.vector.tensor_reduce(sa, tmp, AX.X, ALU.add))
            link(nc.vector.tensor_tensor(S, S, over_rows(1), ALU.mult))
            link(nc.vector.tensor_tensor(tmp, over_cols(sa), over_rows(5), ALU.mult))
            link(nc.vector.tensor_tensor(S, S, tmp, ALU.subtract))
            link(nc.vector.tensor_tensor(tmp, over_cols(vrow), over_rows(2), ALU.mult))
            nc.vector.tensor_tensor(S, S, tmp, ALU.add).then_inc(stepped.sem, 1)
            dve.wait_ge(stepped.sem, 1)
            link(nc.vector.tensor_tensor(tmp, S, over_rows(0), ALU.mult))
            nc.vector.tensor_reduce(o, tmp, AX.X, ALU.add).then_inc(stepped.sem, 1)


@stage
def rwkv_finish(k):
    nc = k.nc
    r, kk_, v, gl = k.C[:, 0:4], k.C[:, 4:8], k.C[:, 8:12], k.C[:, 13]
    o, out = k.C[:, 14:18], k.A[:, 4:8]
    J, G = range(RT), range(NT)
    pe_s = Steps(k, "fin_sums", [(m, j) for j in J for m in ("mean", "bonus", "var", "g")])
    act_s = Steps(k, "fin_functions", [(m, j) for j in J for m in ("root", "g")])
    dve_s = Steps(k, "fin_elementwise", [(m, j) for j in J for m in ("rk", "centred", "done")])
    chain = Count(k, "fin_chain")
    landed = Count(k, "g2_landed")
    g2 = k.W[:, 0, 0:RD]
    bonus = k.sq[:, 0, :]
    square = k.sq[:, 1, :]
    with nc.Block() as block:
        @block.sync
        def _(sp):
            sp.dma_start(g2, k.io["rwkv_g2"][0]).then_inc(landed.sem, 16)

        @block.tensor
        def _(pe):
            pe.wait_ge(landed.sem, 16)
            for j in J:
                if j:
                    dve_s.wait(pe, ("done", j - 1))
                for g in G:
                    ins = nc.tensor.matmul(k.ps[g][:, 0:TG], k.headones[:, :], o[:, j, grp(g)], start=True, stop=True)
                pe_s.done(ins, ("mean", j))
                dve_s.wait(pe, ("rk", j))
                for g in G:
                    ins = nc.tensor.matmul(k.ps[3 + g][:, 0:TG], k.headones[:, :], bonus[:, grp(g)], start=True, stop=True)
                pe_s.done(ins, ("bonus", j))
                dve_s.wait(pe, ("centred", j))
                for g in G:
                    ins = nc.tensor.matmul(k.ps[g][:, 0:TG], k.headones[:, :], square[:, grp(g)], start=True, stop=True)
                pe_s.done(ins, ("var", j))
                act_s.wait(pe, ("root", j))
                for g in G:
                    ins = nc.tensor.matmul(k.ps[g][:, 0:TG], g2[:, j * P:(j + 1) * P], gl[:, grp(g)], start=True, stop=True)
                pe_s.done(ins, ("g", j))

        @block.scalar
        def _(act):
            for j in J:
                pe_s.wait(act, ("var", j))
                if j:
                    dve_s.wait(act, ("done", j - 1))
                for g in G:
                    ins = nc.scalar.activation(k.rs[:, grp(g)], k.ps[g][:, 0:TG], ACT.Sqrt, scale=1.0 / RN,
                                               bias=k.lnx_eps[:, 0:1])
                act_s.done(ins, ("root", j))
                pe_s.wait(act, ("g", j))
                if j:
                    dve_s.wait(act, ("done", j - 1))
                for g in G:
                    ins = nc.scalar.activation(k.gbuf[:, grp(g)], k.ps[g][:, 0:TG], ACT.Copy)
                act_s.done(ins, ("g", j))

        @block.vector
        def _(dve):
            def link(ins):
                chain.up(ins)
                dve.wait_ge(chain.sem, chain.n)
            for j in J:
                dve_s.done(nc.vector.scalar_tensor_tensor(out=bonus, in0=r[:, j], scalar=k.r_k[:, j:j + 1],
                                                          in1=kk_[:, j], op0=ALU.mult, op1=ALU.mult), ("rk", j))
                pe_s.wait(dve, ("mean", j))
                for g in G:
                    nc.vector.scalar_tensor_tensor(out=o[:, j, grp(g)], in0=k.ps[g][:, 0:TG], scalar=-1.0 / RN,
                                                   in1=o[:, j, grp(g)], op0=ALU.mult, op1=ALU.add)\
                        .then_inc(chain.sem, 1)
                chain.n += NT
                dve.wait_ge(chain.sem, chain.n)
                dve_s.done(nc.vector.tensor_tensor(square, o[:, j], o[:, j], ALU.mult), ("centred", j))
                pe_s.wait(dve, ("bonus", j))
                for g in G:
                    nc.vector.tensor_tensor(out[:, j, grp(g)], k.ps[3 + g][:, 0:TG], v[:, j, grp(g)], ALU.mult)\
                        .then_inc(chain.sem, 1)
                chain.n += NT
                act_s.wait(dve, ("root", j))
                dve.wait_ge(chain.sem, chain.n)
                link(nc.vector.reciprocal(k.rs[:, :], k.rs[:, :]))
                link(nc.vector.scalar_tensor_tensor(out=o[:, j], in0=o[:, j], scalar=k.lnx_g[:, j:j + 1],
                                                    in1=k.rs[:, :], op0=ALU.mult, op1=ALU.mult))
                link(nc.vector.scalar_tensor_tensor(out=out[:, j], in0=o[:, j], scalar=k.lnx_b[:, j:j + 1],
                                                    in1=out[:, j], op0=ALU.add, op1=ALU.add))
                act_s.wait(dve, ("g", j))
                dve_s.done(nc.vector.tensor_tensor(out[:, j], out[:, j], k.gbuf[:, :], ALU.mult), ("done", j))
                dve_s.wait(dve, ("done", j))


MH_, RT_ = 8, 4
NOPE, ROPE, VH = 64, 32, 64
QH = NOPE + ROPE
QL, KVL = 768, 256
QT, KT = QL // P, KVL // P
CW = KVL + ROPE
MLA_SCALE = QH ** -0.5
PAST, PAGE = 2048, 128
NPAGE = PAST // PAGE
MEM, MH = 256, 4
MTOK = MEM // P
MEM_SCALE = P ** -0.5
COL_Q = RPROJ
COL_PE = COL_Q + QL + KVL
COL_MEM = COL_PE + ROPE
COL_GATE = COL_MEM + MH * P
NEG = -1e30
NQ = SEQ // P


@stage
def key_rope(k):
    nc = k.nc
    pe_rows = slice(NOPE, QH)
    cos, sin = k.C[pe_rows, 9, :], k.C[pe_rows, 10, :]
    key, tmp = k.C[pe_rows, 8, :], k.C[pe_rows, 11, :]
    w = k.W[:, 0, 0:DT * ROPE].rearrange("p (f c) -> p f c", f=DT)
    G = range(NT)
    landed = Count(k, "pe_w_landed")
    pe_s = Steps(k, "pe_products", ["key", "swap"] + [("rows", i) for i in range(NQ + 1)])
    act_s = Steps(k, "pe_copies", ["key"] + [("rows", i) for i in range(NQ + 1)])
    dve_s = Steps(k, "pe_rotated", ["cos", "sin", "key"])
    stored = [Count(k, f"rows_stored{s}") for s in range(2)]
    stage = [k.W[:, 0, 512 + CW * s:512 + CW * (s + 1)] for s in range(2)]
    with nc.Block() as block:
        @block.sync
        def _(sp):
            src = k.io["w_in"][0].rearrange("(f p) n -> p f n", p=P)[:, :, COL_PE:COL_PE + ROPE]
            with nc.allow_non_contiguous_dma("32 columns"):
                sp.dma_start(w, src).then_inc(landed.sem, 16)
            sp.dma_start(cos, k.io["c_cos"]).then_inc(landed.sem, 16)
            sp.dma_start(sin, k.io["c_sin"]).then_inc(landed.sem, 16)
            sp.dma_start(k.perm[pe_rows, :], k.io["c_perm"]).then_inc(landed.sem, 16)
            for i in range(NQ):
                act_s.wait(sp, ("rows", i))
                sp.dma_start(k.io["rows_prompt"][0, 0, i * P:(i + 1) * P, :], stage[i % 2]).then_inc(stored[i % 2].sem, 16)
            act_s.wait(sp, ("rows", NQ))
            sp.dma_start(k.io["rows_sample"][0].rearrange("b o c -> (b o) c"), stage[NQ % 2][0:DEC])\
                .then_inc(stored[NQ % 2].sem, 16)
            for s in range(2):
                sp.wait_ge(stored[s].sem, 16 * len(range(s, NQ + 1, 2)))

        @block.tensor
        def _(pe):
            pe.wait_ge(landed.sem, 64)
            for g in G:
                for f in range(DT):
                    ins = nc.tensor.matmul(k.ps[g][pe_rows, 0:TG], w[:, f], k.B[:, f, grp(g)],
                                           start=(f == 0), stop=(f == DT - 1))
            pe_s.done(ins, "key")
            act_s.wait(pe, "key")
            for g in G:
                ins = nc.tensor.matmul(k.ps[3 + g][pe_rows, 0:TG], k.perm[pe_rows, :], key[:, grp(g)],
                                       start=True, stop=True)
            pe_s.done(ins, "swap")
            dve_s.wait(pe, "key")
            for i in range(NQ + 1):
                n = P if i < NQ else DEC
                cols = slice(i * P, i * P + n)
                b = k.ps[6 + i % 2]
                if i >= 2:
                    act_s.wait(pe, ("rows", i - 2))
                for f in range(KT):
                    nc.tensor.transpose(b[0:n, f * P:(f + 1) * P], k.C[:, 6 + f, cols], k.ident[:, :])
                pe_s.done(nc.tensor.transpose(b[0:n, KVL:CW], k.C[pe_rows, 8, cols], k.ident[pe_rows, pe_rows]),
                          ("rows", i))

        @block.scalar
        def _(act):
            pe_s.wait(act, "key")
            for g in G:
                ins = nc.scalar.activation(key[:, grp(g)], k.ps[g][pe_rows, 0:TG], ACT.Copy)
            act_s.done(ins, "key")
            for i in range(NQ + 1):
                n = P if i < NQ else DEC
                pe_s.wait(act, ("rows", i))
                if i >= 2:
                    act.wait_ge(stored[i % 2].sem, 16 * (i // 2))
                act_s.done(nc.scalar.activation(stage[i % 2][0:n], k.ps[6 + i % 2][0:n, 0:CW], ACT.Copy), ("rows", i))

        @block.vector
        def _(dve):
            dve.wait_ge(landed.sem, 64)
            pe_s.wait(dve, "swap")
            for g in G:
                ins = nc.vector.tensor_tensor(tmp[:, grp(g)], k.ps[3 + g][pe_rows, 0:TG], sin[:, grp(g)], ALU.mult)
            dve_s.done(ins, "cos")
            act_s.wait(dve, "key")
            dve_s.done(nc.vector.tensor_tensor(key, key, cos, ALU.mult), "sin")
            dve_s.wait(dve, "sin")
            dve_s.done(nc.vector.tensor_tensor(key, key, tmp, ALU.add), "key")
            dve_s.wait(dve, "key")
            for s in range(2):
                nc.vector.tensor_copy(k.C[pe_rows, 13 + s, :], key)


@stage
def prompt_attention(k, name, mla):
    nc = k.nc
    heads = MH_ if mla else MH
    depth = QH if mla else P
    nq = NQ
    S2, G = range(2), range(NT)
    kq = QT if mla else DT
    xq = k.C[:, 0:QT] if mla else k.B
    scale = MLA_SCALE if mla else MEM_SCALE
    wide = VH if mla else P
    q_buf = [k.C[:, 11 + s, :] if mla else k.C[:, s, :] for s in S2]
    k_buf = [k.C[:, 13 + s, :] if mla else k.C[:, 2 + s, 0:MEM] for s in S2]
    v_buf = [(k.C[:, 15, s * 512:(s + 1) * 512].rearrange("p (t c) -> p t c", t=NQ) if mla else
              k.C[:, 4, s * 256:(s + 1) * 256].rearrange("p (t c) -> p t c", t=MTOK)) for s in S2]
    prob = [k.C[:, 16 + s, 0:SEQ] if mla else k.C[:, 6 + s, 0:SEQ] for s in S2]
    probT = [k.C[:, 18 + s, 0:SEQ] if mla else k.C[:, 8 + s, 0:SEQ] for s in S2]
    wq = [k.W[:, s, 0:kq * depth].rearrange("p (f c) -> p f c", f=kq) for s in S2]
    wk = [k.W[:, s, 1024:1024 + KT * NOPE].rearrange("p (f c) -> p f c", f=KT) for s in S2]
    wv = [k.W[:, s, 1280:1280 + KT * VH].rearrange("p (f c) -> p f c", f=KT) for s in S2]
    nw = 3 if mla else 1
    keys = [(i + 1) * P if mla else MEM for i in range(nq)]
    blocks = [n // P for n in keys]
    pe_rows = slice(NOPE, QH)
    cos, sin = k.C[pe_rows, 9, :], k.C[pe_rows, 10, :]

    landed = [Count(k, f"{name}_w_landed{s}") for s in S2]
    head_steps = [("q", g) for g in G] + ([("k", g) for g in G] + ["v"] if mla else [])
    order = []
    for i in range(nq + 2):
        order += [("S", i)] * (i < nq) + [("T", i - 1)] * (1 <= i <= nq) + [("O", i - 2)] * (i >= 2)
    pe_s = Steps(k, name + "_products", [(s, x) for s in S2 for x in head_steps + (["swap"] if mla else []) + order],
                 primed=True)
    act_s = Steps(k, name + "_functions",
                  [(s, x) for s in S2 for x in head_steps + [y for y in order for y in
                   ([("exp", y[1])] if y[0] == "S" else [("T", y[1])] if y[0] == "T" else [("O", y[1])])]],
                  primed=True)
    dve_s = Steps(k, name + "_softmax",
                  [(s, x) for s in S2 for x in ["q"] + [(m, i) for i in range(nq) for m in ("max", "prob")]],
                  primed=True)
    pool_s = Steps(k, name + "_operands", list(S2)) if not mla else None
    chain = Count(k, name + "_chain")
    links = [0]
    per_chain = 2 * ((1 if mla else 0) + 2 * nq)

    with nc.Block() as block:
        @block.sync
        def _(sp):
            with sp.Fori(0, heads // 2) as it:
                for s in S2:
                    h = it * 2 + s
                    pe_s.wait(sp, (s, "swap" if mla else ("q", NT - 1)), it, before=1)
                    if mla:
                        sp.dma_start(wq[s], k.io["mla_w_qb"][0].rearrange("(f p) n -> p f n", p=P)[:, :, bass.ds(h * QH, QH)])\
                            .then_inc(landed[s].sem, 16)
                        sp.dma_start(wk[s], k.io["mla_w_uk"][0].rearrange("(f p) h n -> p f (h n)", p=P)
                                     [:, :, bass.ds(h * NOPE, NOPE)]).then_inc(landed[s].sem, 16)
                        sp.dma_start(wv[s], k.io["mla_w_uv"][0].rearrange("(f p) h n -> p f (h n)", p=P)
                                     [:, :, bass.ds(h * VH, VH)]).then_inc(landed[s].sem, 16)
                    else:
                        sp.dma_start(wq[s], k.io["w_in"][0].rearrange("(f p) n -> p f n", p=P)
                                     [:, :, bass.ds(COL_MEM + h * P, P)]).then_inc(landed[s].sem, 16)

        if not mla:
            @block.gpsimd
            def _(pool):
                with pool.Fori(0, heads // 2) as it:
                    for s in S2:
                        pe_s.wait(pool, (s, ("O", nq - 1)), it, before=1)
                        nc.gpsimd.tensor_copy(k_buf[s].rearrange("p (a t) -> p a t", a=1),
                                              k.memT[:, bass.ds(it * 2 + s, 1), :])
                        pool_s.done(nc.gpsimd.tensor_copy(v_buf[s], k.memV[:, :, bass.ds((it * 2 + s) * P, P)]), s)

        @block.tensor
        def _(pe):
            def settled():
                pe.sem_inc(k.settled.sem, 1)

            pe_s.prime(pe)
            with pe.Fori(0, heads // 2) as it:
                for s in S2:
                    pe.wait_ge(landed[s].sem, it * (16 * nw) + 16 * nw)
                    if s == 0:
                        act_s.wait(pe, (1, ("O", nq - 1)), it, before=1)
                    else:
                        act_s.wait(pe, (0, ("O", nq - 1)), it)
                    for g in G:
                        for f in range(kq):
                            ins = nc.tensor.matmul(k.ps[g][0:depth, 0:TG], wq[s][:, f], xq[:, f, grp(g)],
                                                   start=(f == 0), stop=(f == kq - 1))
                        pe_s.done(ins, (s, ("q", g)))
                    if mla:
                        for g in G:
                            for f in range(KT):
                                ins = nc.tensor.matmul(k.ps[3 + g][0:NOPE, 0:TG], wk[s][:, f], k.C[:, 6 + f, grp(g)],
                                                       start=(f == 0), stop=(f == KT - 1))
                            pe_s.done(ins, (s, ("k", g)))
                        for t in range(NQ):
                            for f in range(KT):
                                ins = nc.tensor.matmul(k.ps[7][:, t * VH:(t + 1) * VH],
                                                       k.C[:, 6 + f, t * P:(t + 1) * P], wv[s][:, f],
                                                       start=(f == 0), stop=(f == KT - 1))
                        pe_s.done(ins, (s, "v"))
                        act_s.wait(pe, (s, ("q", NT - 1)), it)
                        settled()
                        for g in G:
                            ins = nc.tensor.matmul(k.ps[g][pe_rows, 0:TG], k.perm[pe_rows, :],
                                                   q_buf[s][pe_rows, grp(g)], start=True, stop=True)
                        pe_s.done(ins, (s, "swap"))
                    else:
                        pool_s.wait(pe, s, it)
                    for m, i in order:
                        if m == "S":
                            if i == 0:
                                dve_s.wait(pe, (s, "q"), it)
                                if mla:
                                    act_s.wait(pe, (s, "v"), it)
                            if i >= 2:
                                act_s.wait(pe, (s, ("exp", i - 2)), it)
                            for b in range((keys[i] + 511) // 512):
                                n = min(512, keys[i] - 512 * b)
                                last = mla and b == (keys[i] - 1) // 512
                                out = k.ps[2 * (i % 2) + b]
                                ins = nc.tensor.matmul(out[:, 0:n], q_buf[s][0:depth, i * P:(i + 1) * P],
                                                       k_buf[s][0:depth, 512 * b:512 * b + n],
                                                       start=True, stop=not last)
                                if last:
                                    ins = nc.tensor.matmul(out[:, n - P:n], k.ident[:, :], k.causal[:, :],
                                                           start=False, stop=True)
                        elif m == "T":
                            dve_s.wait(pe, (s, ("prob", i)), it)
                            if i >= 1:
                                act_s.wait(pe, (s, ("T", i - 1)), it)
                            for b in range(blocks[i]):
                                ins = nc.tensor.transpose(k.ps[4 + b // 4][:, (b % 4) * P:(b % 4 + 1) * P],
                                                          prob[i % 2][:, b * P:(b + 1) * P], k.ident[:, :])
                        else:
                            act_s.wait(pe, (s, ("T", i)), it)
                            if i >= 2:
                                act_s.wait(pe, (s, ("O", i - 2)), it)
                            lo = VH * s if mla else 0
                            settled()
                            for b in range(blocks[i]):
                                ins = nc.tensor.matmul(k.ps[6 + i % 2][lo:lo + wide, 0:P], v_buf[s][:, b, :],
                                                       probT[i % 2][:, b * P:(b + 1) * P],
                                                       start=(b == 0), stop=(b == blocks[i] - 1))
                        pe_s.done(ins, (s, (m, i)))

        @block.scalar
        def _(act):
            act_s.prime(act)
            with act.Fori(0, heads // 2) as it:
                for s in S2:
                    for g in G:
                        pe_s.wait(act, (s, ("q", g)), it)
                        act_s.done(nc.scalar.activation(q_buf[s][0:depth, grp(g)], k.ps[g][0:depth, 0:TG], ACT.Copy),
                                   (s, ("q", g)))
                    if mla:
                        for g in G:
                            pe_s.wait(act, (s, ("k", g)), it)
                            act_s.done(nc.scalar.activation(k_buf[s][0:NOPE, grp(g)], k.ps[3 + g][0:NOPE, 0:TG],
                                                            ACT.Copy), (s, ("k", g)))
                        pe_s.wait(act, (s, "v"), it)
                        act_s.done(nc.scalar.activation(v_buf[s], k.ps[7][:, :].rearrange("p (t c) -> p t c", t=NQ),
                                                        ACT.Copy), (s, "v"))
                    for m, i in order:
                        if m == "S":
                            dve_s.wait(act, (s, ("max", i)), it)
                            act_s.done(nc.scalar.activation(prob[i % 2][:, 0:keys[i]], k.psw[i % 2][:, 0:keys[i]],
                                                            ACT.Exp, scale=scale, bias=k.nmax[:, i % 2:i % 2 + 1],
                                                            accum_out=k.rsum[:, i % 2:i % 2 + 1]), (s, ("exp", i)))
                        elif m == "T":
                            pe_s.wait(act, (s, ("T", i)), it)
                            act_s.done(nc.scalar.activation(probT[i % 2][:, 0:keys[i]], k.psw[2][:, 0:keys[i]],
                                                            ACT.Copy), (s, ("T", i)))
                        else:
                            pe_s.wait(act, (s, ("O", i)), it)
                            lo = VH * s if mla else 0
                            at = bass.ds(it, 1) if mla else bass.ds(it * 2 + s, 1)
                            out = (k.A[:, 0:4] if mla else k.C[:, 18:22])[lo:lo + wide, at, i * P:(i + 1) * P]
                            act_s.done(nc.scalar.activation(out, k.ps[6 + i % 2][lo:lo + wide, 0:P]
                                                            .rearrange("p (a t) -> p a t", a=1), ACT.Copy),
                                       (s, ("O", i)))

        @block.vector
        def _(dve):
            dve_s.prime(dve)
            with dve.Fori(0, heads // 2) as it:
                links[0] = 0

                def link(ins):
                    links[0] += 1
                    ins.then_inc(chain.sem, 1)
                    dve.wait_ge(chain.sem, it * per_chain + links[0])

                for s in S2:
                    q_s = (k.q_dec if mla else k.qm_dec)[0:depth, bass.ds(it * 2 + s, 1), :]
                    q_cols = q_buf[s][0:depth, SEQ:T].rearrange("p (a t) -> p a t", a=1)
                    if mla:
                        pe_s.wait(dve, (s, "swap"), it)
                        act_s.wait(dve, (s, ("q", NT - 1)), it)
                        for g in G:
                            nc.vector.tensor_tensor(k.sq[pe_rows, 0, grp(g)], k.ps[g][pe_rows, 0:TG], sin[:, grp(g)],
                                                    ALU.mult)
                        link(nc.vector.tensor_tensor(k.sq[pe_rows, 1, :], q_buf[s][pe_rows, :], cos, ALU.mult))
                        dve_s.done(nc.vector.tensor_tensor(q_buf[s][pe_rows, :], k.sq[pe_rows, 0, :],
                                                           k.sq[pe_rows, 1, :], ALU.add), (s, "q"))
                        dve_s.wait(dve, (s, "q"), it)
                        nc.vector.tensor_copy(q_s, q_cols)
                    else:
                        act_s.wait(dve, (s, ("q", NT - 1)), it)
                        dve_s.done(nc.vector.tensor_copy(q_s, q_cols), (s, "q"))
                    for i in range(nq):
                        nmax, rsum = k.nmax[:, i % 2:i % 2 + 1], k.rsum[:, i % 2:i % 2 + 1]
                        pe_s.wait(dve, (s, ("S", i)), it)
                        link(nc.vector.tensor_reduce(nmax, k.psw[i % 2][:, 0:keys[i]], AX.X, ALU.max))
                        dve_s.done(nc.vector.tensor_scalar(nmax, nmax, -scale, None, ALU.mult), (s, ("max", i)))
                        act_s.wait(dve, (s, ("exp", i)), it)
                        link(nc.vector.reciprocal(rsum, rsum))
                        dve_s.done(nc.vector.tensor_scalar(prob[i % 2][:, 0:keys[i]], prob[i % 2][:, 0:keys[i]],
                                                           rsum, None, ALU.mult), (s, ("prob", i)))
            assert 2 * links[0] == per_chain * 2


@stage
def decode_attention(k):
    nc = k.nc
    S2 = range(2)
    wuk = k.C[:, 9, 0:KT * 512].rearrange("p (f c) -> p f c", f=KT)
    wuv = k.C[:, 10, 0:KT * 512].rearrange("p (f c) -> p f c", f=KT)
    cache = k.Bc
    wukT = k.W[0:NOPE, 0, 0:MH_ * KVL].rearrange("p (h c) -> p h c", h=MH_)
    cT = [k.W[:, 1, 512 * f:512 * (f + 1)] for f in range(KT + 1)]
    nT = k.W[:, 1, 1536:1540]
    misc = k.W[:, 1, 1600:2816]
    qlat = misc[:, 0:KT * 64].rearrange("p (f b h) -> p f b h", f=KT, b=DEC)
    qpe = misc[0:ROPE, 128:192].rearrange("p (h b) -> p h b", b=DEC)
    q_now = misc[:, 192:192 + 24].rearrange("p (f h) -> p f h", f=3)
    sc = misc[:, 256:256 + 136].rearrange("p (g h) -> p g h", h=MH_)
    mx, m8, dg = misc[:, 400:408], misc[0:8, 408:409], misc[0:8, 416:424]
    rs = misc[:, 432:440]
    ctx = misc[:, 448:448 + 128].rearrange("p (f h b) -> p f h b", f=KT, h=MH_)
    ng = NPAGE // 4
    setup = Count(k, "dec_setup_landed")
    set_pe = Steps(k, "dec_setup_products", [("wukT", j) for j in range(4)] + ["qlat"])
    set_act = Steps(k, "dec_setup_copies", [("wukT", j) for j in range(4)] + ["qlat"])
    qpe_moved = Count(k, "dec_qpe_moved")
    landed = [Count(k, f"dec_cache_landed{s}") for s in S2]
    pe_s = Steps(k, "dec_products", [(s, x) for s in S2 for x in
                 [(m, g) for g in range(ng) for m in ("T", "S")] + ["nT", "nS", "mT", "mB", "sum", "ctx"]], primed=True)
    act_s = Steps(k, "dec_copies", [(s, x) for s in S2 for x in [("T", g) for g in range(ng)] + ["nT", "exp"]],
                  primed=True)
    dve_s = Steps(k, "dec_softmax", [(s, x) for s in S2 for x in
                  ["q"] + [("T", g) for g in range(ng)] + ["mx", "diag", "sub", "rs", "ctx"]], primed=True)
    chain = Count(k, "dec_chain")
    per_chain = 8
    pages_may_land = Count(k, "dec_pages_may_land")
    out_pe = Count(k, "dec_out_multiplied")
    links = [0]

    with nc.Block() as block:
        @block.sync
        def _(sp):
            sp.dma_start(wuk, k.io["mla_w_uk"][0].rearrange("(f p) h n -> p f (h n)", p=P)).then_inc(setup.sem, 16)
            sp.dma_start(wuv, k.io["mla_w_uv"][0].rearrange("(f p) h n -> p f (h n)", p=P)).then_inc(setup.sem, 16)
            sp.dma_start(qpe, k.q_dec[NOPE:QH, :, :]).then_inc(qpe_moved.sem, 16)
            n_phys = k.io["cache_mla"].shape[1]
            with sp.Fori(0, DEC // 2) as it:
                for s in S2:
                    b = it * 2 + s
                    pe_s.wait(sp, (s, "ctx"), it, before=1)
                    sp.sem_inc(pages_may_land.sem, 1)
                    with sp.Fori(0, NPAGE) as page:
                        at = sp.value_load(k.pages[0:1, bass.ds(b * NPAGE + page, 1)], min_val=0, max_val=n_phys - 1)
                        sp.dma_start(cache[:, s, bass.ds(page, 1), :],
                                     k.io["cache_mla"][0, bass.ds(at, 1)].rearrange("a p c -> p a c"))\
                            .then_inc(landed[s].sem, 16)
                    sp.dma_start(cache[0:1, s, NPAGE, :], k.io["rows_sample"][0, bass.ds(b, 1), 0, :])\
                        .then_inc(landed[s].sem, 16)

        @block.tensor
        def _(pe):
            def settled():
                pe.sem_inc(k.settled.sem, 1)

            pe.wait_ge(setup.sem, 32)
            for j in range(4):
                for i in range(4):
                    h, f = (4 * j + i) // KT, (4 * j + i) % KT
                    ins = nc.tensor.transpose(k.ps[j][0:NOPE, i * P:(i + 1) * P], wuk[:, f, h * NOPE:(h + 1) * NOPE],
                                              k.ident[:, :])
                set_pe.done(ins, ("wukT", j))
            set_act.wait(pe, ("wukT", 3))
            for f in range(KT):
                for h in range(MH_):
                    ins = nc.tensor.matmul(k.ps[4][:, (f * MH_ + h) * DEC:(f * MH_ + h + 1) * DEC],
                                           wukT[:, h, f * P:(f + 1) * P], k.q_dec[0:NOPE, h, :], start=True, stop=True)
            set_pe.done(ins, "qlat")
            pe_s.prime(pe)
            set_act.wait(pe, "qlat")
            with pe.Fori(0, DEC // 2) as it:
                for s in S2:
                    pe.wait_ge(landed[s].sem, (it + 1) * (16 * (NPAGE + 1)))
                    dve_s.wait(pe, (s, "q"), it)
                    for g in range(ng):
                        if g:
                            act_s.wait(pe, (s, ("T", g - 1)), it)
                            dve_s.wait(pe, (s, ("T", g - 1)), it)
                        elif s:
                            dve_s.wait(pe, (0, "ctx"), it)
                        else:
                            dve_s.wait(pe, (1, "ctx"), it, before=1)
                        for f in range(KT + 1):
                            n = P if f < KT else ROPE
                            for i in range(4):
                                ins = nc.tensor.transpose(k.ps[f][0:n, i * P:(i + 1) * P],
                                                          cache[:, s, 4 * g + i, f * P:f * P + n], k.ident[:, :])
                        pe_s.done(ins, (s, ("T", g)))
                        act_s.wait(pe, (s, ("T", g)), it)
                        dve_s.wait(pe, (s, ("T", g)), it)
                        for i in range(4):
                            for f in range(KT + 1):
                                n = P if f < KT else ROPE
                                o = (4 * g + i) * MH_
                                ins = nc.tensor.matmul(k.ps[3][:, o:o + MH_], cT[f][0:n, i * P:(i + 1) * P],
                                                       q_now[0:n, f, :], start=(f == 0), stop=(f == KT))
                        pe_s.done(ins, (s, ("S", g)))
                    settled()
                    for f in range(KT + 1):
                        n = P if f < KT else ROPE
                        ins = nc.tensor.transpose(k.ps[4][0:n, f:f + 1], cache[0:1, s, NPAGE, f * P:f * P + n],
                                                  k.ident[0:1, 0:1])
                    pe_s.done(ins, (s, "nT"))
                    act_s.wait(pe, (s, "nT"), it)
                    settled()
                    for f in range(KT + 1):
                        n = P if f < KT else ROPE
                        ins = nc.tensor.matmul(k.ps[3][0:1, 128:136], nT[0:n, f:f + 1], q_now[0:n, f, :],
                                               start=(f == 0), stop=(f == KT))
                    pe_s.done(ins, (s, "nS"))
                    dve_s.wait(pe, (s, "mx"), it)
                    settled()
                    pe_s.done(nc.tensor.transpose(k.ps[5][0:MH_, 0:P], mx, k.ident[:, :]), (s, "mT"))
                    dve_s.wait(pe, (s, "diag"), it)
                    settled()
                    pe_s.done(nc.tensor.matmul(k.ps[5][:, 128:136], k.ones[0:8, :], dg, start=True, stop=True), (s, "mB"))
                    act_s.wait(pe, (s, "exp"), it)
                    pe_s.done(nc.tensor.matmul(k.ps[6][:, 0:136], k.ones[:, :], sc.rearrange("p g h -> p (g h)"),
                                               start=True, stop=True), (s, "sum"))
                    for f in range(KT):
                        for g in range(NPAGE):
                            nc.tensor.matmul(k.ps[7][:, f * MH_:(f + 1) * MH_], cache[:, s, g, f * P:(f + 1) * P],
                                             sc[:, g, :], start=(g == 0), stop=False)
                        ins = nc.tensor.matmul(k.ps[7][:, f * MH_:(f + 1) * MH_], cache[0:1, s, NPAGE, f * P:(f + 1) * P],
                                               sc[0:1, NPAGE, :], start=False, stop=True)
                    pe_s.done(ins, (s, "ctx"))
            dve_s.wait(pe, (1, "ctx"), DEC // 2 - 1)
            for h in range(MH_):
                lo = (h % 2) * VH
                for f in range(KT):
                    ins = nc.tensor.matmul(k.ps[0][lo:lo + VH, (h // 2) * DEC:(h // 2 + 1) * DEC],
                                           wuv[:, f, h * VH:(h + 1) * VH], ctx[:, f, h, :],
                                           start=(f == 0), stop=(f == KT - 1))
            ins.then_inc(out_pe.sem, 1)

        @block.scalar
        def _(act):
            for j in range(4):
                set_pe.wait(act, ("wukT", j))
                dst = k.W[0:NOPE, 0, 512 * j:512 * (j + 1)]
                set_act.done(nc.scalar.activation(dst, k.ps[j][0:NOPE, :], ACT.Copy), ("wukT", j))
            set_pe.wait(act, "qlat")
            for f in range(KT):
                ins = nc.scalar.activation(qlat[:, f].rearrange("p b h -> p h b"),
                                           k.ps[4][:, f * 64:(f + 1) * 64].rearrange("p (h b) -> p h b", h=MH_), ACT.Copy)
            set_act.done(ins, "qlat")
            act_s.prime(act)
            with act.Fori(0, DEC // 2) as it:
                for s in S2:
                    for g in range(ng):
                        pe_s.wait(act, (s, ("T", g)), it)
                        if g:
                            pe_s.wait(act, (s, ("S", g - 1)), it)
                        nc.scalar.activation(cT[0], k.ps[0][:, :], ACT.Copy)
                        act_s.done(nc.scalar.activation(cT[2][0:ROPE], k.ps[2][0:ROPE, :], ACT.Copy), (s, ("T", g)))
                    pe_s.wait(act, (s, "nT"), it)
                    nc.scalar.activation(nT[:, 0:2], k.ps[4][:, 0:2], ACT.Copy)
                    act_s.done(nc.scalar.activation(nT[0:ROPE, 2:3], k.ps[4][0:ROPE, 2:3], ACT.Copy), (s, "nT"))
                    dve_s.wait(act, (s, "sub"), it)
                    act_s.done(nc.scalar.activation(sc, sc, ACT.Exp, scale=MLA_SCALE), (s, "exp"))
            act.wait_ge(out_pe.sem, 1)
            nc.scalar.activation(k.A[:, 0:4, SEQ:T], k.ps[0][:, 0:4 * DEC].rearrange("p (j b) -> p j b", b=DEC), ACT.Copy)

        @block.vector
        def _(dve):
            set_act.wait(dve, "qlat")
            dve.wait_ge(qpe_moved.sem, 16)
            dve_s.prime(dve)
            with dve.Fori(0, DEC // 2) as it:
                links[0] = 0

                def link(ins):
                    links[0] += 1
                    ins.then_inc(chain.sem, 1)
                    dve.wait_ge(chain.sem, it * per_chain + links[0])

                for s in S2:
                    pe_s.wait(dve, (1 - s, "ctx"), it, before=1 - s)
                    nc.vector.tensor_copy(q_now[:, 0:KT, :].unsqueeze(2), qlat[:, :, bass.ds(it * 2 + s, 1), :])
                    dve_s.done(nc.vector.tensor_copy(q_now[0:ROPE, KT, :].unsqueeze(2), qpe[:, :, bass.ds(it * 2 + s, 1)]),
                               (s, "q"))
                    for g in range(ng):
                        pe_s.wait(dve, (s, ("T", g)), it)
                        if g:
                            pe_s.wait(dve, (s, ("S", g - 1)), it)
                        dve_s.done(nc.vector.tensor_copy(cT[1], k.ps[1][:, :]), (s, ("T", g)))
                    link(nc.vector.memset(sc[:, NPAGE, :], NEG))
                    pe_s.wait(dve, (s, "nS"), it)
                    nc.vector.tensor_copy(sc[:, 0:NPAGE, :], k.ps[3][:, 0:128].rearrange("p (g h) -> p g h", h=MH_))
                    link(nc.vector.tensor_copy(sc[0:1, NPAGE, :], k.ps[3][0:1, 128:136]))
                    dve_s.done(nc.vector.tensor_reduce(mx, sc.rearrange("p g h -> p h g"), AX.X, ALU.max), (s, "mx"))
                    pe_s.wait(dve, (s, "mT"), it)
                    link(nc.vector.tensor_reduce(m8, k.ps[5][0:MH_, 0:P], AX.X, ALU.max))
                    dve_s.done(nc.vector.tensor_scalar(dg, k.ident[0:8, 0:8], m8, None, ALU.mult), (s, "diag"))
                    pe_s.wait(dve, (s, "mB"), it)
                    dve_s.done(nc.vector.tensor_tensor(sc, sc, k.ps[5][:, 128:136].unsqueeze(1)
                                                       .to_broadcast([P, NPAGE + 1, MH_]), ALU.subtract), (s, "sub"))
                    pe_s.wait(dve, (s, "sum"), it)
                    link(nc.vector.tensor_reduce(rs, k.ps[6][:, 0:136].rearrange("p (g h) -> p h g", h=MH_), AX.X, ALU.add))
                    dve_s.done(nc.vector.reciprocal(rs, rs), (s, "rs"))
                    dve_s.wait(dve, (s, "rs"), it)
                    pe_s.wait(dve, (s, "ctx"), it)
                    dve_s.done(nc.vector.tensor_tensor(ctx[:, :, :, bass.ds(it * 2 + s, 1)],
                                                       k.ps[7][:, 0:2 * MH_].rearrange("p (f h a) -> p f h a", f=KT, a=1),
                                                       rs.unsqueeze(1).unsqueeze(3).to_broadcast([P, KT, MH_, 1]),
                                                       ALU.mult), (s, "ctx"))


@stage
def memory_keys(k, gain):
    nc = k.nc
    mT = k.C[:, 0:2, :].rearrange("p a t -> p (a t)")[:, 0:DT * MEM].rearrange("p (f t) -> p f t", f=DT)
    w = [k.C[:, 2 + 4 * m:6 + 4 * m, :].rearrange("p a t -> p (a t)")[:, 0:4096].rearrange("p (f c) -> p f c", f=DT)
         for m in range(2)]
    raw = [k.C[:, 10 + t, 0:D] for t in range(MTOK)]
    rows = [k.C[:, 12, 0:MTOK * 512].rearrange("p (t c) -> p t c", t=MTOK), k.memV]
    landed = Count(k, "mem_landed")
    wlanded = Count(k, "mem_w_landed")
    pe_s = Steps(k, "mem_turned", range(4))
    act_s = Steps(k, "mem_copied", range(4))
    with nc.Block() as block:
        @block.sync
        def _(sp):
            for t in range(MTOK):
                sp.dma_start(raw[t], k.io["mem_prompt"][0, t * P:(t + 1) * P, :]).then_inc(landed.sem, 16)
            for m, src in enumerate((k.io["mem_w_k"], k.io["mem_w_v"])):
                sp.dma_start(w[m], src[0].rearrange("(f p) n -> p f n", p=P)).then_inc(wlanded.sem, 16)
            sp.wait_ge(wlanded.sem, 32)

        @block.tensor
        def _(pe):
            pe.wait_ge(landed.sem, 32)
            for x in range(4):
                t, q = divmod(x, 2)
                for f in range(4):
                    ins = nc.tensor.transpose(k.ps[x][:, f * P:(f + 1) * P], raw[t][:, (4 * q + f) * P:(4 * q + f + 1) * P],
                                              k.ident[:, :])
                pe_s.done(ins, x)

        @block.scalar
        def _(act):
            for x in range(4):
                t, q = divmod(x, 2)
                pe_s.wait(act, x)
                act_s.done(nc.scalar.activation(mT[:, 4 * q:4 * q + 4, t * P:(t + 1) * P],
                                                k.ps[x][:, :].rearrange("p (f t) -> p f t", f=4), ACT.Copy), x)
    rms_norm(k, "mem_norm", mT, DT, gain, cols=MEM)
    pe_s = Steps(k, "mem_multiplied", [(m, t) for m in range(2) for t in range(MTOK)] + ["kT0", "kT1"])
    act_s = Steps(k, "mem_rows", [(m, t) for m in range(2) for t in range(MTOK)] + ["kT0", "kT1"])
    stored = Count(k, "mem_stored")
    with nc.Block() as block:
        @block.tensor
        def _(pe):
            for m in range(2):
                for t in range(MTOK):
                    for f in range(DT):
                        ins = nc.tensor.matmul(k.ps[2 * m + t][:, :], mT[:, f, t * P:(t + 1) * P], w[m][:, f, :],
                                               start=(f == 0), stop=(f == DT - 1))
                    pe_s.done(ins, (m, t))
            act_s.wait(pe, (0, MTOK - 1))
            for t in range(MTOK):
                for h in range(MH):
                    ins = nc.tensor.transpose(k.ps[4 + t][:, h * P:(h + 1) * P], rows[0][:, t, h * P:(h + 1) * P],
                                              k.ident[:, :])
                pe_s.done(ins, f"kT{t}")

        @block.scalar
        def _(act):
            for m in range(2):
                for t in range(MTOK):
                    pe_s.wait(act, (m, t))
                    act_s.done(nc.scalar.activation(rows[m][:, t, :], k.ps[2 * m + t][:, :], ACT.Copy), (m, t))
            for t in range(MTOK):
                pe_s.wait(act, f"kT{t}")
                act_s.done(nc.scalar.activation(k.memT[:, :, t * P:(t + 1) * P],
                                                k.ps[4 + t][:, :].rearrange("p (h t) -> p h t", h=MH), ACT.Copy), f"kT{t}")

        @block.sync
        def _(sp):
            for m, out in enumerate((k.io["mem_k_prompt"], k.io["mem_v_prompt"])):
                for t in range(MTOK):
                    act_s.wait(sp, (m, t))
                    sp.dma_start(out[0, 0, t * P:(t + 1) * P].rearrange("p h c -> p (h c)"), rows[m][:, t, :])\
                        .then_inc(stored.sem, 16)
            sp.wait_ge(stored.sem, 64)


@stage
def decode_memory(k):
    nc = k.nc
    B8 = range(DEC)
    qrow = k.W[0:DEC, 0, 0:512]
    qall = k.C[:, 5:9, :].rearrange("p a t -> p (a t)")[:, 0:DEC * 512].rearrange("p (b c) -> p b c", b=DEC)
    keys = [k.C[:, s, 0:1024].rearrange("p (t c) -> p t c", t=MTOK) for s in range(2)]
    vals = [k.C[:, 2 + s, 0:1024].rearrange("p (t c) -> p t c", t=MTOK) for s in range(2)]
    prod = k.C[:, 4, 0:1024].rearrange("p (t c) -> p t c", t=MTOK)
    sc = k.W[:, 1, 0:64].rearrange("p (b t h) -> p b t h", b=DEC, t=MTOK)
    mx, m1, dg = k.W[:, 1, 64:96], k.W[0:32, 1, 96:97], k.W[0:32, 1, 100:132]
    rs = k.W[:, 1, 132:164]
    pe_s = Steps(k, "dm_products", ["q", "mT", "mB", "sum"] + [("o", b) for b in B8])
    act_s = Steps(k, "dm_copies", ["q", "exp"])
    dve_s = Steps(k, "dm_softmax", [("s", b) for b in B8] + ["mx", "diag", "sub", "rs", "out"])
    put, got = Count(k, "dm_q_put"), Count(k, "dm_q_got")
    klanded = [Count(k, f"dm_keys_landed{s}") for s in range(2)]
    vlanded = [Count(k, f"dm_values_landed{s}") for s in range(2)]
    chain = Count(k, "dm_chain")

    def rows(src, b):
        return src[0, b].rearrange("(t p) h c -> p t (h c)", p=P)

    with nc.Block() as block:
        @block.sync
        def _(sp):
            for b in range(2):
                sp.dma_start(keys[b], rows(k.io["cache_mem_k"], b)).then_inc(klanded[b].sem, 16)
                sp.dma_start(vals[b], rows(k.io["cache_mem_v"], b)).then_inc(vlanded[b].sem, 16)
            act_s.wait(sp, "q")
            sp.dma_start(k.q_scratch, qrow).then_inc(put.sem, 16)
            sp.wait_ge(put.sem, 16)
            sp.dma_start(qall, k.q_scratch.rearrange("b c -> (b c)").unsqueeze(0).to_broadcast([P, DEC * 512])
                         .rearrange("p (b c) -> p b c", b=DEC)).then_inc(got.sem, 16)
            for b in range(2, DEC):
                dve_s.wait(sp, ("s", b - 2))
                sp.dma_start(keys[b % 2], rows(k.io["cache_mem_k"], b)).then_inc(klanded[b % 2].sem, 16)
            for b in range(2, DEC):
                pe_s.wait(sp, ("o", b - 2))
                sp.dma_start(vals[b % 2], rows(k.io["cache_mem_v"], b)).then_inc(vlanded[b % 2].sem, 16)

        @block.tensor
        def _(pe):
            for h in range(MH):
                ins = nc.tensor.transpose(k.ps[0][0:DEC, h * P:(h + 1) * P], k.qm_dec[:, h, :], k.ident[:, :])
            pe_s.done(ins, "q")
            dve_s.wait(pe, "mx")
            pe_s.done(nc.tensor.transpose(k.ps[1][0:32, 0:P], mx, k.ident[:, :]), "mT")
            dve_s.wait(pe, "diag")
            pe_s.done(nc.tensor.matmul(k.ps[2][:, 0:32], k.ones[0:32, :], dg, start=True, stop=True), "mB")
            act_s.wait(pe, "exp")
            pe_s.done(nc.tensor.matmul(k.ps[3][:, 0:64], k.ones[:, :], sc.rearrange("p b t h -> p (b t h)"),
                                       start=True, stop=True), "sum")
            for b in B8:
                pe.wait_ge(vlanded[b % 2].sem, 16 * (b // 2 + 1))
                for h in range(MH):
                    for t in range(MTOK):
                        ins = nc.tensor.matmul(k.ps[4][:, b * MH + h:b * MH + h + 1], vals[b % 2][:, t, h * P:(h + 1) * P],
                                               sc[:, b, t, h:h + 1], start=(t == 0), stop=(t == MTOK - 1))
                pe_s.done(ins, ("o", b))

        @block.scalar
        def _(act):
            pe_s.wait(act, "q")
            act_s.done(nc.scalar.activation(qrow, k.ps[0][0:DEC, :], ACT.Copy), "q")
            dve_s.wait(act, "sub")
            act_s.done(nc.scalar.activation(sc, sc, ACT.Exp, scale=MEM_SCALE), "exp")

        @block.vector
        def _(dve):
            def link(ins):
                chain.up(ins)
                dve.wait_ge(chain.sem, chain.n)

            dve.wait_ge(got.sem, 16)
            for b in B8:
                dve.wait_ge(klanded[b % 2].sem, 16 * (b // 2 + 1))
                if b:
                    dve_s.wait(dve, ("s", b - 1))
                link(nc.vector.tensor_tensor(prod, keys[b % 2], qall[:, b].unsqueeze(1).to_broadcast([P, MTOK, 512]),
                                             ALU.mult))
                dve_s.done(nc.vector.tensor_reduce(sc[:, b], prod.rearrange("p t (h c) -> p t h c", h=MH), AX.X, ALU.add),
                           ("s", b))
            dve_s.wait(dve, ("s", DEC - 1))
            dve_s.done(nc.vector.tensor_tensor(mx.rearrange("p (b h) -> p b h", b=DEC), sc[:, :, 0], sc[:, :, 1], ALU.max),
                       "mx")
            pe_s.wait(dve, "mT")
            link(nc.vector.tensor_reduce(m1, k.ps[1][0:32, 0:P], AX.X, ALU.max))
            dve_s.done(nc.vector.tensor_scalar(dg, k.ident[0:32, 0:32], m1, None, ALU.mult), "diag")
            pe_s.wait(dve, "mB")
            top = k.ps[2][:, 0:32].rearrange("p (b h) -> p b h", b=DEC)
            dve_s.done(nc.vector.tensor_tensor(sc, sc, top.unsqueeze(2).to_broadcast([P, DEC, MTOK, MH]), ALU.subtract),
                       "sub")
            pe_s.wait(dve, "sum")
            sums = k.ps[3][:, 0:64].rearrange("p (b t h) -> p b h t", b=DEC, t=MTOK)
            link(nc.vector.tensor_reduce(rs.rearrange("p (b h) -> p b h", b=DEC), sums, AX.X, ALU.add))
            dve_s.done(nc.vector.reciprocal(rs, rs), "rs")
            dve_s.wait(dve, "rs")
            pe_s.wait(dve, ("o", DEC - 1))
            dve_s.done(nc.vector.tensor_tensor(k.C[:, 18:22, SEQ:T].rearrange("p h b -> p b h"),
                                               k.ps[4][:, 0:32].rearrange("p (b h) -> p b h", b=DEC),
                                               rs.rearrange("p (b h) -> p b h", b=DEC), ALU.mult), "out")


@stage
def merge(k):
    nc = k.nc
    branches = [(k.A[:, 4:8], k.io["rwkv_w_o"][0]), (k.A[:, 0:4], k.io["mla_w_o"][0]), (k.C[:, 18:22], k.io["mem_w_o"][0])]
    NB = len(branches)
    flat = k.W[:, :, :].rearrange("p s c -> p (s c)")
    w = [flat[:, b * 12 * P:(b + 1) * 12 * P].rearrange("p (f c) -> p f c", f=12) for b in range(NB)]
    landed = [Count(k, f"merge_w_landed{b}") for b in range(NB)]
    multiplied = Count(k, "merge_multiplied")
    gated = Count(k, "merge_gated")
    weighed = Count(k, "merge_weighed")
    added = Count(k, "merge_added")
    per = NB * NT
    gate_w = k.io["w_in"][0].rearrange("(f p) n -> p f n", p=P)

    def load(sp, b, j):
        sp.dma_start(w[b][:, 0:DT], gate_w[:, :, bass.ds(COL_GATE + b * D + j * P, P)]).then_inc(landed[b].sem, 16)
        sp.dma_start(w[b][:, DT:12], branches[b][1].rearrange("(f p) n -> p f n", p=P)[:, :, bass.ds(j * P, P)])\
            .then_inc(landed[b].sem, 16)

    with nc.Block() as block:
        @block.sync
        def _(sp):
            for b in range(NB):
                load(sp, b, 0)
            with sp.Fori(0, DT - 1) as j:
                for b in range(NB):
                    sp.wait_ge(multiplied.sem, j * per + NT * (b + 1))
                    load(sp, b, j + 1)

        @block.tensor
        def _(pe):
            with pe.Fori(0, DT) as j:
                for b in range(NB):
                    pe.wait_ge(landed[b].sem, j * 32 + 32)
                    for g in range(NT):
                        pe.wait_ge(added.sem, j * per + NT * b + g + 1)
                        for f in range(DT):
                            nc.tensor.matmul(k.ps[2 * g][:, 0:TG], w[b][:, f], k.B[:, f, grp(g)],
                                             start=(f == 0), stop=(f == DT - 1))
                        for f in range(4):
                            ins = nc.tensor.matmul(k.ps[2 * g + 1][:, 0:TG], w[b][:, DT + f], branches[b][0][:, f, grp(g)],
                                                   start=(f == 0), stop=(f == 3))
                        ins.then_inc(multiplied.sem, 1)

        @block.scalar
        def _(act):
            with act.Fori(0, DT) as j:
                for b in range(NB):
                    for g in range(NT):
                        act.wait_ge(multiplied.sem, j * per + NT * b + g + 1)
                        act.wait_ge(added.sem, j * per + NT * b + g + 1)
                        nc.scalar.activation(k.t3[:, g, :], k.ps[2 * g][:, 0:TG], ACT.Sigmoid).then_inc(gated.sem, 1)

        @block.vector
        def _(dve):
            dve.sem_inc(added.sem, NT)
            with dve.Fori(0, DT) as j:
                for b in range(NB):
                    for g in range(NT):
                        out = k.C[:, bass.ds(j, 1), grp(g)]
                        t = k.t3[:, g, :].rearrange("p (a t) -> p a t", a=1)
                        x = k.ps[2 * g + 1][:, 0:TG].rearrange("p (a t) -> p a t", a=1)
                        dve.wait_ge(gated.sem, j * per + NT * b + g + 1)
                        if b == 0:
                            nc.vector.tensor_tensor(out, t, x, ALU.mult).then_inc(added.sem, 1)
                            continue
                        nc.vector.tensor_tensor(t, t, x, ALU.mult).then_inc(weighed.sem, 1)
                        dve.wait_ge(weighed.sem, j * (per - NT) + NT * (b - 1) + g + 1)
                        dve.wait_ge(added.sem, j * per + NT * (b - 1) + g + 1 + NT)
                        nc.vector.tensor_tensor(out, out, t, ALU.add).then_inc(added.sem, 1)


def shape_constants():
    c = np.arange(P)
    s, t = c[:, None] % CH, np.arange(CH)[None, :]
    resets = np.broadcast_to((np.arange(SEQ) % CH != 0), (P, SEQ))
    strict, upto = s < t, s <= t
    masks = [(t % 2 == 0) & (s == t + 1), (s % 2 == 0) & (t == s + 1), s == t]
    masks += [(s // (2 * l) == t // (2 * l)) & (s % (2 * l) < l) & (t % (2 * l) >= l) for l in (2, 4, 8, 16, 32)]
    half = ROPE // 2
    freqs = np.float32(10000.0) ** (-np.arange(half, dtype=np.float32) / np.float32(half))
    pos = np.concatenate([np.arange(SEQ), np.full(DEC, PAST)]).astype(np.float32)
    ang = (freqs[:, None] * pos[None, :]).astype(np.float64)
    i = np.arange(ROPE)
    perm = i[:, None] == (i[None, :] + half) % ROPE
    cos = np.concatenate([np.cos(ang), np.cos(ang)])
    sin = np.concatenate([-np.sin(ang), np.sin(ang)])
    causal = np.where(c[None, :] <= c[:, None], 0.0, NEG)
    out = {"c_cos": cos, "c_sin": sin, "c_perm": perm, "c_causal": causal, "c_ident": np.eye(P), "c_headones": (c[:, None] // RN) == (c[None, :] // RN), "c_resets": resets,
           "c_gram": np.concatenate([strict, upto], 1), "c_masks": np.stack(masks, 1)}
    return {name: np.ascontiguousarray(a, dtype=np.float32) for name, a in out.items()}


VECTORS = [("ffn1_pre", DT), ("ffn1_post", DT), ("mix_pre", DT), ("mix_post", DT), ("ffn2_pre", DT),
           ("ffn2_post", DT), ("rwkv_mu", RPT), ("rwkv_w0", RT), ("rwkv_a0", RT), ("rwkv_k_k", RT), ("rwkv_k_a", RT),
           ("rwkv_r_k", RT), ("rwkv_lnx_g", RT), ("rwkv_lnx_b", RT), ("mla_q_norm", 6), ("mla_kv_norm", 2),
           ("mem_norm", DT)]


def build(nc, dram, outs):
    k = Kit()
    k.nc = nc
    k.semaphores = []
    k.io = {**dram, **outs}
    with ExitStack() as ctx:
        k.ctx = ctx

        def sb(name, shape):
            return ctx.enter_context(nc.sbuf_tensor(name, shape, F32))

        k.A, k.B, k.C = sb("A", [P, DT, T]), sb("B", [P, DT, T]), sb("C", [P, FT, T])
        k.W = sb("W", [P, 2, FT * P])
        k.rs, k.sq = sb("rs", [P, T]), sb("sq", [P, 2, T])
        k.t3 = k.sq[:, :, :].rearrange("p a t -> p (a t)")[:, 0:NT * TG].rearrange("p (g t) -> p g t", g=NT)
        k.ident, k.ones, k.headones = sb("ident", [P, P]), sb("ones", [P, P]), sb("headones", [P, P])
        k.eps_col, k.lnx_eps, k.mu_now = sb("eps", [P, 1]), sb("lnx_eps", [P, 1]), sb("mu_now", [P, 1])
        k.vec = sb("vec", [P, sum(n for _, n in VECTORS)])
        k.gram = sb("gram", [P, 2 * CH])
        k.masks = sb("masks", [P, 8, CH])
        k.ST, k.st_rows = sb("ST", [P, RT, RN]), sb("st_rows", [P, RT, RN])
        k.chunk_decay, k.decay_now = sb("chunk_decay", [P, NCH, RT]), sb("decay_now", [P, 2, RT])
        k.rwflat = k.A[:, 4:8, :].rearrange("p a t -> p (a t)")
        k.rw = k.rwflat[:, 0:2 * 1792].rearrange("p (s c) -> p s c", s=2)
        k.rowbuf = k.W[:, 1, 1024:1024 + T + 1]
        k.gbuf = k.W[:, 1, 0:T]
        k.gram_mask = k.gram[:, :].unsqueeze(1).to_broadcast([P, RT, 2 * CH])

        def over_pairs(i):
            return k.masks[:, i, :].unsqueeze(1).to_broadcast([P, RT, CH])

        k.first_mask, k.first_mask_t, k.ident4 = over_pairs(0), over_pairs(1), over_pairs(2)
        k.level_mask = {l: over_pairs(3 + i) for i, l in enumerate((2, 4, 8, 16, 32))}
        psum = ctx.enter_context(nc.psum_tensor("banks", [P, 8, 512], F32))
        k.ps = [psum[:, i, :] for i in range(8)]
        k.psw = [psum[:, 2 * i:2 * i + 2, :].rearrange("p b c -> p (b c)") for i in range(4)]
        k.h_spill = nc.dram_tensor("h_spill", [P, DT, T], F32).ap()
        k.t_scratch = nc.dram_tensor("t_scratch", [6, DEC, RD], F32).ap()
        k.o_scratch = nc.dram_tensor("o_scratch", [DEC, RD], F32).ap()

        k.perm, k.causal = sb("perm", [P, ROPE]), sb("causal", [P, P])
        k.nmax, k.rsum = sb("nmax", [P, 2]), sb("rsum", [P, 2])
        k.q_dec, k.qm_dec = sb("q_dec", [P, MH_, DEC]), sb("qm_dec", [P, MH, DEC])
        k.pages = ctx.enter_context(nc.sbuf_tensor("pages", [1, DEC * NPAGE], mybir.dt.int32))
        k.q_scratch = nc.dram_tensor("q_scratch", [DEC, MH * P], F32).ap()
        k.settled = Count(k, "products_may_start")
        k.memT = k.C[:, 14, 0:MH * MEM].rearrange("p (h t) -> p h t", h=MH)
        k.memV = k.C[:, 13, 0:MTOK * 512].rearrange("p (t c) -> p t c", t=MTOK)
        k.Bc = k.C[:, 12:22, :].rearrange("p a t -> p (a t)")[:, 0:2 * (NPAGE + 1) * CW]\
            .rearrange("p (s g c) -> p s g c", s=2, g=NPAGE + 1)
        k.const_loads = [(k.causal[:, :], k.io["c_causal"]), (k.pages[:, :], k.io["page_table"].rearrange("b g -> (b g)").unsqueeze(0)),
                         (k.ident[:, :], k.io["c_ident"]), (k.headones[:, :], k.io["c_headones"]), (k.gram[:, :], k.io["c_gram"]),
                         (k.masks[:, :, :], k.io["c_masks"])]
        at, v = 0, {}
        for name, n in VECTORS:
            v[name] = k.vec[:, at:at + n]
            src = dram[name][0]
            if name == "rwkv_r_k":
                src = src.rearrange("h n -> (h n)")
            k.const_loads.append((v[name], src.rearrange("(f p) -> p f", p=P)))
            at += n
        k.mu, k.w0, k.a0, k.k_k, k.k_a = (v["rwkv_" + x] for x in ("mu", "w0", "a0", "k_k", "k_a"))
        k.r_k, k.lnx_g, k.lnx_b = (v["rwkv_" + x] for x in ("r_k", "lnx_g", "lnx_b"))
        ms = Count(k, "memset")
        with nc.Block() as block:
            @block.gpsimd
            def _(pool):
                nc.gpsimd.memset(k.ones[:, :], 1.0).then_inc(ms.sem, 1)
                nc.gpsimd.memset(k.eps_col[:, :], RMS_EPS).then_inc(ms.sem, 1)
                nc.gpsimd.memset(k.lnx_eps[:, :], LNX_EPS).then_inc(ms.sem, 1)
        with nc.allow_non_contiguous_dma("per-feature vectors go across partitions"):
            load_constants(k)
        load_x(k)
        ffn(k, "ffn1", v["ffn1_pre"], v["ffn1_post"], k.io["ffn1_gate"][0], k.io["ffn1_up"][0], k.io["ffn1_down"][0])
        rms_norm(k, "mix_pre", k.A, DT, v["mix_pre"], dst=k.B)
        spill(k, "h_spilled", k.h_spill, k.A[:, :, :])
        rwkv_project(k)
        rwkv_vectors(k)
        rwkv_scan(k)
        rwkv_sample_step(k)
        rwkv_finish(k)
        project(k, "latents", k.B, DT, k.io["w_in"][0], COL_Q, QT + KT, k.C)
        rms_norm(k, "q_norm", k.C[:, 0:QT], QT, v["mla_q_norm"])
        rms_norm(k, "kv_norm", k.C[:, QT:QT + KT], KT, v["mla_kv_norm"])
        key_rope(k)
        prompt_attention(k, "mla", True)
        decode_attention(k)
        memory_keys(k, v["mem_norm"])
        prompt_attention(k, "mem", False)
        decode_memory(k)
        merge(k)
        project(k, "mix_out", k.C, DT, k.io["w_out"][0], 0, DT, k.B)
        spill(k, "h_back", k.A[:, :, :], k.h_spill)
        rms_norm(k, "mix_post", k.B, DT, v["mix_post"], residual=k.A)
        ffn(k, "ffn2", v["ffn2_pre"], v["ffn2_post"], k.io["ffn2_gate"][0], k.io["ffn2_up"][0], k.io["ffn2_down"][0])
        store_y(k, k.A)



_OUTS = [("y_prompt", (1, SEQ, D)), ("y_sample", (DEC, 1, D)),
         ("rows_prompt", (1, 1, SEQ, CW)), ("rows_sample", (1, DEC, 1, CW)),
         ("wkv_prompt", (1, 1, RH, RN, RN)), ("wkv_sample", (1, DEC, RH, RN, RN)),
         ("shift_prompt", (1, 1, RPROJ)), ("shift_sample", (1, DEC, RPROJ)),
         ("mem_k_prompt", (1, 1, MEM, MH, P)), ("mem_v_prompt", (1, 1, MEM, MH, P))]


def kernel(**inputs):
    import concourse.bacc as bacc
    from concourse.bass_utils import run_bass_kernel_spmd

    nc = bacc.Bacc("TRN2", target_bir_lowering=False, num_devices=1)
    arrays, dram = {}, {}
    for name, a in {**inputs, **shape_constants()}.items():
        a = np.ascontiguousarray(a)
        arrays[f"in_{name}"] = a
        dram[name] = nc.dram_tensor(f"in_{name}", a.shape, mybir.dt.from_np(a.dtype), kind="ExternalInput").ap()
    outs = {name: nc.dram_tensor(f"out_{name}", shape, F32, kind="ExternalOutput").ap() for name, shape in _OUTS}
    build(nc, dram, outs)
    r = run_bass_kernel_spmd(nc, [arrays], core_ids=[0])
    return tuple(r.results[0][f"out_{name}"] for name, _ in _OUTS)
```

```python
import numpy as np
import concourse.bass as bass
from concourse import mybir
from contextlib import ExitStack

F32 = mybir.dt.float32
ALU = mybir.AluOpType
ACT = mybir.ActivationFunctionType
AX = mybir.AxisListType

P = 128
D = 1024
DT = D // P
SEQ = 1024
DEC = 8
T = SEQ + DEC
NT = 3
TG = T // NT
FFN = 2816
FT = FFN // P
RMS_EPS = 1e-6


class Count:

    def __init__(self, k, name):
        self.sem = k.nc.alloc_semaphore(name=name)
        k.semaphores.append(self.sem)
        self.n = 0

    def up(self, instruction, by=1):
        instruction.then_inc(self.sem, by)
        self.n += by
        return self.n


class Kit:
    pass


def stage(program):
    def whole(k, *args, **kwargs):
        before, k.semaphores = k.semaphores, []
        program(k, *args, **kwargs)
        k.nc.clear_and_free_semaphores(k.semaphores)
        k.nc.all_engine_barrier()
        k.semaphores = before
    return whole


def grp(g):
    return slice(g * TG, (g + 1) * TG)



@stage
def load_constants(k):
    nc = k.nc
    landed = Count(k, "constants_landed")
    with nc.Block() as block:
        @block.sync
        def _(sp):
            for dst, src in k.const_loads:
                landed.up(sp.dma_start(dst, src), 16)
            sp.wait_ge(landed.sem, landed.n)

        @block.gpsimd
        def _(pool):
            pass


@stage
def load_x(k):
    nc = k.nc
    n_tiles = SEQ // P
    tiles_landed = [Count(k, f"x_tile_landed{s}") for s in range(2)]
    transposed = Count(k, "x_quads_transposed")
    drained = Count(k, "x_quads_drained")
    stage = k.W
    bank = [k.ps[s][:, :].rearrange("p (f t) -> p f t", f=4) for s in range(4)]

    def src(i):
        return k.io["x_prompt"][0, bass.ds(i * P, P), :]

    with nc.Block() as block:
        @block.sync
        def _(sp):
            for s in range(2):
                sp.dma_start(stage[:, s, 0:D], src(s)).then_inc(tiles_landed[s].sem, 16)
            with sp.Fori(0, (n_tiles - 2) // 2) as pair:
                i = pair * 2
                for s in range(2):
                    sp.wait_ge(transposed.sem, 2 * i + 2 * (s + 1))
                    sp.dma_start(stage[:, s, 0:D], src(i + 2 + s)).then_inc(tiles_landed[s].sem, 16)
            sp.wait_ge(transposed.sem, 2 * (n_tiles - 1))
            sp.dma_start(stage[0:DEC, 0, 0:D], k.io["x_sample"].rearrange("b o d -> (b o) d"))\
                .then_inc(tiles_landed[0].sem, 16)

        @block.tensor
        def _(pe):
            with pe.Fori(0, n_tiles // 2) as pair:
                i = pair * 2
                for s in range(2):
                    pe.wait_ge(tiles_landed[s].sem, 8 * i + 16)
                    for q in range(2):
                        pe.wait_ge(drained.sem, 2 * i + 2 * s + q + 1)
                        for f in range(4):
                            ins = nc.tensor.transpose(bank[2 * s + q][:, f, :],
                                                      stage[:, s, (4 * q + f) * P:(4 * q + f + 1) * P],
                                                      k.ident[:, :])
                        ins.then_inc(transposed.sem, 1)
            pe.wait_ge(tiles_landed[0].sem, 16 * (n_tiles // 2 + 1))
            for q in range(2):
                pe.wait_ge(drained.sem, 2 * n_tiles + q + 1)
                for f in range(4):
                    ins = nc.tensor.transpose(bank[q][:, f, 0:DEC],
                                              stage[0:DEC, 0, (4 * q + f) * P:(4 * q + f + 1) * P],
                                              k.ident[0:DEC, 0:DEC])
                ins.then_inc(transposed.sem, 1)

        @block.vector
        def _(dve):
            dve.sem_inc(drained.sem, 4)
            with dve.Fori(0, n_tiles // 2) as pair:
                i = pair * 2
                for s in range(2):
                    for q in range(2):
                        dve.wait_ge(transposed.sem, 2 * i + 2 * s + q + 1)
                        nc.vector.tensor_copy(k.A[:, 4 * q:4 * q + 4, bass.ds((i + s) * P, P)],
                                              bank[2 * s + q]).then_inc(drained.sem, 1)
            for q in range(2):
                dve.wait_ge(transposed.sem, 2 * n_tiles + q + 1)
                nc.vector.tensor_copy(k.A[:, 4 * q:4 * q + 4, SEQ:T], bank[q][:, :, 0:DEC])\
                    .then_inc(drained.sem, 1)


@stage
def store_y(k, src):
    nc = k.nc
    n_tiles = SEQ // P
    transposed = Count(k, "y_quads_transposed")
    drained = Count(k, "y_quads_drained")
    stored = [Count(k, f"y_stored{s}") for s in range(2)]
    stage = k.W
    bank = [k.ps[s][:, :].rearrange("p (f t) -> p f t", f=4) for s in range(4)]
    copied = Count(k, "y_lhs_copied")
    lhs = k.C[:, 0:2, 0:D].rearrange("p s (f t) -> p s f t", f=DT)

    with nc.Block() as block:
        @block.gpsimd
        def _(pool):
            with pool.Fori(0, n_tiles // 2) as pair:
                i = pair * 2
                for s in range(2):
                    pool.wait_ge(transposed.sem, 2 * i + 2 * s + 2)
                    nc.gpsimd.tensor_copy(lhs[:, s], src[:, :, bass.ds((i + s) * P, P)]).then_inc(copied.sem, 1)

        @block.tensor
        def _(pe):
            pe.sem_inc(transposed.sem, 4)
            with pe.Fori(0, n_tiles // 2) as pair:
                i = pair * 2
                for s in range(2):
                    pe.wait_ge(copied.sem, i + s + 1)
                    for q in range(2):
                        pe.wait_ge(drained.sem, 2 * i + 2 * s + q + 1)
                        for f in range(4):
                            ins = nc.tensor.transpose(bank[2 * s + q][:, f, :], lhs[:, s, 4 * q + f, :],
                                                      k.ident[:, :])
                        ins.then_inc(transposed.sem, 1)
            for q in range(2):
                pe.wait_ge(drained.sem, 2 * n_tiles + q + 1)
                for f in range(4):
                    ins = nc.tensor.transpose(bank[q][0:DEC, f, :], src[:, 4 * q + f, SEQ:T], k.ident[:, :])
                ins.then_inc(transposed.sem, 1)

        @block.vector
        def _(dve):
            dve.sem_inc(drained.sem, 4)
            with dve.Fori(0, n_tiles // 2) as pair:
                i = pair * 2
                for s in range(2):
                    dve.wait_ge(stored[s].sem, 8 * i + 16)
                    for q in range(2):
                        dve.wait_ge(transposed.sem, 2 * i + 2 * s + q + 1 + 4)
                        nc.vector.tensor_copy(stage[:, s, 512 * q:512 * (q + 1)],
                                              bank[2 * s + q].rearrange("p f t -> p (f t)"))\
                            .then_inc(drained.sem, 1)
            dve.wait_ge(stored[0].sem, 16 * (n_tiles // 2 + 1))
            for q in range(2):
                dve.wait_ge(transposed.sem, 2 * n_tiles + q + 1 + 4)
                nc.vector.tensor_copy(stage[0:DEC, 0, 512 * q:512 * (q + 1)],
                                      bank[q][0:DEC].rearrange("p f t -> p (f t)")).then_inc(drained.sem, 1)

        @block.sync
        def _(sp):
            for s in range(2):
                sp.sem_inc(stored[s].sem, 16)
            with sp.Fori(0, n_tiles // 2) as pair:
                i = pair * 2
                for s in range(2):
                    sp.wait_ge(drained.sem, 2 * i + 2 * (s + 1) + 4)
                    sp.dma_start(k.io["y_prompt"][0, bass.ds((i + s) * P, P), :], stage[:, s, 0:D])\
                        .then_inc(stored[s].sem, 16)
            sp.wait_ge(drained.sem, 2 * n_tiles + 2 + 4)
            sp.dma_start(k.io["y_sample"].rearrange("b o d -> (b o) d"), stage[0:DEC, 0, 0:D])\
                .then_inc(stored[0].sem, 16)
            sp.wait_ge(stored[0].sem, 16 * (n_tiles // 2 + 2))
            sp.wait_ge(stored[1].sem, 16 * (n_tiles // 2 + 1))


class InverseRms:

    def __init__(self, k, name, src, n, cols, half=1.0):
        self.k, self.src, self.n, self.cols, self.half = k, src, n, cols, half
        self.tiles = [(j, min(P, cols - j * P)) for j in range((cols + P - 1) // P)]
        spare = k.W[:, :, :].rearrange("p a c -> p (a c)")
        self.slots = [(k.sq[:, 0, 0:cols], k.sq[:, 1, 0:cols]), (spare[:, 0:cols], spare[:, T:T + cols])]
        self.sums = k.ps[7][:, 0:n // 2 * 16].rearrange("p (i j) -> p j i", j=16)
        self.full = cols // P
        self.factor = k.psum_flat[:, 0:cols]
        self.act_s = Steps(k, name + "_squares", [("sq", f) for f in range(n)] + ["root"])
        self.dve_s = Steps(k, name + "_pairs", [("pair", i) for i in range(n // 2)] + ["sum", "inverse"])
        self.pe_s = Steps(k, name + "_sums", list(range(n // 2)) + ["spread"])
        self.chain = Count(k, name + "_inverse_chain")

    def columns(self, op):
        ins = op(self.k.rms_col[:, 0:self.full], self.sums[:, 0:self.full, :])
        if self.cols % P:
            m = self.cols % P
            ins = op(self.k.rms_col[0:m, self.full:self.full + 1], self.sums[0:m, self.full:self.full + 1, :])
        return ins

    def on_act(self, act):
        for f in range(self.n):
            if f % 2 == 0 and f >= 4:
                self.pe_s.wait(act, f // 2 - 2)
            self.act_s.done(self.k.nc.scalar.activation(self.slots[f // 2 % 2][f % 2], self.src[:, f, 0:self.cols],
                                                        ACT.Square), ("sq", f))
        self.dve_s.wait(act, "sum")
        self.act_s.done(self.columns(lambda out, x: self.k.nc.scalar.activation(
            out, out, ACT.Sqrt, scale=1.0 / (self.n * P), bias=self.k.eps_col[0:out.shape[0], 0:1])), "root")

    def on_dve(self, dve):
        for i in range(self.n // 2):
            a, b = self.slots[i % 2]
            self.act_s.wait(dve, ("sq", 2 * i + 1))
            self.dve_s.done(self.k.nc.vector.tensor_tensor(a, a, b, ALU.add), ("pair", i))
        self.pe_s.wait(dve, self.n // 2 - 1)
        self.dve_s.done(self.columns(lambda out, x: self.k.nc.vector.tensor_reduce(out, x, AX.X, ALU.add)), "sum")
        self.act_s.wait(dve, "root")
        ins = self.columns(lambda out, x: self.k.nc.vector.reciprocal(out, out))
        if self.half != 1.0:
            self.chain.up(ins)
            dve.wait_ge(self.chain.sem, self.chain.n)
            ins = self.columns(lambda out, x: self.k.nc.vector.tensor_scalar(out, out, self.half, None, ALU.mult))
        self.dve_s.done(ins, "inverse")
        self.pe_s.wait(dve, "spread")

    def on_pe(self, pe):
        for i in range(self.n // 2):
            self.dve_s.wait(pe, ("pair", i))
            for j, m in self.tiles:
                ins = self.k.nc.tensor.matmul(self.sums[0:m, j, i:i + 1], self.slots[i % 2][0][:, j * P:j * P + m],
                                              self.k.ones[:, 0:1], start=True, stop=True)
            self.pe_s.done(ins, i)
        self.dve_s.wait(pe, "inverse")
        for j, m in self.tiles:
            ins = self.k.nc.tensor.matmul(self.factor[:, j * P:j * P + m],
                                          self.k.rms_col[0:m, j:j + 1].to_broadcast([m, P]), self.k.ident[0:m, 0:m],
                                          start=True, stop=True)
        self.pe_s.done(ins, "spread")


@stage
def rms_norm(k, name, src, n, gain, dst=None, residual=None, half=1.0, cols=T, to_src=False, fetch=None):
    nc = k.nc
    inverse = InverseRms(k, name, src, n, cols, half)
    scaled = Count(k, name + "_scaled")
    fetched = Count(k, name + "_residual_landed")
    by_pool = [2, 4, 6] if residual is not None else []
    out = src if dst is None else dst
    to = src if to_src else residual

    with nc.Block() as block:
        if fetch is not None:
            @block.sync
            def _(sp):
                sp.dma_start(residual[:, :, :], fetch).then_inc(fetched.sem, 16)

        @block.scalar
        def _(act):
            inverse.on_act(act)

        @block.tensor
        def _(pe):
            inverse.on_pe(pe)

        def add(eng, f):
            return eng.tensor_tensor(to[:, f, :], out[:, f, :], residual[:, f, :], ALU.add)

        @block.gpsimd
        def _(pool):
            for f in by_pool:
                if fetch is not None:
                    pool.wait_ge(fetched.sem, 16)
                pool.wait_ge(scaled.sem, f + 1)
                add(nc.gpsimd, f)

        @block.vector
        def _(dve):
            inverse.on_dve(dve)
            for f in range(n):
                nc.vector.scalar_tensor_tensor(out=out[:, f, 0:cols], in0=src[:, f, 0:cols],
                                               scalar=gain[:, f:f + 1], in1=inverse.factor,
                                               op0=ALU.mult, op1=ALU.mult).then_inc(scaled.sem, 1)
            if residual is not None:
                if fetch is not None:
                    dve.wait_ge(fetched.sem, 16)
                for f in range(n):
                    if f not in by_pool:
                        dve.wait_ge(scaled.sem, f + 1)
                        add(nc.vector, f)


@stage
def project(k, name, x, kt, w_dram, col0, n, out):
    nc = k.nc
    landed = [Count(k, f"{name}_weights_landed{s}") for s in range(2)]
    multiplied = Count(k, name + "_multiplied")
    stored = Count(k, name + "_stored")
    w = k.W[:, :, 0:kt * P].rearrange("p s (f c) -> p s f c", f=kt)
    src = w_dram.rearrange("(f p) n -> p f n", p=P)

    def load(sp, s, i):
        sp.dma_start(w[:, s], src[:, :, bass.ds(col0 + i * P, P)]).then_inc(landed[s].sem, 16)

    with nc.Block() as block:
        @block.sync
        def _(sp):
            load(sp, 0, 0)
            load(sp, 1, 1)
            with sp.Fori(0, (n - 2) // 2) as pair:
                i = pair * 2
                for s in range(2):
                    sp.wait_ge(multiplied.sem, NT * i + NT * (s + 1))
                    load(sp, s, i + 2 + s)

        @block.tensor
        def _(pe):
            with pe.Fori(0, n // 2) as pair:
                i = pair * 2
                for s in range(2):
                    pe.wait_ge(landed[s].sem, 8 * i + 16)
                    for g in range(NT):
                        pe.wait_ge(stored.sem, NT * i + NT * s + g + 1)
                        for f in range(kt):
                            ins = nc.tensor.matmul(k.ps[NT * s + g][:, 0:TG], w[:, s, f], x[:, f, grp(g)],
                                                   start=(f == 0), stop=(f == kt - 1))
                        ins.then_inc(multiplied.sem, 1)

        @block.scalar
        def _(act):
            act.sem_inc(stored.sem, 2 * NT)
            with act.Fori(0, n // 2) as pair:
                i = pair * 2
                for s in range(2):
                    for g in range(NT):
                        act.wait_ge(multiplied.sem, NT * i + NT * s + g + 1)
                        nc.scalar.activation(out[:, bass.ds(i + s, 1), grp(g)],
                                             k.ps[NT * s + g][:, 0:TG].rearrange("p (a t) -> p a t", a=1),
                                             ACT.Copy).then_inc(stored.sem, 1)




class Steps:

    def __init__(self, k, name, steps, primed=False):
        self.sem = k.nc.alloc_semaphore(name=name)
        k.semaphores.append(self.sem)
        self.steps, self.per, self.primed, self.at = list(steps), len(steps), primed, 0

    def prime(self, eng):
        eng.sem_inc(self.sem, self.per)

    def done(self, ins, step):
        assert self.steps[self.at % self.per] == step, (self.steps[self.at % self.per], step)
        self.at += 1
        ins.then_inc(self.sem, 1)

    def wait(self, eng, step, it=0, before=0):
        n = self.steps.index(step) + 1 + self.per * (int(self.primed) - before)
        eng.wait_ge(self.sem, it * self.per + n)


RH, RN = 8, 64
RD = RH * RN
RT = RD // P
RPROJ = 3 * RD + 64 + 64 + 128
RPT = RPROJ // P
CH = 64
NCH = SEQ // CH
LNX_EPS = 64e-5
DECAY = float(np.exp(-0.5))


@stage
def spill(k, name, dst, src):
    landed = Count(k, name)
    with k.nc.Block() as block:
        @block.sync
        def _(sp):
            landed.up(sp.dma_start(dst, src), 16)
            sp.wait_ge(landed.sem, landed.n)


@stage
def rwkv_project(k):
    nc = k.nc
    n = RPT
    landed = [Count(k, f"rwkv_w_landed{s}") for s in range(2)]
    shift_landed = Count(k, "rwkv_shift_landed")
    shift_ready = Count(k, "rwkv_shift_ready")
    multiplied = Count(k, "rwkv_p_multiplied")
    copied = Count(k, "rwkv_p_copied")
    mixed = Count(k, "rwkv_p_mixed")
    chain = Count(k, "rwkv_mix_chain")
    rows_ready = Count(k, "shift_rows_ready")
    rows_copied = Count(k, "shift_rows_copied")
    rows_stored = Count(k, "shift_rows_stored")
    w = k.W[:, :, 0:D].rearrange("p s (f c) -> p s f c", f=DT)
    src = k.io["w_in"][0].rearrange("(f p) n -> p f n", p=P)
    rows = k.W[0:DEC + 1, 0, D:D + RPROJ]
    before = k.sq[:, 1, 0:RPT * DEC].rearrange("p (j b) -> p j b", b=DEC)
    last = k.sq[:, 1, 256:256 + RPT * (DEC + 1)].rearrange("p (j b) -> p j b", b=DEC + 1)
    flat = k.rowbuf
    diff = k.rs

    def load(sp, s, i):
        sp.dma_start(w[:, s], src[:, :, bass.ds(i * P, P)]).then_inc(landed[s].sem, 16)

    with nc.Block() as block:
        @block.sync
        def _(sp):
            load(sp, 0, 0)
            load(sp, 1, 1)
            sp.dma_start(rows[0:DEC, :], k.io["state_shift"][0]).then_inc(shift_landed.sem, 16)
            with sp.Fori(0, (n - 2) // 2) as pair:
                i = pair * 2
                for s in range(2):
                    sp.wait_ge(multiplied.sem, NT * i + NT * (s + 1))
                    load(sp, s, i + 2 + s)
            sp.wait_ge(rows_copied.sem, 4)
            sp.dma_start(k.io["shift_prompt"][0], rows[0:1, :]).then_inc(rows_stored.sem, 16)
            sp.dma_start(k.io["shift_sample"][0], rows[1:DEC + 1, :]).then_inc(rows_stored.sem, 16)
            sp.wait_ge(rows_stored.sem, 32)

        @block.tensor
        def _(pe):
            pe.wait_ge(shift_landed.sem, 16)
            for j in range(n):
                ins = nc.tensor.transpose(k.ps[7][:, j * DEC:(j + 1) * DEC], rows[0:DEC, j * P:(j + 1) * P],
                                          k.ident[0:DEC, 0:DEC])
            ins.then_inc(shift_ready.sem, 1)
            with pe.Fori(0, n // 2) as pair:
                i = pair * 2
                for s in range(2):
                    pe.wait_ge(landed[s].sem, 8 * i + 16)
                    for g in range(NT):
                        pe.wait_ge(copied.sem, NT * i + NT * s + g + 1)
                        for f in range(DT):
                            ins = nc.tensor.matmul(k.ps[NT * s + g][:, 0:TG], w[:, s, f], k.B[:, f, grp(g)],
                                                   start=(f == 0), stop=(f == DT - 1))
                        ins.then_inc(multiplied.sem, 1)
            pe.wait_ge(mixed.sem, 1 + n)
            pe.wait_ge(copied.sem, NT * n + 2 * NT)
            for q in range(4):
                for j in range(4 * q, min(4 * q + 4, n)):
                    ins = nc.tensor.transpose(k.ps[q][0:DEC + 1, (j % 4) * P:(j % 4 + 1) * P], last[:, j, :],
                                              k.ident[:, :])
                ins.then_inc(rows_ready.sem, 1)

        @block.scalar
        def _(act):
            act.sem_inc(copied.sem, 2 * NT)
            with act.Fori(0, n // 2) as pair:
                i = pair * 2
                for s in range(2):
                    act.wait_ge(mixed.sem, i + s + 1)
                    for g in range(NT):
                        act.wait_ge(multiplied.sem, NT * i + NT * s + g + 1)
                        nc.scalar.activation(flat[:, 1 + g * TG:1 + (g + 1) * TG], k.ps[NT * s + g][:, 0:TG],
                                             ACT.Copy).then_inc(copied.sem, 1)
            for q in range(4):
                act.wait_ge(rows_ready.sem, q + 1)
                wide = min(4 * P, RPROJ - 4 * q * P)
                nc.scalar.activation(rows[:, 4 * q * P:4 * q * P + wide], k.ps[q][0:DEC + 1, 0:wide], ACT.Copy)\
                    .then_inc(rows_copied.sem, 1)

        @block.vector
        def _(dve):
            nc.vector.memset(flat[:, 0:1], 0.0).then_inc(chain.sem, 1)
            dve.wait_ge(chain.sem, 1)
            dve.wait_ge(shift_ready.sem, 1)
            nc.vector.tensor_copy(before, k.ps[7][:, 0:n * DEC].rearrange("p (j b) -> p j b", b=DEC))\
                .then_inc(mixed.sem, 1)
            dve.wait_ge(mixed.sem, 1)
            with dve.Fori(0, n) as j:
                dve.wait_ge(copied.sem, NT * j + NT + 2 * NT)
                nc.vector.tensor_tensor(diff[:, 0:SEQ], flat[:, 0:SEQ], flat[:, 1:SEQ + 1], ALU.subtract)\
                    .then_inc(chain.sem, 1)
                nc.vector.tensor_tensor(diff[:, SEQ:T].rearrange("p (a b) -> p a b", a=1),
                                        before[:, bass.ds(j, 1), :],
                                        flat[:, SEQ + 1:T + 1].rearrange("p (a b) -> p a b", a=1), ALU.subtract)\
                    .then_inc(chain.sem, 1)
                nc.vector.tensor_copy(k.mu_now[:, 0:1], k.mu[:, bass.ds(j, 1)]).then_inc(chain.sem, 1)
                nc.vector.tensor_copy(last[:, bass.ds(j, 1), :],
                                      flat[:, SEQ:T + 1].rearrange("p (a b) -> p a b", a=1)).then_inc(chain.sem, 1)
                dve.wait_ge(chain.sem, 4 * j + 5)
                nc.vector.scalar_tensor_tensor(out=k.C[:, bass.ds(j, 1), :], in0=diff[:, :].rearrange("p (a t) -> p a t", a=1),
                                               scalar=k.mu_now[:, 0:1],
                                               in1=flat[:, 1:T + 1].rearrange("p (a t) -> p a t", a=1),
                                               op0=ALU.mult, op1=ALU.add).then_inc(mixed.sem, 1)
                dve.wait_ge(mixed.sem, j + 2)


@stage
def rwkv_vectors(k):
    nc = k.nc
    r, kk_, v = k.C[:, 0:4], k.C[:, 4:8], k.C[:, 8:12]
    s_, a_, kn = k.C[:, 14:18], k.C[:, 18:22], k.A[:, 0:4]
    low, gl = k.C[:, 12], k.C[:, 13]
    w2 = k.W[0:64, 0, 0:RD]
    a2 = k.W[64:128, 0, 0:RD]
    J = range(RT)
    G = range(NT)
    pe_s = Steps(k, "vec_products", [(m, j) for j in J for m in "za"] + [("sum", j) for j in J])
    act_s = Steps(k, "vec_functions", ["tanh", "gate"] + [(m, j) for j in J for m in "sa"] +
                  [("root", j) for j in J] + [(m, j) for j in J for m in ("up", "down", "prev")])
    dve_s = Steps(k, "vec_elementwise", [(m, j) for j in J for m in ("sq",)] +
                  [("kn", j) for j in J] + [(m, j) for j in J for m in ("cum", "scaled")])
    chain = Count(k, "vec_chain")
    landed = Count(k, "vec_w_landed")
    resets = k.W[:, 1, 0:SEQ]
    up, down, prev = k.sq[:, 0, 0:SEQ], k.sq[:, 1, 0:SEQ], k.rs[:, 0:SEQ]
    tmp, cum = k.A[:, 4, :], k.A[:, 5, 0:SEQ]
    cumprev = k.A[:, 6, 0:SEQ]

    with nc.Block() as block:
        @block.sync
        def _(sp):
            landed.up(sp.dma_start(w2, k.io["rwkv_w2"][0]), 16)
            landed.up(sp.dma_start(a2, k.io["rwkv_a2"][0]), 16)
            landed.up(sp.dma_start(resets, k.io["c_resets"]), 16)

        @block.tensor
        def _(pe):
            pe.wait_ge(landed.sem, 48)
            act_s.wait(pe, "tanh")
            for j in J:
                if j >= 1:
                    act_s.wait(pe, ("s", j - 1))
                for g in G:
                    ins = nc.tensor.matmul(k.ps[g][:, 0:TG], w2[:, j * P:(j + 1) * P], low[0:64, grp(g)],
                                           start=True, stop=True)
                pe_s.done(ins, ("z", j))
                if j >= 1:
                    act_s.wait(pe, ("a", j - 1))
                for g in G:
                    ins = nc.tensor.matmul(k.ps[3 + g][:, 0:TG], a2[:, j * P:(j + 1) * P], low[64:128, grp(g)],
                                           start=True, stop=True)
                pe_s.done(ins, ("a", j))
            act_s.wait(pe, ("a", RT - 1))
            for j in J:
                dve_s.wait(pe, ("sq", j))
                if j >= 1:
                    act_s.wait(pe, ("root", j - 1))
                for g in G:
                    ins = nc.tensor.matmul(k.ps[g][:, 0:TG], k.headones[:, :], k.A[:, 4 + j, grp(g)],
                                           start=True, stop=True)
                pe_s.done(ins, ("sum", j))

        @block.scalar
        def _(act):
            act_s.done(nc.scalar.activation(low[0:64], low[0:64], ACT.Tanh), "tanh")
            act_s.done(nc.scalar.activation(gl, gl, ACT.Sigmoid), "gate")
            for j in J:
                pe_s.wait(act, ("z", j))
                for g in G:
                    ins = nc.scalar.activation(s_[:, j, grp(g)], k.ps[g][:, 0:TG], ACT.Sigmoid,
                                               bias=k.w0[:, j:j + 1])
                act_s.done(ins, ("s", j))
                pe_s.wait(act, ("a", j))
                for g in G:
                    ins = nc.scalar.activation(a_[:, j, grp(g)], k.ps[3 + g][:, 0:TG], ACT.Sigmoid,
                                               bias=k.a0[:, j:j + 1])
                act_s.done(ins, ("a", j))
            for j in J:
                pe_s.wait(act, ("sum", j))
                for g in G:
                    ins = nc.scalar.activation(k.A[:, 4 + j, grp(g)], k.ps[g][:, 0:TG], ACT.Sqrt)
                act_s.done(ins, ("root", j))
            for j in J:
                dve_s.wait(act, ("cum", j))
                act_s.done(nc.scalar.activation(up, cum, ACT.Exp, scale=-DECAY), ("up", j))
                act_s.done(nc.scalar.activation(down, cum, ACT.Exp, scale=DECAY), ("down", j))
                act_s.done(nc.scalar.activation(prev, cumprev, ACT.Exp, scale=-DECAY), ("prev", j))

        @block.vector
        def _(dve):
            def link(ins):
                chain.up(ins)
                dve.wait_ge(chain.sem, chain.n)

            dve.wait_ge(landed.sem, 48)
            for j in J:
                link(nc.vector.tensor_scalar(kn[:, j], kk_[:, j], k.k_k[:, j:j + 1], None, ALU.mult))
                dve_s.done(nc.vector.tensor_tensor(k.A[:, 4 + j], kn[:, j], kn[:, j], ALU.mult), ("sq", j))
            for j in J:
                act_s.wait(dve, ("root", j))
                norm = k.A[:, 4 + j]
                link(nc.vector.tensor_scalar(norm, norm, 1e-12, None, ALU.max))
                link(nc.vector.reciprocal(norm, norm))
                link(nc.vector.tensor_tensor(kn[:, j], kn[:, j], norm, ALU.mult))
                link(nc.vector.tensor_scalar(norm, a_[:, j], -1.0, k.k_a[:, j:j + 1], ALU.add, ALU.mult))
                link(nc.vector.scalar_tensor_tensor(out=kk_[:, j], in0=norm, scalar=1.0, in1=kk_[:, j],
                                                    op0=ALU.add, op1=ALU.mult))
                dve_s.done(nc.vector.tensor_tensor(a_[:, j], kn[:, j], a_[:, j], ALU.mult), ("kn", j))
            dve_s.wait(dve, ("kn", RT - 1))
            for j in J:
                if j >= 1:
                    act_s.wait(dve, ("prev", j - 1))
                link(nc.vector.tensor_tensor_scan(cum, resets, s_[:, j, 0:SEQ], 0.0,
                                                  ALU.mult, ALU.add))
                dve_s.done(nc.vector.tensor_tensor(cumprev, cum, s_[:, j, 0:SEQ], ALU.subtract), ("cum", j))
                act_s.wait(dve, ("up", j))
                link(nc.vector.tensor_tensor(r[:, j, 0:SEQ], r[:, j, 0:SEQ], up, ALU.mult))
                link(nc.vector.tensor_copy(k.chunk_decay[:, :, j],
                                           up.rearrange("p (c t) -> p c t", t=CH)[:, :, CH - 1]))
                act_s.wait(dve, ("down", j))
                link(nc.vector.tensor_tensor(kk_[:, j, 0:SEQ], kk_[:, j, 0:SEQ], down, ALU.mult))
                link(nc.vector.tensor_tensor(a_[:, j, 0:SEQ], a_[:, j, 0:SEQ], down, ALU.mult))
                act_s.wait(dve, ("prev", j))
                dve_s.done(nc.vector.scalar_tensor_tensor(out=kn[:, j, 0:SEQ], in0=kn[:, j, 0:SEQ], scalar=-1.0,
                                                          in1=prev, op0=ALU.mult, op1=ALU.mult), ("scaled", j))


@stage
def rwkv_scan(k):
    nc = k.nc
    nhead = [(h, q) for h in range(RT) for q in range(2)]
    R2 = range(2)
    LV = [2, 4, 8, 16, 32]
    W0, W1 = k.W[:, 0], k.W[:, 1]
    base = [W0, W1]
    def view(s, at, c):
        return base[s][:, at:at + RT * c].rearrange("p (h c) -> p h c", h=RT)
    AR = [view(s, 0, 128) for s in R2]
    Bt = [view(s, 512, 64) for s in R2]
    Kt = [view(s, 768, 64) for s in R2]
    Vt = [view(s, 1024, 64) for s in R2]
    G1 = [view(s, 1280, 128) for s in R2]
    G2 = [view(s, 1792, 128) for s in R2]
    X = k.rw
    def wide(s, i, c=64):
        return X[:, s, i * 256:i * 256 + RT * c].rearrange("p (h c) -> p h c", h=RT)
    Vm = [view(s, 2304, 64) for s in R2]
    Bm = [view(s, 2560, 64) for s in R2]
    Km = [wide(s, 0) for s in R2]
    NT_ = [wide(s, 1) for s in R2]
    Tm = [wide(s, 2) for s in R2]
    TT = [wide(s, 3) for s in R2]
    Ym = [wide(s, 4) for s in R2]
    Wm = [wide(s, 5) for s in R2]
    Um = [wide(s, 6) for s in R2]
    ST = k.ST
    bank = [[k.ps[4 * s + b][:, :] for b in range(4)] for s in R2]

    def half(b, lo, c):
        return b[:, lo:lo + RT * c].rearrange("p (h c) -> p h c", h=RT)

    pe_s = Steps(k, "scan_products",
                 [(m, s) for s in R2 for m in ("gram", "turned")] +
                 [(m, s, l) for l in LV for m in ("Y", "Z") for s in R2] +
                 [(m, s) for s in R2 for m in ("W", "U", "OS")], primed=True)
    act_s = Steps(k, "scan_copies",
                  [("turned", s) for s in R2] + [("Y", s, l) for l in LV for s in R2] +
                  [(m, s) for s in R2 for m in ("W", "U", "O")], primed=True)
    dve_s = Steps(k, "scan_masks_and_sums",
                  [("gram", s) for s in R2] + [("first", s) for s in R2] +
                  [("T", s, l) for l in LV for s in R2] + [("state", s) for s in R2], primed=True)
    pool_s = Steps(k, "scan_operands", [("load", s) for s in R2] + [("level", s, l) for l in LV for s in R2])
    load_c = Count(k, "scan_loads")
    zeroed = Count(k, "scan_zeroed")
    chain = Count(k, "scan_state_chain")
    settled_at = Count(k, "scan_products_may_start")

    with nc.Block() as block:
        @block.gpsimd
        def _(pool):
            nc.gpsimd.memset(ST[:, :, :], 0.0).then_inc(zeroed.sem, 1)
            with pool.Fori(0, NCH // 2) as it:
                for s in R2:
                    pe_s.wait(pool, ("OS", s), it, before=1)
                    dve_s.wait(pool, ("state", s), it, before=1)
                    at = bass.ds((it * 2 + s) * CH, CH)
                    for src, dst in ((k.A[:, 0:4, at], AR[s][:, :, 0:64]), (k.C[:, 0:4, at], AR[s][:, :, 64:128]),
                                     (k.C[:, 18:22, at], Bt[s]), (k.C[:, 4:8, at], Kt[s]),
                                     (k.C[:, 8:12, at], Vt[s])):
                        nc.gpsimd.tensor_copy(dst, src).then_inc(load_c.sem, 1)
                    pool.wait_ge(load_c.sem, it * 10 + 5 * s + 5)
                    pool_s.done(nc.gpsimd.tensor_copy(k.decay_now[:, s:s + 1, :],
                                                      k.chunk_decay[:, bass.ds(it * 2 + s, 1), :]), ("load", s))
                for l in LV:
                    for s in R2:
                        dve_s.wait(pool, ("gram", s), it)
                        if l > 2:
                            pe_s.wait(pool, ("Y", s, l // 2), it)
                        pool_s.done(nc.gpsimd.tensor_tensor(NT_[s], G1[s][:, :, 0:64], k.level_mask[l], ALU.mult),
                                    ("level", s, l))

        @block.tensor
        def _(pe):
            pe_s.prime(pe)
            pe.wait_ge(zeroed.sem, 1)

            def settled():
                pe.sem_inc(settled_at.sem, 1)

            def mm(out, lhsT, rhs, start=True, stop=True, q=0):
                return nc.tensor.matmul(out, lhsT, rhs, start=start, stop=stop)

            def lane(t, h, q, lo=0, c=64):
                return t[64 * q:64 * q + 64, h, lo:lo + c]

            with pe.Fori(0, NCH // 2) as it:
                for s in R2:
                    b = bank[s]
                    pool_s.wait(pe, ("load", s), it)
                    act_s.wait(pe, ("O", s), it, before=1)
                    dve_s.wait(pe, ("state", s), it, before=1)
                    settled()
                    for h, q in nhead:
                        mm(lane(half(b[0], 0, 128), h, q, 0, 128), lane(Bt[s], h, q), lane(AR[s], h, q, 0, 128))
                    for h, q in nhead:
                        mm(lane(half(b[1], 0, 128), h, q, 0, 128), lane(Kt[s], h, q), lane(AR[s], h, q, 0, 128))
                    for h, q in nhead:
                        ins = mm(lane(half(b[2], 0, 64), h, q), lane(AR[s], h, q), lane(Bt[s], h, q))
                    pe_s.done(ins, ("gram", s))
                    for src, dst in ((Vt[s], half(b[3], 0, 64)), (Bt[s], half(b[3], 256, 64)), (Kt[s], half(b[2], 256, 64))):
                        if src is Kt[s]:
                            dve_s.wait(pe, ("gram", s), it)
                            settled()
                        for h, q in nhead:
                            ins = mm(lane(dst, h, q), lane(src, h, q), k.ident[64 * q:64 * q + 64, 64 * q:64 * q + 64])
                    pe_s.done(ins, ("turned", s))
                for l in LV:
                    for s in R2:
                        b = bank[s]
                        pool_s.wait(pe, ("level", s, l), it)
                        if l == 2:
                            dve_s.wait(pe, ("first", s), it)
                        else:
                            dve_s.wait(pe, ("T", s, l // 2), it)
                        settled()
                        for h, q in nhead:
                            ins = mm(lane(half(b[0], 0, 64), h, q), lane(NT_[s], h, q), lane(Tm[s], h, q))
                        pe_s.done(ins, ("Y", s, l))
                    for s in R2:
                        b = bank[s]
                        act_s.wait(pe, ("Y", s, l), it)
                        settled()
                        for h, q in nhead:
                            mm(lane(half(b[1], 0, 64), h, q), lane(TT[s], h, q), lane(Ym[s], h, q))
                        for h, q in nhead:
                            ins = mm(lane(half(b[1], 256, 64), h, q), lane(Ym[s], h, q), lane(TT[s], h, q))
                        pe_s.done(ins, ("Z", s, l))
                for s in R2:
                    b = bank[s]
                    if s == 1:
                        dve_s.wait(pe, ("state", 0), it)
                    else:
                        dve_s.wait(pe, ("state", 1), it, before=1)
                    act_s.wait(pe, ("turned", s), it)
                    dve_s.wait(pe, ("T", s, LV[-1]), it)
                    settled()
                    for h, q in nhead:
                        mm(lane(half(b[0], 0, 64), h, q), lane(AR[s], h, q), lane(ST, h, q), stop=False)
                        ins = mm(lane(half(b[0], 0, 64), h, q), lane(G2[s], h, q), lane(Vm[s], h, q), start=False)
                    pe_s.done(ins, ("W", s))
                    act_s.wait(pe, ("W", s), it)
                    settled()
                    for h, q in nhead:
                        ins = mm(lane(half(b[1], 0, 64), h, q), lane(TT[s], h, q), lane(Wm[s], h, q))
                    pe_s.done(ins, ("U", s))
                    act_s.wait(pe, ("U", s), it)
                    settled()
                    for h, q in nhead:
                        mm(lane(half(b[3], 0, 64), h, q), lane(Bm[s], h, q), lane(Um[s], h, q), stop=False)
                        mm(lane(half(b[3], 0, 64), h, q), lane(Km[s], h, q), lane(Vm[s], h, q), start=False)
                    for h, q in nhead:
                        o = lane(half(b[2], 0, 64), h, q)
                        mm(o, lane(ST, h, q), lane(AR[s], h, q, 64), stop=False)
                        mm(o, lane(Um[s], h, q), lane(G1[s], h, q, 64), start=False, stop=False)
                        ins = mm(o, lane(Vm[s], h, q), lane(G2[s], h, q, 64), start=False)
                    pe_s.done(ins, ("OS", s))

        @block.scalar
        def _(act):
            act_s.prime(act)
            with act.Fori(0, NCH // 2) as it:
                for s in R2:
                    b = bank[s]
                    pe_s.wait(act, ("turned", s), it)
                    nc.scalar.activation(Vm[s], half(b[3], 0, 64), ACT.Copy)
                    nc.scalar.activation(Bm[s], half(b[3], 256, 64), ACT.Copy)
                    act_s.done(nc.scalar.activation(Km[s], half(b[2], 256, 64), ACT.Copy), ("turned", s))
                for l in LV:
                    for s in R2:
                        pe_s.wait(act, ("Y", s, l), it)
                        act_s.done(nc.scalar.activation(Ym[s], half(bank[s][0], 0, 64), ACT.Copy), ("Y", s, l))
                for s in R2:
                    b = bank[s]
                    pe_s.wait(act, ("W", s), it)
                    act_s.done(nc.scalar.activation(Wm[s], half(b[0], 0, 64), ACT.Copy), ("W", s))
                    pe_s.wait(act, ("U", s), it)
                    act_s.done(nc.scalar.activation(Um[s], half(b[1], 0, 64), ACT.Copy), ("U", s))
                    pe_s.wait(act, ("OS", s), it)
                    act_s.done(nc.scalar.activation(k.C[:, 14:18, bass.ds((it * 2 + s) * CH, CH)],
                                                    half(b[2], 0, 64), ACT.Copy), ("O", s))

        @block.vector
        def _(dve):
            dve_s.prime(dve)
            with dve.Fori(0, NCH // 2) as it:
                for s in R2:
                    b = bank[s]
                    pe_s.wait(dve, ("gram", s), it)
                    pool_s.wait(dve, ("load", s), it)
                    nc.vector.tensor_tensor(G1[s], half(b[0], 0, 128), k.gram_mask, ALU.mult)
                    nc.vector.tensor_tensor(G2[s], half(b[1], 0, 128), k.gram_mask, ALU.mult)
                    dve_s.done(nc.vector.tensor_tensor(Tm[s], half(b[2], 0, 64), k.first_mask, ALU.mult),
                               ("gram", s))
                for s in R2:
                    dve_s.wait(dve, ("gram", s), it)
                    nc.vector.tensor_tensor(TT[s], G1[s][:, :, 0:64], k.first_mask_t, ALU.mult).then_inc(chain.sem, 1)
                    dve.wait_ge(chain.sem, it * 6 + 2 * s + 1)
                    nc.vector.tensor_tensor(Tm[s], Tm[s], k.ident4, ALU.add).then_inc(chain.sem, 1)
                    dve.wait_ge(chain.sem, it * 6 + 2 * s + 2)
                    dve_s.done(nc.vector.tensor_tensor(TT[s], TT[s], k.ident4, ALU.add), ("first", s))
                for l in LV:
                    for s in R2:
                        pe_s.wait(dve, ("Z", s, l), it)
                        if l == 2:
                            dve_s.wait(dve, ("first", s), it)
                        else:
                            dve_s.wait(dve, ("T", s, l // 2), it)
                        nc.vector.tensor_tensor(Tm[s], Tm[s], half(bank[s][1], 0, 64), ALU.add)
                        dve_s.done(nc.vector.tensor_tensor(TT[s], TT[s], half(bank[s][1], 256, 64), ALU.add),
                                   ("T", s, l))
                for s in R2:
                    pe_s.wait(dve, ("OS", s), it)
                    nc.vector.tensor_tensor(ST[:, :, :], ST[:, :, :], half(bank[s][3], 0, 64), ALU.add)\
                        .then_inc(chain.sem, 1)
                    dve.wait_ge(chain.sem, it * 6 + s + 5)
                    dve_s.done(nc.vector.tensor_tensor(ST[:, :, :], ST[:, :, :],
                                                       k.decay_now[:, s, :].unsqueeze(2).to_broadcast([P, RT, RN]),
                                                       ALU.mult), ("state", s))
                    dve_s.wait(dve, ("state", s), it)


@stage
def rwkv_sample_step(k):
    nc = k.nc
    names = "rwkvab"
    srcs = [k.C[:, 0:4], k.C[:, 14:18], k.C[:, 4:8], k.C[:, 8:12], k.A[:, 0:4], k.C[:, 18:22]]
    W = k.W[:, :, :].rearrange("p s c -> p (s c)")
    S = W[:, 0:2048].rearrange("p (i j) -> p i j", j=RN)
    tmp = W[:, 2048:4096].rearrange("p (i j) -> p i j", j=RN)
    rows = k.rwflat[0:DEC, 0:6 * RD].rearrange("p (m c) -> p m c", m=6)
    vec = W[:, 4096:4096 + 6 * 64].rearrange("p (m c) -> p m c", m=6)
    sa = W[:, 4480:4512]
    o = W[:, 4512:4544]
    vrow = W[:, 4544:4576]
    orow = k.rwflat[0:DEC, 0:RD]
    state_landed = Count(k, "state_landed")
    turned = Count(k, "vectors_turned")
    copied = Count(k, "vectors_copied")
    put = Count(k, "vectors_put")
    got = Count(k, "vectors_got")
    decayed = Count(k, "decay_ready")
    chain = Count(k, "step_chain")
    stepped = Count(k, "step_done")
    stored = Count(k, "step_stored")
    o_put = Count(k, "o_put")
    o_got = Count(k, "o_got")
    o_turned = Count(k, "o_turned")
    st_turned = Count(k, "prompt_state_turned")
    st_copied = Count(k, "prompt_state_copied")
    rows2 = k.t_scratch.rearrange("m b c -> b m c")
    state = k.io["state_rwkv"][0].rearrange("b h (x i) j -> (b h x) i j", x=2)
    state_out = k.io["wkv_sample"][0].rearrange("b h (x i) j -> (b h x) i j", x=2)

    with nc.Block() as block:
        @block.sync
        def _(sp):
            sp.dma_start(S, state).then_inc(state_landed.sem, 16)
            sp.wait_ge(copied.sem, 6)
            sp.dma_start(rows2, rows).then_inc(put.sem, 16)
            sp.wait_ge(put.sem, 16)
            for m in range(6):
                src = k.t_scratch[m].rearrange("b (h c) -> (b h) c", c=RN).unsqueeze(1).to_broadcast([64, 2, RN])
                sp.dma_start(vec[:, m], src).then_inc(got.sem, 16)
            sp.dma_start(vrow, k.t_scratch[3].rearrange("b (x c) -> (b x) c", c=32)).then_inc(got.sem, 16)
            sp.wait_ge(st_copied.sem, 1)
            for q in range(2):
                sp.dma_start(k.io["wkv_prompt"][0, 0].rearrange("(h q) i j -> q i h j", q=2)[q],
                             k.st_rows[64 * q:64 * q + 64]).then_inc(stored.sem, 16)
            sp.wait_ge(stepped.sem, 1)
            sp.dma_start(state_out, S).then_inc(stored.sem, 16)
            sp.wait_ge(stepped.sem, 2)
            sp.dma_start(k.o_scratch.rearrange("b (x c) -> (b x) c", c=32), o).then_inc(o_put.sem, 16)
            sp.wait_ge(o_put.sem, 16)
            sp.dma_start(orow, k.o_scratch).then_inc(o_got.sem, 16)
            sp.wait_ge(stored.sem, 48)

        @block.tensor
        def _(pe):
            for m in range(6):
                if m == 1:
                    pe.wait_ge(decayed.sem, 1)
                for j in range(RT):
                    ins = nc.tensor.transpose(k.ps[m][0:DEC, j * P:(j + 1) * P], srcs[m][:, j, SEQ:T], k.ident[:, :])
                ins.then_inc(turned.sem, 1)
            for h in range(RT):
                for q in range(2):
                    l = slice(64 * q, 64 * q + 64)
                    ins = nc.tensor.matmul(k.ps[6][l, h * RN:(h + 1) * RN], k.ST[l, h, :], k.ident[l, l],
                                           start=True, stop=True)
            ins.then_inc(st_turned.sem, 1)
            pe.wait_ge(o_got.sem, 16)
            for j in range(RT):
                ins = nc.tensor.transpose(k.ps[7][:, j * DEC:(j + 1) * DEC], orow[:, j * P:(j + 1) * P],
                                          k.ident[0:DEC, 0:DEC])
            ins.then_inc(o_turned.sem, 1)

        @block.scalar
        def _(act):
            nc.scalar.activation(srcs[1][:, :, SEQ:T], srcs[1][:, :, SEQ:T], ACT.Exp, scale=-DECAY)\
                .then_inc(decayed.sem, 1)
            for m in range(6):
                act.wait_ge(turned.sem, m + 1)
                nc.scalar.activation(rows[:, m], k.ps[m][0:DEC, :], ACT.Copy).then_inc(copied.sem, 1)
            act.wait_ge(st_turned.sem, 1)
            nc.scalar.activation(k.st_rows[:, :, :], k.ps[6][:, 0:RT * RN].rearrange("p (h c) -> p h c", h=RT),
                                 ACT.Copy).then_inc(st_copied.sem, 1)
            act.wait_ge(o_turned.sem, 1)
            nc.scalar.activation(k.C[:, 14:18, SEQ:T], k.ps[7][:, 0:RT * DEC].rearrange("p (j b) -> p j b", b=DEC),
                                 ACT.Copy)

        @block.vector
        def _(dve):
            def link(ins):
                chain.up(ins)
                dve.wait_ge(chain.sem, chain.n)

            def over_rows(m):
                return vec[:, m].unsqueeze(1).to_broadcast([P, 32, RN])

            def over_cols(x):
                return x.unsqueeze(2).to_broadcast([P, 32, RN])

            dve.wait_ge(state_landed.sem, 16)
            dve.wait_ge(got.sem, 7 * 16)
            link(nc.vector.tensor_tensor(tmp, S, over_rows(4), ALU.mult))
            link(nc.vector.tensor_reduce(sa, tmp, AX.X, ALU.add))
            link(nc.vector.tensor_tensor(S, S, over_rows(1), ALU.mult))
            link(nc.vector.tensor_tensor(tmp, over_cols(sa), over_rows(5), ALU.mult))
            link(nc.vector.tensor_tensor(S, S, tmp, ALU.subtract))
            link(nc.vector.tensor_tensor(tmp, over_cols(vrow), over_rows(2), ALU.mult))
            nc.vector.tensor_tensor(S, S, tmp, ALU.add).then_inc(stepped.sem, 1)
            dve.wait_ge(stepped.sem, 1)
            link(nc.vector.tensor_tensor(tmp, S, over_rows(0), ALU.mult))
            nc.vector.tensor_reduce(o, tmp, AX.X, ALU.add).then_inc(stepped.sem, 1)


@stage
def rwkv_finish(k):
    nc = k.nc
    r, kk_, v, gl = k.C[:, 0:4], k.C[:, 4:8], k.C[:, 8:12], k.C[:, 13]
    o, out = k.C[:, 14:18], k.A[:, 4:8]
    J, G = range(RT), range(NT)
    pe_s = Steps(k, "fin_sums", [(m, j) for j in J for m in ("mean", "bonus", "var", "g")])
    act_s = Steps(k, "fin_functions", [(m, j) for j in J for m in ("root", "g")])
    dve_s = Steps(k, "fin_elementwise", [(m, j) for j in J for m in ("rk", "centred", "done")])
    chain = Count(k, "fin_chain")
    landed = Count(k, "g2_landed")
    g2 = k.W[:, 0, 0:RD]
    bonus = k.sq[:, 0, :]
    square = k.sq[:, 1, :]
    with nc.Block() as block:
        @block.sync
        def _(sp):
            sp.dma_start(g2, k.io["rwkv_g2"][0]).then_inc(landed.sem, 16)

        @block.tensor
        def _(pe):
            pe.wait_ge(landed.sem, 16)
            for j in J:
                if j:
                    dve_s.wait(pe, ("done", j - 1))
                for g in G:
                    ins = nc.tensor.matmul(k.ps[g][:, 0:TG], k.headones[:, :], o[:, j, grp(g)], start=True, stop=True)
                pe_s.done(ins, ("mean", j))
                dve_s.wait(pe, ("rk", j))
                for g in G:
                    ins = nc.tensor.matmul(k.ps[3 + g][:, 0:TG], k.headones[:, :], bonus[:, grp(g)], start=True, stop=True)
                pe_s.done(ins, ("bonus", j))
                dve_s.wait(pe, ("centred", j))
                for g in G:
                    ins = nc.tensor.matmul(k.ps[g][:, 0:TG], k.headones[:, :], square[:, grp(g)], start=True, stop=True)
                pe_s.done(ins, ("var", j))
                act_s.wait(pe, ("root", j))
                for g in G:
                    ins = nc.tensor.matmul(k.ps[g][:, 0:TG], g2[:, j * P:(j + 1) * P], gl[:, grp(g)], start=True, stop=True)
                pe_s.done(ins, ("g", j))

        @block.scalar
        def _(act):
            for j in J:
                pe_s.wait(act, ("var", j))
                if j:
                    dve_s.wait(act, ("done", j - 1))
                for g in G:
                    ins = nc.scalar.activation(k.rs[:, grp(g)], k.ps[g][:, 0:TG], ACT.Sqrt, scale=1.0 / RN,
                                               bias=k.lnx_eps[:, 0:1])
                act_s.done(ins, ("root", j))
                pe_s.wait(act, ("g", j))
                if j:
                    dve_s.wait(act, ("done", j - 1))
                for g in G:
                    ins = nc.scalar.activation(k.gbuf[:, grp(g)], k.ps[g][:, 0:TG], ACT.Copy)
                act_s.done(ins, ("g", j))

        @block.vector
        def _(dve):
            def link(ins):
                chain.up(ins)
                dve.wait_ge(chain.sem, chain.n)
            for j in J:
                dve_s.done(nc.vector.scalar_tensor_tensor(out=bonus, in0=r[:, j], scalar=k.r_k[:, j:j + 1],
                                                          in1=kk_[:, j], op0=ALU.mult, op1=ALU.mult), ("rk", j))
                pe_s.wait(dve, ("mean", j))
                for g in G:
                    nc.vector.scalar_tensor_tensor(out=o[:, j, grp(g)], in0=k.ps[g][:, 0:TG], scalar=-1.0 / RN,
                                                   in1=o[:, j, grp(g)], op0=ALU.mult, op1=ALU.add)\
                        .then_inc(chain.sem, 1)
                chain.n += NT
                dve.wait_ge(chain.sem, chain.n)
                dve_s.done(nc.vector.tensor_tensor(square, o[:, j], o[:, j], ALU.mult), ("centred", j))
                pe_s.wait(dve, ("bonus", j))
                for g in G:
                    nc.vector.tensor_tensor(out[:, j, grp(g)], k.ps[3 + g][:, 0:TG], v[:, j, grp(g)], ALU.mult)\
                        .then_inc(chain.sem, 1)
                chain.n += NT
                act_s.wait(dve, ("root", j))
                dve.wait_ge(chain.sem, chain.n)
                link(nc.vector.reciprocal(k.rs[:, :], k.rs[:, :]))
                link(nc.vector.scalar_tensor_tensor(out=o[:, j], in0=o[:, j], scalar=k.lnx_g[:, j:j + 1],
                                                    in1=k.rs[:, :], op0=ALU.mult, op1=ALU.mult))
                link(nc.vector.scalar_tensor_tensor(out=out[:, j], in0=o[:, j], scalar=k.lnx_b[:, j:j + 1],
                                                    in1=out[:, j], op0=ALU.add, op1=ALU.add))
                act_s.wait(dve, ("g", j))
                dve_s.done(nc.vector.tensor_tensor(out[:, j], out[:, j], k.gbuf[:, :], ALU.mult), ("done", j))
                dve_s.wait(dve, ("done", j))



R32 = mybir.dt.float32r


@stage
def rms_split(k, name, gain, spill_to):
    nc = k.nc
    inverse = InverseRms(k, name, k.A, DT, T)
    high = Count(k, name + "_high")
    scaled = Count(k, name + "_scaled")
    spilled = Count(k, name + "_spilled")
    by_pool = [1, 3, 5]
    with nc.Block() as block:
        @block.sync
        def _(sp):
            sp.dma_start(spill_to, k.A[:, :, :]).then_inc(spilled.sem, 16)

        @block.tensor
        def _(pe):
            inverse.on_pe(pe)

        @block.scalar
        def _(act):
            inverse.on_act(act)
            for f in range(DT):
                act.wait_ge(scaled.sem, f + 1)
                nc.scalar.activation(k.XR[:, 0, f, :], k.A[:, f, :], ACT.Copy).then_inc(high.sem, 1)

        def low_part(eng, on, f):
            eng.wait_ge(high.sem, f + 1)
            on.tensor_tensor(k.XR[:, 1, f, :], k.A[:, f, :], k.XR[:, 0, f, :].bitcast(F32), ALU.subtract)

        @block.gpsimd
        def _(pool):
            for f in by_pool:
                low_part(pool, nc.gpsimd, f)

        @block.vector
        def _(dve):
            inverse.on_dve(dve)
            dve.wait_ge(spilled.sem, 16)
            for f in range(DT + 1):
                if f < DT:
                    nc.vector.scalar_tensor_tensor(out=k.A[:, f, :], in0=k.A[:, f, :], scalar=gain[:, f:f + 1],
                                                   in1=inverse.factor, op0=ALU.mult, op1=ALU.mult)\
                        .then_inc(scaled.sem, 1)
                if f > 0 and f - 1 not in by_pool:
                    low_part(dve, nc.vector, f - 1)


@stage
def ffn_core(k, name, w_gate, w_up, w_down):
    nc = k.nc
    N = FT // 2
    G = range(NT)
    U = ("gu0", "gu1", "down")
    raw = {u: k.wraw[:, i, :] for i, u in enumerate(U)}
    wr = {u: k.wR[:, i] for i, u in enumerate(U)}
    gu_src = [t.rearrange("(f p) n -> p f n", p=P) for t in (w_gate, w_up)]
    dn_src = w_down.rearrange("(f p) n -> p f n", p=P)
    gu_steps = [("gu", t, g) for t in range(2) for g in G]
    dn_steps = [("dn", g, j) for g in G for j in range(DT)]
    landed = {u: Count(k, f"{name}_{u}_landed") for u in U}
    pe_s = Steps(k, name + "_products", gu_steps + dn_steps, primed=True)
    work = [("w", "gu1"), (0, 0), ("w", "down"), (0, 1), (0, 2), (1, 0), ("w", "gu0"), (1, 1), (1, 2)]

    def steps_of(kinds):
        return [s for m in work for s in ([m] if m[0] == "w" else [(x,) + m for x in kinds])]

    act_s = Steps(k, name + "_functions", steps_of(("sig", "hi")), primed=True)
    dve_s = Steps(k, name + "_sums", steps_of(("silu", "h", "lo")) + dn_steps, primed=True)
    first = Count(k, name + "_first_weights_high")
    first_split = Count(k, name + "_first_weights_split")
    cleared = Count(k, name + "_cleared")
    sig = [k.t6[:, i, :] for i in range(3)]
    h = [k.t6[:, 3 + i, :] for i in range(3)]
    last_gu = {"gu0": ("gu", 0, NT - 1), "gu1": ("gu", 1, NT - 1), "down": ("dn", NT - 1, DT - 1)}

    def load(sp, u, i):
        if u == "down":
            sp.dma_start(raw[u].rearrange("p (f c) -> p f c", f=2), dn_src[:, bass.ds(i * 2, 2), :])\
                .then_inc(landed[u].sem, 16)
            return
        t = int(u[2])
        for m in range(2):
            sp.dma_start(raw[u][:, m * D:(m + 1) * D].rearrange("p (f c) -> p f c", f=DT),
                         gu_src[m][:, :, bass.ds((i * 2 + t) * P, P)]).then_inc(landed[u].sem, 16)

    with nc.Block() as block:
        @block.gpsimd
        def _(pool):
            nc.gpsimd.memset(k.A[:, :, :], 0.0).then_inc(cleared.sem, 1)

        @block.sync
        def _(sp):
            for u in U:
                load(sp, u, 0)
            sp.wait_ge(first_split.sem, 1)
            load(sp, "gu0", 1)

            def refill(u, it, i):
                dve_s.wait(sp, ("w", u), it)
                sp.sem_inc(k.settled.sem, 1)
                load(sp, u, i)

            with sp.Fori(0, N - 2) as it:
                refill("gu1", it, it + 1)
                refill("down", it, it + 1)
                refill("gu0", it, it + 2)
            refill("gu1", N - 2, N - 1)
            refill("down", N - 2, N - 1)

        @block.tensor
        def _(pe):
            pe_s.prime(pe)

            def three(out, wgt, cols, x, g, first, last):
                for n, (a, b) in enumerate(((0, 0), (0, 1), (1, 0))):
                    ins = nc.tensor.matmul(out, wgt[:, a, cols], x(b)[:, grp(g)],
                                           start=first and n == 0, stop=last and n == 2)
                return ins

            pe.wait_ge(first_split.sem, 1)
            with pe.Fori(0, N) as it:
                for t in range(2):
                    u = f"gu{t}"
                    dve_s.wait(pe, ("w", u), it, before=1 - t)
                    for g in G:
                        n = NT * t + g
                        if n >= 2:
                            dve_s.wait(pe, ("h",) + gu_steps[n - 2][1:], it)
                        else:
                            dve_s.wait(pe, ("h",) + gu_steps[2 * NT - 2 + n][1:], it, before=1)
                        for m in range(2):
                            for f in range(DT):
                                ins = three(k.ps[2 * (n % 2) + m][:, 0:TG], wr[u],
                                            slice(m * D + f * P, m * D + (f + 1) * P),
                                            lambda b, f=f: k.XR[:, b, f, :], g, f == 0, f == DT - 1)
                        pe_s.done(ins, ("gu", t, g))
                dve_s.wait(pe, ("w", "down"), it)
                for g in G:
                    dve_s.wait(pe, ("lo", 1, g), it)
                    for j in range(DT):
                        n = g * DT + j
                        if n >= 4:
                            dve_s.wait(pe, dn_steps[n - 4], it)
                        else:
                            dve_s.wait(pe, dn_steps[len(dn_steps) - 4 + n], it, before=1)
                        for t in range(2):
                            ins = three(k.ps[4 + n % 4][:, 0:TG], wr["down"], slice(t * D + j * P, t * D + (j + 1) * P),
                                        lambda b, t=t: k.hidR[:, b, t, :], g, t == 0, t == 1)
                        pe_s.done(ins, ("dn", g, j))

        def whole(eng, once):
            with eng.Fori(0, N - 1) as it:
                once(it, False)
            once(N - 1, True)

        @block.scalar
        def _(act):
            act.wait_ge(landed["gu0"].sem, 32)
            nc.scalar.activation(wr["gu0"][:, 0, :], raw["gu0"], ACT.Copy).then_inc(first.sem, 1)
            act_s.prime(act)

            def once(it, last):
                for m in work:
                    if m[0] == "w":
                        u = m[1]
                        if u == "gu0":
                            if not last:
                                act.wait_ge(landed[u].sem, (it + 2) * 32)
                            pe_s.wait(act, last_gu[u], it)
                        else:
                            act.wait_ge(landed[u].sem, (it + 1) * (16 if u == "down" else 32))
                            pe_s.wait(act, last_gu[u], it, before=1)
                        n = 1 if last and u == "gu0" else 2 * D
                        act_s.done(nc.scalar.activation(wr[u][:, 0, 0:n], raw[u][:, 0:n], ACT.Copy), m)
                        continue
                    t, g = m
                    n = NT * t + g
                    pe_s.wait(act, ("gu", t, g), it)
                    dve_s.wait(act, ("h", 1 - t, g), it, before=1 - t)
                    act_s.done(nc.scalar.activation(sig[g], k.ps[2 * (n % 2)][:, 0:TG], ACT.Sigmoid), ("sig", t, g))
                    dve_s.wait(act, ("h", t, g), it)
                    if t == 0 and g == 0:
                        pe_s.wait(act, last_gu["down"], it, before=1)
                    act_s.done(nc.scalar.activation(k.hidR[:, 0, t, grp(g)], h[g], ACT.Copy), ("hi", t, g))

            whole(act, once)

        @block.vector
        def _(dve):
            dve.wait_ge(first.sem, 1)
            nc.vector.tensor_tensor(wr["gu0"][:, 1, :], raw["gu0"], wr["gu0"][:, 0, :].bitcast(F32), ALU.subtract)\
                .then_inc(first_split.sem, 1)
            dve_s.prime(dve)
            dve.wait_ge(cleared.sem, 1)

            def once(it, last):
                for m in work:
                    if m[0] == "w":
                        u = m[1]
                        act_s.wait(dve, m, it)
                        n = 1 if last and u == "gu0" else 2 * D
                        dve_s.done(nc.vector.tensor_tensor(wr[u][:, 1, 0:n], raw[u][:, 0:n], wr[u][:, 0, 0:n].bitcast(F32),
                                                           ALU.subtract), m)
                        continue
                    t, g = m
                    n = NT * t + g
                    act_s.wait(dve, ("sig", t, g), it)
                    dve_s.done(nc.vector.tensor_tensor(sig[g], sig[g], k.ps[2 * (n % 2)][:, 0:TG], ALU.mult),
                               ("silu", t, g))
                    dve_s.wait(dve, ("silu", t, g), it)
                    dve_s.done(nc.vector.tensor_tensor(h[g], sig[g], k.ps[2 * (n % 2) + 1][:, 0:TG], ALU.mult),
                               ("h", t, g))
                    act_s.wait(dve, ("hi", t, g), it)
                    dve_s.done(nc.vector.tensor_tensor(k.hidR[:, 1, t, grp(g)], h[g],
                                                       k.hidR[:, 0, t, grp(g)].bitcast(F32), ALU.subtract),
                               ("lo", t, g))
                for n, (_, g, j) in enumerate(dn_steps):
                    pe_s.wait(dve, ("dn", g, j), it)
                    if n == 0:
                        dve_s.wait(dve, dn_steps[-1], it, before=1)
                    dve_s.done(nc.vector.tensor_tensor(k.A[:, j, grp(g)], k.A[:, j, grp(g)], k.ps[4 + n % 4][:, 0:TG],
                                                       ALU.add), ("dn", g, j))

            whole(dve, once)


def ffn(k, name, pre, post, w_gate, w_up, w_down):
    rms_split(k, name + "_pre", pre, k.h_spill)
    ffn_core(k, name, w_gate, w_up, w_down)
    rms_norm(k, name + "_post", k.A, DT, post, residual=k.B, half=0.5, to_src=True, fetch=k.h_spill)


MH_, RT_ = 8, 4
NOPE, ROPE, VH = 64, 32, 64
QH = NOPE + ROPE
QL, KVL = 768, 256
QT, KT = QL // P, KVL // P
CW = KVL + ROPE
MLA_SCALE = QH ** -0.5
PAST, PAGE = 2048, 128
NPAGE = PAST // PAGE
MEM, MH = 256, 4
MTOK = MEM // P
MEM_SCALE = P ** -0.5
COL_Q = RPROJ
COL_PE = COL_Q + QL + KVL
COL_MEM = COL_PE + ROPE
COL_GATE = COL_MEM + MH * P
NEG = -1e30
NQ = SEQ // P


@stage
def key_rope(k):
    nc = k.nc
    pe_rows = slice(NOPE, QH)
    cos, sin = k.C[pe_rows, 9, :], k.C[pe_rows, 10, :]
    key, tmp = k.C[pe_rows, 8, :], k.C[pe_rows, 11, :]
    w = k.W[:, 0, 0:DT * ROPE].rearrange("p (f c) -> p f c", f=DT)
    G = range(NT)
    landed = Count(k, "pe_w_landed")
    pe_s = Steps(k, "pe_products", ["key", "swap"] + [("rows", i) for i in range(NQ + 1)])
    act_s = Steps(k, "pe_copies", ["key"] + [("rows", i) for i in range(NQ + 1)])
    dve_s = Steps(k, "pe_rotated", ["cos", "sin", "key"])
    stored = [Count(k, f"rows_stored{s}") for s in range(2)]
    stage = [k.W[:, 0, 512 + CW * s:512 + CW * (s + 1)] for s in range(2)]
    with nc.Block() as block:
        @block.sync
        def _(sp):
            src = k.io["w_in"][0].rearrange("(f p) n -> p f n", p=P)[:, :, COL_PE:COL_PE + ROPE]
            with nc.allow_non_contiguous_dma("32 columns"):
                sp.dma_start(w, src).then_inc(landed.sem, 16)
            sp.dma_start(cos, k.io["c_cos"]).then_inc(landed.sem, 16)
            sp.dma_start(sin, k.io["c_sin"]).then_inc(landed.sem, 16)
            sp.dma_start(k.perm[pe_rows, :], k.io["c_perm"]).then_inc(landed.sem, 16)
            for i in range(NQ):
                act_s.wait(sp, ("rows", i))
                sp.dma_start(k.io["rows_prompt"][0, 0, i * P:(i + 1) * P, :], stage[i % 2]).then_inc(stored[i % 2].sem, 16)
            act_s.wait(sp, ("rows", NQ))
            sp.dma_start(k.io["rows_sample"][0].rearrange("b o c -> (b o) c"), stage[NQ % 2][0:DEC])\
                .then_inc(stored[NQ % 2].sem, 16)
            for s in range(2):
                sp.wait_ge(stored[s].sem, 16 * len(range(s, NQ + 1, 2)))

        @block.tensor
        def _(pe):
            pe.wait_ge(landed.sem, 64)
            for g in G:
                for f in range(DT):
                    ins = nc.tensor.matmul(k.ps[g][pe_rows, 0:TG], w[:, f], k.B[:, f, grp(g)],
                                           start=(f == 0), stop=(f == DT - 1))
            pe_s.done(ins, "key")
            act_s.wait(pe, "key")
            for g in G:
                ins = nc.tensor.matmul(k.ps[3 + g][pe_rows, 0:TG], k.perm[pe_rows, :], key[:, grp(g)],
                                       start=True, stop=True)
            pe_s.done(ins, "swap")
            dve_s.wait(pe, "key")
            for i in range(NQ + 1):
                n = P if i < NQ else DEC
                cols = slice(i * P, i * P + n)
                b = k.ps[6 + i % 2]
                if i >= 2:
                    act_s.wait(pe, ("rows", i - 2))
                for f in range(KT):
                    nc.tensor.transpose(b[0:n, f * P:(f + 1) * P], k.C[:, 6 + f, cols], k.ident[:, :])
                pe_s.done(nc.tensor.transpose(b[0:n, KVL:CW], k.C[pe_rows, 8, cols], k.ident[pe_rows, pe_rows]),
                          ("rows", i))

        @block.scalar
        def _(act):
            pe_s.wait(act, "key")
            for g in G:
                ins = nc.scalar.activation(key[:, grp(g)], k.ps[g][pe_rows, 0:TG], ACT.Copy)
            act_s.done(ins, "key")
            for i in range(NQ + 1):
                n = P if i < NQ else DEC
                pe_s.wait(act, ("rows", i))
                if i >= 2:
                    act.wait_ge(stored[i % 2].sem, 16 * (i // 2))
                act_s.done(nc.scalar.activation(stage[i % 2][0:n], k.ps[6 + i % 2][0:n, 0:CW], ACT.Copy), ("rows", i))

        @block.vector
        def _(dve):
            dve.wait_ge(landed.sem, 64)
            pe_s.wait(dve, "swap")
            for g in G:
                ins = nc.vector.tensor_tensor(tmp[:, grp(g)], k.ps[3 + g][pe_rows, 0:TG], sin[:, grp(g)], ALU.mult)
            dve_s.done(ins, "cos")
            act_s.wait(dve, "key")
            dve_s.done(nc.vector.tensor_tensor(key, key, cos, ALU.mult), "sin")
            dve_s.wait(dve, "sin")
            dve_s.done(nc.vector.tensor_tensor(key, key, tmp, ALU.add), "key")
            dve_s.wait(dve, "key")
            for s in range(2):
                nc.vector.tensor_copy(k.C[pe_rows, 13 + s, :], key)


@stage
def prompt_attention(k, name, mla):
    nc = k.nc
    heads = MH_ if mla else MH
    depth = QH if mla else P
    nq = NQ
    S2, G = range(2), range(NT)
    kq = QT if mla else DT
    xq = k.C[:, 0:QT] if mla else k.B
    scale = MLA_SCALE if mla else MEM_SCALE
    wide = VH if mla else P
    q_buf = [k.C[:, 11 + s, :] if mla else k.C[:, s, :] for s in S2]
    k_buf = [k.C[:, 13 + s, :] if mla else k.C[:, 2 + s, 0:MEM] for s in S2]
    v_buf = [(k.C[:, 15, s * 512:(s + 1) * 512].rearrange("p (t c) -> p t c", t=NQ) if mla else
              k.C[:, 4, s * 256:(s + 1) * 256].rearrange("p (t c) -> p t c", t=MTOK)) for s in S2]
    prob = [k.C[:, 16 + s, 0:SEQ] if mla else k.C[:, 6 + s, 0:SEQ] for s in S2]
    probT = [k.C[:, 18 + s, 0:SEQ] if mla else k.C[:, 8 + s, 0:SEQ] for s in S2]
    wq = [k.W[:, s, 0:kq * depth].rearrange("p (f c) -> p f c", f=kq) for s in S2]
    wk = [k.W[:, s, 1024:1024 + KT * NOPE].rearrange("p (f c) -> p f c", f=KT) for s in S2]
    wv = [k.W[:, s, 1280:1280 + KT * VH].rearrange("p (f c) -> p f c", f=KT) for s in S2]
    nw = 3 if mla else 1
    keys = [(i + 1) * P if mla else MEM for i in range(nq)]
    blocks = [n // P for n in keys]
    pe_rows = slice(NOPE, QH)
    cos, sin = k.C[pe_rows, 9, :], k.C[pe_rows, 10, :]

    landed = [Count(k, f"{name}_w_landed{s}") for s in S2]
    head_steps = [("q", g) for g in G] + ([("k", g) for g in G] + ["v"] if mla else [])
    order = []
    for i in range(nq + 2):
        order += [("S", i)] * (i < nq) + [("T", i - 1)] * (1 <= i <= nq) + [("O", i - 2)] * (i >= 2)
    pe_s = Steps(k, name + "_products", [(s, x) for s in S2 for x in head_steps + (["swap"] if mla else []) + order],
                 primed=True)
    act_s = Steps(k, name + "_functions",
                  [(s, x) for s in S2 for x in head_steps + [y for y in order for y in
                   ([("exp", y[1])] if y[0] == "S" else [("T", y[1])] if y[0] == "T" else [("O", y[1])])]],
                  primed=True)
    dve_s = Steps(k, name + "_softmax",
                  [(s, x) for s in S2 for x in ["q"] + [(m, i) for i in range(nq) for m in ("max", "prob")]],
                  primed=True)
    pool_s = Steps(k, name + "_operands", list(S2)) if not mla else None
    chain = Count(k, name + "_chain")
    links = [0]
    per_chain = 2 * ((1 if mla else 0) + 2 * nq)

    with nc.Block() as block:
        @block.sync
        def _(sp):
            with sp.Fori(0, heads // 2) as it:
                for s in S2:
                    h = it * 2 + s
                    pe_s.wait(sp, (s, "swap" if mla else ("q", NT - 1)), it, before=1)
                    if mla:
                        sp.dma_start(wq[s], k.io["mla_w_qb"][0].rearrange("(f p) n -> p f n", p=P)[:, :, bass.ds(h * QH, QH)])\
                            .then_inc(landed[s].sem, 16)
                        sp.dma_start(wk[s], k.io["mla_w_uk"][0].rearrange("(f p) h n -> p f (h n)", p=P)
                                     [:, :, bass.ds(h * NOPE, NOPE)]).then_inc(landed[s].sem, 16)
                        sp.dma_start(wv[s], k.io["mla_w_uv"][0].rearrange("(f p) h n -> p f (h n)", p=P)
                                     [:, :, bass.ds(h * VH, VH)]).then_inc(landed[s].sem, 16)
                    else:
                        sp.dma_start(wq[s], k.io["w_in"][0].rearrange("(f p) n -> p f n", p=P)
                                     [:, :, bass.ds(COL_MEM + h * P, P)]).then_inc(landed[s].sem, 16)

        if not mla:
            @block.gpsimd
            def _(pool):
                with pool.Fori(0, heads // 2) as it:
                    for s in S2:
                        pe_s.wait(pool, (s, ("O", nq - 1)), it, before=1)
                        nc.gpsimd.tensor_copy(k_buf[s].rearrange("p (a t) -> p a t", a=1),
                                              k.memT[:, bass.ds(it * 2 + s, 1), :])
                        pool_s.done(nc.gpsimd.tensor_copy(v_buf[s], k.memV[:, :, bass.ds((it * 2 + s) * P, P)]), s)

        @block.tensor
        def _(pe):
            def settled():
                pe.sem_inc(k.settled.sem, 1)

            pe_s.prime(pe)
            with pe.Fori(0, heads // 2) as it:
                for s in S2:
                    pe.wait_ge(landed[s].sem, it * (16 * nw) + 16 * nw)
                    if s == 0:
                        act_s.wait(pe, (1, ("O", nq - 1)), it, before=1)
                    else:
                        act_s.wait(pe, (0, ("O", nq - 1)), it)
                    for g in G:
                        for f in range(kq):
                            ins = nc.tensor.matmul(k.ps[g][0:depth, 0:TG], wq[s][:, f], xq[:, f, grp(g)],
                                                   start=(f == 0), stop=(f == kq - 1))
                        pe_s.done(ins, (s, ("q", g)))
                    if mla:
                        for g in G:
                            for f in range(KT):
                                ins = nc.tensor.matmul(k.ps[3 + g][0:NOPE, 0:TG], wk[s][:, f], k.C[:, 6 + f, grp(g)],
                                                       start=(f == 0), stop=(f == KT - 1))
                            pe_s.done(ins, (s, ("k", g)))
                        for t in range(NQ):
                            for f in range(KT):
                                ins = nc.tensor.matmul(k.ps[7][:, t * VH:(t + 1) * VH],
                                                       k.C[:, 6 + f, t * P:(t + 1) * P], wv[s][:, f],
                                                       start=(f == 0), stop=(f == KT - 1))
                        pe_s.done(ins, (s, "v"))
                        act_s.wait(pe, (s, ("q", NT - 1)), it)
                        settled()
                        for g in G:
                            ins = nc.tensor.matmul(k.ps[g][pe_rows, 0:TG], k.perm[pe_rows, :],
                                                   q_buf[s][pe_rows, grp(g)], start=True, stop=True)
                        pe_s.done(ins, (s, "swap"))
                    else:
                        pool_s.wait(pe, s, it)
                    for m, i in order:
                        if m == "S":
                            if i == 0:
                                dve_s.wait(pe, (s, "q"), it)
                                if mla:
                                    act_s.wait(pe, (s, "v"), it)
                            if i >= 2:
                                act_s.wait(pe, (s, ("exp", i - 2)), it)
                            for b in range((keys[i] + 511) // 512):
                                n = min(512, keys[i] - 512 * b)
                                last = mla and b == (keys[i] - 1) // 512
                                out = k.ps[2 * (i % 2) + b]
                                ins = nc.tensor.matmul(out[:, 0:n], q_buf[s][0:depth, i * P:(i + 1) * P],
                                                       k_buf[s][0:depth, 512 * b:512 * b + n],
                                                       start=True, stop=not last)
                                if last:
                                    ins = nc.tensor.matmul(out[:, n - P:n], k.ident[:, :], k.causal[:, :],
                                                           start=False, stop=True)
                        elif m == "T":
                            dve_s.wait(pe, (s, ("prob", i)), it)
                            if i >= 1:
                                act_s.wait(pe, (s, ("T", i - 1)), it)
                            for b in range(blocks[i]):
                                ins = nc.tensor.transpose(k.ps[4 + b // 4][:, (b % 4) * P:(b % 4 + 1) * P],
                                                          prob[i % 2][:, b * P:(b + 1) * P], k.ident[:, :])
                        else:
                            act_s.wait(pe, (s, ("T", i)), it)
                            if i >= 2:
                                act_s.wait(pe, (s, ("O", i - 2)), it)
                            lo = VH * s if mla else 0
                            settled()
                            for b in range(blocks[i]):
                                ins = nc.tensor.matmul(k.ps[6 + i % 2][lo:lo + wide, 0:P], v_buf[s][:, b, :],
                                                       probT[i % 2][:, b * P:(b + 1) * P],
                                                       start=(b == 0), stop=(b == blocks[i] - 1))
                        pe_s.done(ins, (s, (m, i)))

        @block.scalar
        def _(act):
            act_s.prime(act)
            with act.Fori(0, heads // 2) as it:
                for s in S2:
                    for g in G:
                        pe_s.wait(act, (s, ("q", g)), it)
                        act_s.done(nc.scalar.activation(q_buf[s][0:depth, grp(g)], k.ps[g][0:depth, 0:TG], ACT.Copy),
                                   (s, ("q", g)))
                    if mla:
                        for g in G:
                            pe_s.wait(act, (s, ("k", g)), it)
                            act_s.done(nc.scalar.activation(k_buf[s][0:NOPE, grp(g)], k.ps[3 + g][0:NOPE, 0:TG],
                                                            ACT.Copy), (s, ("k", g)))
                        pe_s.wait(act, (s, "v"), it)
                        act_s.done(nc.scalar.activation(v_buf[s], k.ps[7][:, :].rearrange("p (t c) -> p t c", t=NQ),
                                                        ACT.Copy), (s, "v"))
                    for m, i in order:
                        if m == "S":
                            dve_s.wait(act, (s, ("max", i)), it)
                            act_s.done(nc.scalar.activation(prob[i % 2][:, 0:keys[i]], k.psw[i % 2][:, 0:keys[i]],
                                                            ACT.Exp, scale=scale, bias=k.nmax[:, i % 2:i % 2 + 1],
                                                            accum_out=k.rsum[:, i % 2:i % 2 + 1]), (s, ("exp", i)))
                        elif m == "T":
                            pe_s.wait(act, (s, ("T", i)), it)
                            act_s.done(nc.scalar.activation(probT[i % 2][:, 0:keys[i]], k.psw[2][:, 0:keys[i]],
                                                            ACT.Copy), (s, ("T", i)))
                        else:
                            pe_s.wait(act, (s, ("O", i)), it)
                            lo = VH * s if mla else 0
                            at = bass.ds(it, 1) if mla else bass.ds(it * 2 + s, 1)
                            out = (k.A[:, 0:4] if mla else k.C[:, 18:22])[lo:lo + wide, at, i * P:(i + 1) * P]
                            act_s.done(nc.scalar.activation(out, k.ps[6 + i % 2][lo:lo + wide, 0:P]
                                                            .rearrange("p (a t) -> p a t", a=1), ACT.Copy),
                                       (s, ("O", i)))

        @block.vector
        def _(dve):
            dve_s.prime(dve)
            with dve.Fori(0, heads // 2) as it:
                links[0] = 0

                def link(ins):
                    links[0] += 1
                    ins.then_inc(chain.sem, 1)
                    dve.wait_ge(chain.sem, it * per_chain + links[0])

                for s in S2:
                    q_s = (k.q_dec if mla else k.qm_dec)[0:depth, bass.ds(it * 2 + s, 1), :]
                    q_cols = q_buf[s][0:depth, SEQ:T].rearrange("p (a t) -> p a t", a=1)
                    if mla:
                        pe_s.wait(dve, (s, "swap"), it)
                        act_s.wait(dve, (s, ("q", NT - 1)), it)
                        for g in G:
                            nc.vector.tensor_tensor(k.sq[pe_rows, 0, grp(g)], k.ps[g][pe_rows, 0:TG], sin[:, grp(g)],
                                                    ALU.mult)
                        link(nc.vector.tensor_tensor(k.sq[pe_rows, 1, :], q_buf[s][pe_rows, :], cos, ALU.mult))
                        dve_s.done(nc.vector.tensor_tensor(q_buf[s][pe_rows, :], k.sq[pe_rows, 0, :],
                                                           k.sq[pe_rows, 1, :], ALU.add), (s, "q"))
                        dve_s.wait(dve, (s, "q"), it)
                        nc.vector.tensor_copy(q_s, q_cols)
                    else:
                        act_s.wait(dve, (s, ("q", NT - 1)), it)
                        dve_s.done(nc.vector.tensor_copy(q_s, q_cols), (s, "q"))
                    for i in range(nq):
                        nmax, rsum = k.nmax[:, i % 2:i % 2 + 1], k.rsum[:, i % 2:i % 2 + 1]
                        pe_s.wait(dve, (s, ("S", i)), it)
                        link(nc.vector.tensor_reduce(nmax, k.psw[i % 2][:, 0:keys[i]], AX.X, ALU.max))
                        dve_s.done(nc.vector.tensor_scalar(nmax, nmax, -scale, None, ALU.mult), (s, ("max", i)))
                        act_s.wait(dve, (s, ("exp", i)), it)
                        link(nc.vector.reciprocal(rsum, rsum))
                        dve_s.done(nc.vector.tensor_scalar(prob[i % 2][:, 0:keys[i]], prob[i % 2][:, 0:keys[i]],
                                                           rsum, None, ALU.mult), (s, ("prob", i)))
            assert 2 * links[0] == per_chain * 2


@stage
def decode_attention(k):
    nc = k.nc
    S2 = range(2)
    wuk = k.C[:, 9, 0:KT * 512].rearrange("p (f c) -> p f c", f=KT)
    wuv = k.C[:, 10, 0:KT * 512].rearrange("p (f c) -> p f c", f=KT)
    cache = k.Bc
    wukT = k.W[0:NOPE, 0, 0:MH_ * KVL].rearrange("p (h c) -> p h c", h=MH_)
    cT = [k.W[:, 1, 512 * f:512 * (f + 1)] for f in range(KT + 1)]
    nT = k.W[:, 1, 1536:1540]
    misc = k.W[:, 1, 1600:2816]
    qlat = misc[:, 0:KT * 64].rearrange("p (f b h) -> p f b h", f=KT, b=DEC)
    qpe = misc[0:ROPE, 128:192].rearrange("p (h b) -> p h b", b=DEC)
    q_now = misc[:, 192:192 + 24].rearrange("p (f h) -> p f h", f=3)
    sc = misc[:, 256:256 + 136].rearrange("p (g h) -> p g h", h=MH_)
    mx, m8, dg = misc[:, 400:408], misc[0:8, 408:409], misc[0:8, 416:424]
    rs = misc[:, 432:440]
    ctx = misc[:, 448:448 + 128].rearrange("p (f h b) -> p f h b", f=KT, h=MH_)
    ng = NPAGE // 4
    setup = Count(k, "dec_setup_landed")
    set_pe = Steps(k, "dec_setup_products", [("wukT", j) for j in range(4)] + ["qlat"])
    set_act = Steps(k, "dec_setup_copies", [("wukT", j) for j in range(4)] + ["qlat"])
    qpe_moved = Count(k, "dec_qpe_moved")
    landed = [Count(k, f"dec_cache_landed{s}") for s in S2]
    landed_sw = [Count(k, f"dec_cache_landed_sw{s}") for s in S2]
    pe_s = Steps(k, "dec_products", [(s, x) for s in S2 for x in
                 [(m, g) for g in range(ng) for m in ("T", "S")] + ["nT", "nS", "mT", "mB", "sum", "ctx"]], primed=True)
    act_s = Steps(k, "dec_copies", [(s, x) for s in S2 for x in [("T", g) for g in range(ng)] + ["nT", "exp"]],
                  primed=True)
    dve_s = Steps(k, "dec_softmax", [(s, x) for s in S2 for x in
                  ["q"] + [("T", g) for g in range(ng)] + ["mx", "diag", "sub", "rs", "ctx"]], primed=True)
    chain = Count(k, "dec_chain")
    per_chain = 8
    pages_may_land = Count(k, "dec_pages_may_land")
    out_pe = Count(k, "dec_out_multiplied")
    links = [0]
    n_phys = k.io["cache_mla"].shape[1]

    def pages(eng, it, s, part):
        b = it * 2 + s
        pe_s.wait(eng, (s, "ctx"), it, before=1)
        eng.sem_inc(pages_may_land.sem, 1)
        with eng.Fori(0, NPAGE // 4) as pair:
            at = []
            for i in range(2):
                page = pair * 4 + (2 * i + part)
                at.append(eng.value_load(k.pages[0:1, bass.ds(b * NPAGE + page, 1)], min_val=0, max_val=n_phys - 1))
            for i in range(2):
                eng.dma_start(cache[:, s, bass.ds(pair * 4 + (2 * i + part), 1), :],
                              k.io["cache_mla"][0, bass.ds(at[i], 1)].rearrange("a p c -> p a c"))\
                    .then_inc((landed_sw if part else landed)[s].sem, 16)

    with nc.Block() as block:
        @block.sync
        def _(sp):
            sp.dma_start(wuk, k.io["mla_w_uk"][0].rearrange("(f p) h n -> p f (h n)", p=P)).then_inc(setup.sem, 16)
            sp.dma_start(wuv, k.io["mla_w_uv"][0].rearrange("(f p) h n -> p f (h n)", p=P)).then_inc(setup.sem, 16)
            sp.dma_start(qpe, k.q_dec[NOPE:QH, :, :]).then_inc(qpe_moved.sem, 16)
            with sp.Fori(0, DEC // 2) as it:
                for s in S2:
                    pages(sp, it, s, 0)
                    sp.dma_start(cache[0:1, s, NPAGE, :], k.io["rows_sample"][0, bass.ds(it * 2 + s, 1), 0, :])\
                        .then_inc(landed[s].sem, 16)

        @block.gpsimd
        def _(pool):
            with pool.Fori(0, DEC // 2) as it:
                for s in S2:
                    pages(pool, it, s, 1)

        @block.tensor
        def _(pe):
            def settled():
                pe.sem_inc(k.settled.sem, 1)

            pe.wait_ge(setup.sem, 32)
            for j in range(4):
                for i in range(4):
                    h, f = (4 * j + i) // KT, (4 * j + i) % KT
                    ins = nc.tensor.transpose(k.ps[j][0:NOPE, i * P:(i + 1) * P], wuk[:, f, h * NOPE:(h + 1) * NOPE],
                                              k.ident[:, :])
                set_pe.done(ins, ("wukT", j))
            set_act.wait(pe, ("wukT", 3))
            for f in range(KT):
                for h in range(MH_):
                    ins = nc.tensor.matmul(k.ps[4][:, (f * MH_ + h) * DEC:(f * MH_ + h + 1) * DEC],
                                           wukT[:, h, f * P:(f + 1) * P], k.q_dec[0:NOPE, h, :], start=True, stop=True)
            set_pe.done(ins, "qlat")
            pe_s.prime(pe)
            set_act.wait(pe, "qlat")
            with pe.Fori(0, DEC // 2) as it:
                for s in S2:
                    pe.wait_ge(landed[s].sem, (it + 1) * (16 * (NPAGE // 2 + 1)))
                    pe.wait_ge(landed_sw[s].sem, (it + 1) * (8 * NPAGE))
                    dve_s.wait(pe, (s, "q"), it)
                    for g in range(ng):
                        if g:
                            act_s.wait(pe, (s, ("T", g - 1)), it)
                            dve_s.wait(pe, (s, ("T", g - 1)), it)
                        elif s:
                            dve_s.wait(pe, (0, "ctx"), it)
                        else:
                            dve_s.wait(pe, (1, "ctx"), it, before=1)
                        for f in range(KT + 1):
                            n = P if f < KT else ROPE
                            for i in range(4):
                                ins = nc.tensor.transpose(k.ps[f][0:n, i * P:(i + 1) * P],
                                                          cache[:, s, 4 * g + i, f * P:f * P + n], k.ident[:, :])
                        pe_s.done(ins, (s, ("T", g)))
                        act_s.wait(pe, (s, ("T", g)), it)
                        dve_s.wait(pe, (s, ("T", g)), it)
                        for i in range(4):
                            for f in range(KT + 1):
                                n = P if f < KT else ROPE
                                o = (4 * g + i) * MH_
                                ins = nc.tensor.matmul(k.ps[3][:, o:o + MH_], cT[f][0:n, i * P:(i + 1) * P],
                                                       q_now[0:n, f, :], start=(f == 0), stop=(f == KT))
                        pe_s.done(ins, (s, ("S", g)))
                    settled()
                    for f in range(KT + 1):
                        n = P if f < KT else ROPE
                        ins = nc.tensor.transpose(k.ps[4][0:n, f:f + 1], cache[0:1, s, NPAGE, f * P:f * P + n],
                                                  k.ident[0:1, 0:1])
                    pe_s.done(ins, (s, "nT"))
                    act_s.wait(pe, (s, "nT"), it)
                    settled()
                    for f in range(KT + 1):
                        n = P if f < KT else ROPE
                        ins = nc.tensor.matmul(k.ps[3][0:1, 128:136], nT[0:n, f:f + 1], q_now[0:n, f, :],
                                               start=(f == 0), stop=(f == KT))
                    pe_s.done(ins, (s, "nS"))
                    dve_s.wait(pe, (s, "mx"), it)
                    settled()
                    pe_s.done(nc.tensor.transpose(k.ps[5][0:MH_, 0:P], mx, k.ident[:, :]), (s, "mT"))
                    dve_s.wait(pe, (s, "diag"), it)
                    settled()
                    pe_s.done(nc.tensor.matmul(k.ps[5][:, 128:136], k.ones[0:8, :], dg, start=True, stop=True), (s, "mB"))
                    act_s.wait(pe, (s, "exp"), it)
                    pe_s.done(nc.tensor.matmul(k.ps[6][:, 0:136], k.ones[:, :], sc.rearrange("p g h -> p (g h)"),
                                               start=True, stop=True), (s, "sum"))
                    for f in range(KT):
                        for g in range(NPAGE):
                            nc.tensor.matmul(k.ps[7][:, f * MH_:(f + 1) * MH_], cache[:, s, g, f * P:(f + 1) * P],
                                             sc[:, g, :], start=(g == 0), stop=False)
                        ins = nc.tensor.matmul(k.ps[7][:, f * MH_:(f + 1) * MH_], cache[0:1, s, NPAGE, f * P:(f + 1) * P],
                                               sc[0:1, NPAGE, :], start=False, stop=True)
                    pe_s.done(ins, (s, "ctx"))
            dve_s.wait(pe, (1, "ctx"), DEC // 2 - 1)
            for h in range(MH_):
                lo = (h % 2) * VH
                for f in range(KT):
                    ins = nc.tensor.matmul(k.ps[0][lo:lo + VH, (h // 2) * DEC:(h // 2 + 1) * DEC],
                                           wuv[:, f, h * VH:(h + 1) * VH], ctx[:, f, h, :],
                                           start=(f == 0), stop=(f == KT - 1))
            ins.then_inc(out_pe.sem, 1)

        @block.scalar
        def _(act):
            for j in range(4):
                set_pe.wait(act, ("wukT", j))
                dst = k.W[0:NOPE, 0, 512 * j:512 * (j + 1)]
                set_act.done(nc.scalar.activation(dst, k.ps[j][0:NOPE, :], ACT.Copy), ("wukT", j))
            set_pe.wait(act, "qlat")
            for f in range(KT):
                ins = nc.scalar.activation(qlat[:, f].rearrange("p b h -> p h b"),
                                           k.ps[4][:, f * 64:(f + 1) * 64].rearrange("p (h b) -> p h b", h=MH_), ACT.Copy)
            set_act.done(ins, "qlat")
            act_s.prime(act)
            with act.Fori(0, DEC // 2) as it:
                for s in S2:
                    for g in range(ng):
                        pe_s.wait(act, (s, ("T", g)), it)
                        if g:
                            pe_s.wait(act, (s, ("S", g - 1)), it)
                        nc.scalar.activation(cT[0], k.ps[0][:, :], ACT.Copy)
                        act_s.done(nc.scalar.activation(cT[2][0:ROPE], k.ps[2][0:ROPE, :], ACT.Copy), (s, ("T", g)))
                    pe_s.wait(act, (s, "nT"), it)
                    nc.scalar.activation(nT[:, 0:2], k.ps[4][:, 0:2], ACT.Copy)
                    act_s.done(nc.scalar.activation(nT[0:ROPE, 2:3], k.ps[4][0:ROPE, 2:3], ACT.Copy), (s, "nT"))
                    dve_s.wait(act, (s, "sub"), it)
                    act_s.done(nc.scalar.activation(sc, sc, ACT.Exp, scale=MLA_SCALE), (s, "exp"))
            act.wait_ge(out_pe.sem, 1)
            nc.scalar.activation(k.A[:, 0:4, SEQ:T], k.ps[0][:, 0:4 * DEC].rearrange("p (j b) -> p j b", b=DEC), ACT.Copy)

        @block.vector
        def _(dve):
            set_act.wait(dve, "qlat")
            dve.wait_ge(qpe_moved.sem, 16)
            dve_s.prime(dve)
            with dve.Fori(0, DEC // 2) as it:
                links[0] = 0

                def link(ins):
                    links[0] += 1
                    ins.then_inc(chain.sem, 1)
                    dve.wait_ge(chain.sem, it * per_chain + links[0])

                for s in S2:
                    pe_s.wait(dve, (1 - s, "ctx"), it, before=1 - s)
                    nc.vector.tensor_copy(q_now[:, 0:KT, :].unsqueeze(2), qlat[:, :, bass.ds(it * 2 + s, 1), :])
                    dve_s.done(nc.vector.tensor_copy(q_now[0:ROPE, KT, :].unsqueeze(2), qpe[:, :, bass.ds(it * 2 + s, 1)]),
                               (s, "q"))
                    for g in range(ng):
                        pe_s.wait(dve, (s, ("T", g)), it)
                        if g:
                            pe_s.wait(dve, (s, ("S", g - 1)), it)
                        dve_s.done(nc.vector.tensor_copy(cT[1], k.ps[1][:, :]), (s, ("T", g)))
                    link(nc.vector.memset(sc[:, NPAGE, :], NEG))
                    pe_s.wait(dve, (s, "nS"), it)
                    nc.vector.tensor_copy(sc[:, 0:NPAGE, :], k.ps[3][:, 0:128].rearrange("p (g h) -> p g h", h=MH_))
                    link(nc.vector.tensor_copy(sc[0:1, NPAGE, :], k.ps[3][0:1, 128:136]))
                    dve_s.done(nc.vector.tensor_reduce(mx, sc.rearrange("p g h -> p h g"), AX.X, ALU.max), (s, "mx"))
                    pe_s.wait(dve, (s, "mT"), it)
                    link(nc.vector.tensor_reduce(m8, k.ps[5][0:MH_, 0:P], AX.X, ALU.max))
                    dve_s.done(nc.vector.tensor_scalar(dg, k.ident[0:8, 0:8], m8, None, ALU.mult), (s, "diag"))
                    pe_s.wait(dve, (s, "mB"), it)
                    dve_s.done(nc.vector.tensor_tensor(sc, sc, k.ps[5][:, 128:136].unsqueeze(1)
                                                       .to_broadcast([P, NPAGE + 1, MH_]), ALU.subtract), (s, "sub"))
                    pe_s.wait(dve, (s, "sum"), it)
                    link(nc.vector.tensor_reduce(rs, k.ps[6][:, 0:136].rearrange("p (g h) -> p h g", h=MH_), AX.X, ALU.add))
                    dve_s.done(nc.vector.reciprocal(rs, rs), (s, "rs"))
                    dve_s.wait(dve, (s, "rs"), it)
                    pe_s.wait(dve, (s, "ctx"), it)
                    dve_s.done(nc.vector.tensor_tensor(ctx[:, :, :, bass.ds(it * 2 + s, 1)],
                                                       k.ps[7][:, 0:2 * MH_].rearrange("p (f h a) -> p f h a", f=KT, a=1),
                                                       rs.unsqueeze(1).unsqueeze(3).to_broadcast([P, KT, MH_, 1]),
                                                       ALU.mult), (s, "ctx"))


@stage
def memory_keys(k, gain):
    nc = k.nc
    mT = k.C[:, 0:2, :].rearrange("p a t -> p (a t)")[:, 0:DT * MEM].rearrange("p (f t) -> p f t", f=DT)
    w = [k.C[:, 2 + 4 * m:6 + 4 * m, :].rearrange("p a t -> p (a t)")[:, 0:4096].rearrange("p (f c) -> p f c", f=DT)
         for m in range(2)]
    raw = [k.C[:, 10 + t, 0:D] for t in range(MTOK)]
    rows = [k.C[:, 12, 0:MTOK * 512].rearrange("p (t c) -> p t c", t=MTOK), k.memV]
    landed = Count(k, "mem_landed")
    wlanded = Count(k, "mem_w_landed")
    pe_s = Steps(k, "mem_turned", range(4))
    act_s = Steps(k, "mem_copied", range(4))
    with nc.Block() as block:
        @block.sync
        def _(sp):
            for t in range(MTOK):
                sp.dma_start(raw[t], k.io["mem_prompt"][0, t * P:(t + 1) * P, :]).then_inc(landed.sem, 16)
            for m, src in enumerate((k.io["mem_w_k"], k.io["mem_w_v"])):
                sp.dma_start(w[m], src[0].rearrange("(f p) n -> p f n", p=P)).then_inc(wlanded.sem, 16)
            sp.wait_ge(wlanded.sem, 32)

        @block.tensor
        def _(pe):
            pe.wait_ge(landed.sem, 32)
            for x in range(4):
                t, q = divmod(x, 2)
                for f in range(4):
                    ins = nc.tensor.transpose(k.ps[x][:, f * P:(f + 1) * P], raw[t][:, (4 * q + f) * P:(4 * q + f + 1) * P],
                                              k.ident[:, :])
                pe_s.done(ins, x)

        @block.scalar
        def _(act):
            for x in range(4):
                t, q = divmod(x, 2)
                pe_s.wait(act, x)
                act_s.done(nc.scalar.activation(mT[:, 4 * q:4 * q + 4, t * P:(t + 1) * P],
                                                k.ps[x][:, :].rearrange("p (f t) -> p f t", f=4), ACT.Copy), x)
    rms_norm(k, "mem_norm", mT, DT, gain, cols=MEM)
    pe_s = Steps(k, "mem_multiplied", [(m, t) for m in range(2) for t in range(MTOK)] + ["kT0", "kT1"])
    act_s = Steps(k, "mem_rows", [(m, t) for m in range(2) for t in range(MTOK)] + ["kT0", "kT1"])
    stored = Count(k, "mem_stored")
    with nc.Block() as block:
        @block.tensor
        def _(pe):
            for m in range(2):
                for t in range(MTOK):
                    for f in range(DT):
                        ins = nc.tensor.matmul(k.ps[2 * m + t][:, :], mT[:, f, t * P:(t + 1) * P], w[m][:, f, :],
                                               start=(f == 0), stop=(f == DT - 1))
                    pe_s.done(ins, (m, t))
            act_s.wait(pe, (0, MTOK - 1))
            for t in range(MTOK):
                for h in range(MH):
                    ins = nc.tensor.transpose(k.ps[4 + t][:, h * P:(h + 1) * P], rows[0][:, t, h * P:(h + 1) * P],
                                              k.ident[:, :])
                pe_s.done(ins, f"kT{t}")

        @block.scalar
        def _(act):
            for m in range(2):
                for t in range(MTOK):
                    pe_s.wait(act, (m, t))
                    act_s.done(nc.scalar.activation(rows[m][:, t, :], k.ps[2 * m + t][:, :], ACT.Copy), (m, t))
            for t in range(MTOK):
                pe_s.wait(act, f"kT{t}")
                act_s.done(nc.scalar.activation(k.memT[:, :, t * P:(t + 1) * P],
                                                k.ps[4 + t][:, :].rearrange("p (h t) -> p h t", h=MH), ACT.Copy), f"kT{t}")

        @block.sync
        def _(sp):
            for m, out in enumerate((k.io["mem_k_prompt"], k.io["mem_v_prompt"])):
                for t in range(MTOK):
                    act_s.wait(sp, (m, t))
                    sp.dma_start(out[0, 0, t * P:(t + 1) * P].rearrange("p h c -> p (h c)"), rows[m][:, t, :])\
                        .then_inc(stored.sem, 16)
            sp.wait_ge(stored.sem, 64)


@stage
def decode_memory(k):
    nc = k.nc
    B8 = range(DEC)
    qrow = k.W[0:DEC, 0, 0:512]
    qall = k.C[:, 5:9, :].rearrange("p a t -> p (a t)")[:, 0:DEC * 512].rearrange("p (b c) -> p b c", b=DEC)
    keys = [k.C[:, s, 0:1024].rearrange("p (t c) -> p t c", t=MTOK) for s in range(2)]
    vals = [k.C[:, 2 + s, 0:1024].rearrange("p (t c) -> p t c", t=MTOK) for s in range(2)]
    prod = k.C[:, 4, 0:1024].rearrange("p (t c) -> p t c", t=MTOK)
    sc = k.W[:, 1, 0:64].rearrange("p (b t h) -> p b t h", b=DEC, t=MTOK)
    mx, m1, dg = k.W[:, 1, 64:96], k.W[0:32, 1, 96:97], k.W[0:32, 1, 100:132]
    rs = k.W[:, 1, 132:164]
    pe_s = Steps(k, "dm_products", ["q", "mT", "mB", "sum"] + [("o", b) for b in B8])
    act_s = Steps(k, "dm_copies", ["q", "exp"])
    dve_s = Steps(k, "dm_softmax", [("s", b) for b in B8] + ["mx", "diag", "sub", "rs", "out"])
    put, got = Count(k, "dm_q_put"), Count(k, "dm_q_got")
    klanded = [Count(k, f"dm_keys_landed{s}") for s in range(2)]
    vlanded = [Count(k, f"dm_values_landed{s}") for s in range(2)]
    chain = Count(k, "dm_chain")

    def rows(src, b):
        return src[0, b].rearrange("(t p) h c -> p t (h c)", p=P)

    with nc.Block() as block:
        @block.sync
        def _(sp):
            for b in range(2):
                sp.dma_start(keys[b], rows(k.io["cache_mem_k"], b)).then_inc(klanded[b].sem, 16)
                sp.dma_start(vals[b], rows(k.io["cache_mem_v"], b)).then_inc(vlanded[b].sem, 16)
            act_s.wait(sp, "q")
            sp.dma_start(k.q_scratch, qrow).then_inc(put.sem, 16)
            sp.wait_ge(put.sem, 16)
            sp.dma_start(qall, k.q_scratch.rearrange("b c -> (b c)").unsqueeze(0).to_broadcast([P, DEC * 512])
                         .rearrange("p (b c) -> p b c", b=DEC)).then_inc(got.sem, 16)
            for b in range(2, DEC):
                dve_s.wait(sp, ("s", b - 2))
                sp.dma_start(keys[b % 2], rows(k.io["cache_mem_k"], b)).then_inc(klanded[b % 2].sem, 16)
            for b in range(2, DEC):
                pe_s.wait(sp, ("o", b - 2))
                sp.dma_start(vals[b % 2], rows(k.io["cache_mem_v"], b)).then_inc(vlanded[b % 2].sem, 16)

        @block.tensor
        def _(pe):
            for h in range(MH):
                ins = nc.tensor.transpose(k.ps[0][0:DEC, h * P:(h + 1) * P], k.qm_dec[:, h, :], k.ident[:, :])
            pe_s.done(ins, "q")
            dve_s.wait(pe, "mx")
            pe_s.done(nc.tensor.transpose(k.ps[1][0:32, 0:P], mx, k.ident[:, :]), "mT")
            dve_s.wait(pe, "diag")
            pe_s.done(nc.tensor.matmul(k.ps[2][:, 0:32], k.ones[0:32, :], dg, start=True, stop=True), "mB")
            act_s.wait(pe, "exp")
            pe_s.done(nc.tensor.matmul(k.ps[3][:, 0:64], k.ones[:, :], sc.rearrange("p b t h -> p (b t h)"),
                                       start=True, stop=True), "sum")
            for b in B8:
                pe.wait_ge(vlanded[b % 2].sem, 16 * (b // 2 + 1))
                for h in range(MH):
                    for t in range(MTOK):
                        ins = nc.tensor.matmul(k.ps[4][:, b * MH + h:b * MH + h + 1], vals[b % 2][:, t, h * P:(h + 1) * P],
                                               sc[:, b, t, h:h + 1], start=(t == 0), stop=(t == MTOK - 1))
                pe_s.done(ins, ("o", b))

        @block.scalar
        def _(act):
            pe_s.wait(act, "q")
            act_s.done(nc.scalar.activation(qrow, k.ps[0][0:DEC, :], ACT.Copy), "q")
            dve_s.wait(act, "sub")
            act_s.done(nc.scalar.activation(sc, sc, ACT.Exp, scale=MEM_SCALE), "exp")

        @block.vector
        def _(dve):
            def link(ins):
                chain.up(ins)
                dve.wait_ge(chain.sem, chain.n)

            dve.wait_ge(got.sem, 16)
            for b in B8:
                dve.wait_ge(klanded[b % 2].sem, 16 * (b // 2 + 1))
                if b:
                    dve_s.wait(dve, ("s", b - 1))
                link(nc.vector.tensor_tensor(prod, keys[b % 2], qall[:, b].unsqueeze(1).to_broadcast([P, MTOK, 512]),
                                             ALU.mult))
                dve_s.done(nc.vector.tensor_reduce(sc[:, b], prod.rearrange("p t (h c) -> p t h c", h=MH), AX.X, ALU.add),
                           ("s", b))
            dve_s.wait(dve, ("s", DEC - 1))
            dve_s.done(nc.vector.tensor_tensor(mx.rearrange("p (b h) -> p b h", b=DEC), sc[:, :, 0], sc[:, :, 1], ALU.max),
                       "mx")
            pe_s.wait(dve, "mT")
            link(nc.vector.tensor_reduce(m1, k.ps[1][0:32, 0:P], AX.X, ALU.max))
            dve_s.done(nc.vector.tensor_scalar(dg, k.ident[0:32, 0:32], m1, None, ALU.mult), "diag")
            pe_s.wait(dve, "mB")
            top = k.ps[2][:, 0:32].rearrange("p (b h) -> p b h", b=DEC)
            dve_s.done(nc.vector.tensor_tensor(sc, sc, top.unsqueeze(2).to_broadcast([P, DEC, MTOK, MH]), ALU.subtract),
                       "sub")
            pe_s.wait(dve, "sum")
            sums = k.ps[3][:, 0:64].rearrange("p (b t h) -> p b h t", b=DEC, t=MTOK)
            link(nc.vector.tensor_reduce(rs.rearrange("p (b h) -> p b h", b=DEC), sums, AX.X, ALU.add))
            dve_s.done(nc.vector.reciprocal(rs, rs), "rs")
            dve_s.wait(dve, "rs")
            pe_s.wait(dve, ("o", DEC - 1))
            dve_s.done(nc.vector.tensor_tensor(k.C[:, 18:22, SEQ:T].rearrange("p h b -> p b h"),
                                               k.ps[4][:, 0:32].rearrange("p (b h) -> p b h", b=DEC),
                                               rs.rearrange("p (b h) -> p b h", b=DEC), ALU.mult), "out")


@stage
def merge(k):
    nc = k.nc
    branches = [(k.A[:, 4:8], k.io["rwkv_w_o"][0]), (k.A[:, 0:4], k.io["mla_w_o"][0]), (k.C[:, 18:22], k.io["mem_w_o"][0])]
    NB = len(branches)
    flat = k.W[:, :, :].rearrange("p s c -> p (s c)")
    w = [flat[:, b * 12 * P:(b + 1) * 12 * P].rearrange("p (f c) -> p f c", f=12) for b in range(NB)]
    landed = [Count(k, f"merge_w_landed{b}") for b in range(NB)]
    multiplied = Count(k, "merge_multiplied")
    gated = Count(k, "merge_gated")
    weighed = Count(k, "merge_weighed")
    added = Count(k, "merge_added")
    per = NB * NT
    gate_w = k.io["w_in"][0].rearrange("(f p) n -> p f n", p=P)

    def load(sp, b, j):
        sp.dma_start(w[b][:, 0:DT], gate_w[:, :, bass.ds(COL_GATE + b * D + j * P, P)]).then_inc(landed[b].sem, 16)
        sp.dma_start(w[b][:, DT:12], branches[b][1].rearrange("(f p) n -> p f n", p=P)[:, :, bass.ds(j * P, P)])\
            .then_inc(landed[b].sem, 16)

    with nc.Block() as block:
        @block.sync
        def _(sp):
            for b in range(NB):
                load(sp, b, 0)
            with sp.Fori(0, DT - 1) as j:
                for b in range(NB):
                    sp.wait_ge(multiplied.sem, j * per + NT * (b + 1))
                    load(sp, b, j + 1)

        @block.tensor
        def _(pe):
            with pe.Fori(0, DT) as j:
                for b in range(NB):
                    pe.wait_ge(landed[b].sem, j * 32 + 32)
                    for g in range(NT):
                        pe.wait_ge(added.sem, j * per + NT * b + g + 1)
                        for f in range(DT):
                            nc.tensor.matmul(k.ps[2 * g][:, 0:TG], w[b][:, f], k.B[:, f, grp(g)],
                                             start=(f == 0), stop=(f == DT - 1))
                        for f in range(4):
                            ins = nc.tensor.matmul(k.ps[2 * g + 1][:, 0:TG], w[b][:, DT + f], branches[b][0][:, f, grp(g)],
                                                   start=(f == 0), stop=(f == 3))
                        ins.then_inc(multiplied.sem, 1)

        @block.scalar
        def _(act):
            with act.Fori(0, DT) as j:
                for b in range(NB):
                    for g in range(NT):
                        act.wait_ge(multiplied.sem, j * per + NT * b + g + 1)
                        act.wait_ge(added.sem, j * per + NT * b + g + 1)
                        nc.scalar.activation(k.t3[:, g, :], k.ps[2 * g][:, 0:TG], ACT.Sigmoid).then_inc(gated.sem, 1)

        @block.vector
        def _(dve):
            dve.sem_inc(added.sem, NT)
            with dve.Fori(0, DT) as j:
                for b in range(NB):
                    for g in range(NT):
                        out = k.C[:, bass.ds(j, 1), grp(g)]
                        t = k.t3[:, g, :].rearrange("p (a t) -> p a t", a=1)
                        x = k.ps[2 * g + 1][:, 0:TG].rearrange("p (a t) -> p a t", a=1)
                        dve.wait_ge(gated.sem, j * per + NT * b + g + 1)
                        if b == 0:
                            nc.vector.tensor_tensor(out, t, x, ALU.mult).then_inc(added.sem, 1)
                            continue
                        nc.vector.tensor_tensor(t, t, x, ALU.mult).then_inc(weighed.sem, 1)
                        dve.wait_ge(weighed.sem, j * (per - NT) + NT * (b - 1) + g + 1)
                        dve.wait_ge(added.sem, j * per + NT * (b - 1) + g + 1 + NT)
                        nc.vector.tensor_tensor(out, out, t, ALU.add).then_inc(added.sem, 1)


def shape_constants():
    c = np.arange(P)
    s, t = c[:, None] % CH, np.arange(CH)[None, :]
    resets = np.broadcast_to((np.arange(SEQ) % CH != 0), (P, SEQ))
    strict, upto = s < t, s <= t
    masks = [(t % 2 == 0) & (s == t + 1), (s % 2 == 0) & (t == s + 1), s == t]
    masks += [(s // (2 * l) == t // (2 * l)) & (s % (2 * l) < l) & (t % (2 * l) >= l) for l in (2, 4, 8, 16, 32)]
    half = ROPE // 2
    freqs = np.float32(10000.0) ** (-np.arange(half, dtype=np.float32) / np.float32(half))
    pos = np.concatenate([np.arange(SEQ), np.full(DEC, PAST)]).astype(np.float32)
    ang = (freqs[:, None] * pos[None, :]).astype(np.float64)
    i = np.arange(ROPE)
    perm = i[:, None] == (i[None, :] + half) % ROPE
    cos = np.concatenate([np.cos(ang), np.cos(ang)])
    sin = np.concatenate([-np.sin(ang), np.sin(ang)])
    causal = np.where(c[None, :] <= c[:, None], 0.0, NEG)
    out = {"c_cos": cos, "c_sin": sin, "c_perm": perm, "c_causal": causal, "c_ident": np.eye(P), "c_headones": (c[:, None] // RN) == (c[None, :] // RN), "c_resets": resets,
           "c_gram": np.concatenate([strict, upto], 1), "c_masks": np.stack(masks, 1)}
    return {name: np.ascontiguousarray(a, dtype=np.float32) for name, a in out.items()}


VECTORS = [("ffn1_pre", DT), ("ffn1_post", DT), ("mix_pre", DT), ("mix_post", DT), ("ffn2_pre", DT),
           ("ffn2_post", DT), ("rwkv_mu", RPT), ("rwkv_w0", RT), ("rwkv_a0", RT), ("rwkv_k_k", RT), ("rwkv_k_a", RT),
           ("rwkv_r_k", RT), ("rwkv_lnx_g", RT), ("rwkv_lnx_b", RT), ("mla_q_norm", 6), ("mla_kv_norm", 2),
           ("mem_norm", DT)]


def build(nc, dram, outs):
    k = Kit()
    k.nc = nc
    k.semaphores = []
    k.io = {**dram, **outs}
    with ExitStack() as ctx:
        k.ctx = ctx

        def sb(name, shape):
            return ctx.enter_context(nc.sbuf_tensor(name, shape, F32))

        base = (nc.sbuf_base + 31) // 32 * 32
        sb("area", [P, (3 * DT + 4) * T + 18 * D + 8])

        def at(name, shape, first, dtype=F32):
            return nc.alloc_sbuf_tensor_at(name, shape, dtype, offset=base + 4 * first)

        k.A, k.B, k.C = at("A", [P, DT, T], 0), at("B", [P, DT, T], DT * T), at("C", [P, FT, T], 2 * DT * T)
        k.W = at("W", [P, 2, FT * P], (2 * DT + FT) * T)
        k.XR = at("XR", [P, 2, DT, T], DT * T, R32)
        k.hidR = at("hidR", [P, 2, 2, T], 3 * DT * T, R32)
        k.wR = at("wR", [P, 3, 2, 2 * D], (3 * DT + 4) * T, R32)
        k.wraw = at("wraw", [P, 3, 2 * D], (3 * DT + 4) * T + 12 * D)
        k.rs, k.sq = sb("rs", [P, T]), sb("sq", [P, 2, T])
        k.t3 = k.sq[:, :, :].rearrange("p a t -> p (a t)")[:, 0:NT * TG].rearrange("p (g t) -> p g t", g=NT)
        k.t6 = k.sq[:, :, :].rearrange("p a t -> p (a t)").rearrange("p (g t) -> p g t", g=2 * NT)
        k.ident, k.ones, k.headones = sb("ident", [P, P]), sb("ones", [P, P]), sb("headones", [P, P])
        k.eps_col, k.lnx_eps, k.mu_now = sb("eps", [P, 1]), sb("lnx_eps", [P, 1]), sb("mu_now", [P, 1])
        k.vec = sb("vec", [P, sum(n for _, n in VECTORS)])
        k.gram = sb("gram", [P, 2 * CH])
        k.masks = sb("masks", [P, 8, CH])
        k.ST, k.st_rows = sb("ST", [P, RT, RN]), sb("st_rows", [P, RT, RN])
        k.chunk_decay, k.decay_now = sb("chunk_decay", [P, NCH, RT]), sb("decay_now", [P, 2, RT])
        k.rwflat = k.A[:, 4:8, :].rearrange("p a t -> p (a t)")
        k.rw = k.rwflat[:, 0:2 * 1792].rearrange("p (s c) -> p s c", s=2)
        k.rowbuf = k.W[:, 1, 1024:1024 + T + 1]
        k.gbuf = k.W[:, 1, 0:T]
        k.gram_mask = k.gram[:, :].unsqueeze(1).to_broadcast([P, RT, 2 * CH])

        def over_pairs(i):
            return k.masks[:, i, :].unsqueeze(1).to_broadcast([P, RT, CH])

        k.first_mask, k.first_mask_t, k.ident4 = over_pairs(0), over_pairs(1), over_pairs(2)
        k.level_mask = {l: over_pairs(3 + i) for i, l in enumerate((2, 4, 8, 16, 32))}
        psum = ctx.enter_context(nc.psum_tensor("banks", [P, 8, 512], F32))
        k.psum_flat = psum[:, :, :].rearrange("p b c -> p (b c)")
        k.rms_col = sb("rms_col", [P, T // P + 1])[:, :]
        k.ps = [psum[:, i, :] for i in range(8)]
        k.psw = [psum[:, 2 * i:2 * i + 2, :].rearrange("p b c -> p (b c)") for i in range(4)]
        k.h_spill = nc.dram_tensor("h_spill", [P, DT, T], F32).ap()
        k.t_scratch = nc.dram_tensor("t_scratch", [6, DEC, RD], F32).ap()
        k.o_scratch = nc.dram_tensor("o_scratch", [DEC, RD], F32).ap()

        k.perm, k.causal = sb("perm", [P, ROPE]), sb("causal", [P, P])
        k.nmax, k.rsum = sb("nmax", [P, 2]), sb("rsum", [P, 2])
        k.q_dec, k.qm_dec = sb("q_dec", [P, MH_, DEC]), sb("qm_dec", [P, MH, DEC])
        k.pages = ctx.enter_context(nc.sbuf_tensor("pages", [1, DEC * NPAGE], mybir.dt.int32))
        k.q_scratch = nc.dram_tensor("q_scratch", [DEC, MH * P], F32).ap()
        k.settled = Count(k, "products_may_start")
        k.memT = k.C[:, 14, 0:MH * MEM].rearrange("p (h t) -> p h t", h=MH)
        k.memV = k.C[:, 13, 0:MTOK * 512].rearrange("p (t c) -> p t c", t=MTOK)
        k.Bc = k.C[:, 12:22, :].rearrange("p a t -> p (a t)")[:, 0:2 * (NPAGE + 1) * CW]\
            .rearrange("p (s g c) -> p s g c", s=2, g=NPAGE + 1)
        k.const_loads = [(k.causal[:, :], k.io["c_causal"]), (k.pages[:, :], k.io["page_table"].rearrange("b g -> (b g)").unsqueeze(0)),
                         (k.ident[:, :], k.io["c_ident"]), (k.headones[:, :], k.io["c_headones"]), (k.gram[:, :], k.io["c_gram"]),
                         (k.masks[:, :, :], k.io["c_masks"])]
        at, v = 0, {}
        for name, n in VECTORS:
            v[name] = k.vec[:, at:at + n]
            src = dram[name][0]
            if name == "rwkv_r_k":
                src = src.rearrange("h n -> (h n)")
            k.const_loads.append((v[name], src.rearrange("(f p) -> p f", p=P)))
            at += n
        k.mu, k.w0, k.a0, k.k_k, k.k_a = (v["rwkv_" + x] for x in ("mu", "w0", "a0", "k_k", "k_a"))
        k.r_k, k.lnx_g, k.lnx_b = (v["rwkv_" + x] for x in ("r_k", "lnx_g", "lnx_b"))
        ms = Count(k, "memset")
        with nc.Block() as block:
            @block.gpsimd
            def _(pool):
                nc.gpsimd.memset(k.ones[:, :], 1.0).then_inc(ms.sem, 1)
                nc.gpsimd.memset(k.eps_col[:, :], RMS_EPS).then_inc(ms.sem, 1)
                nc.gpsimd.memset(k.lnx_eps[:, :], LNX_EPS).then_inc(ms.sem, 1)
        with nc.allow_non_contiguous_dma("per-feature vectors go across partitions"):
            load_constants(k)
        load_x(k)
        ffn(k, "ffn1", v["ffn1_pre"], v["ffn1_post"], k.io["ffn1_gate"][0], k.io["ffn1_up"][0], k.io["ffn1_down"][0])
        rms_norm(k, "mix_pre", k.A, DT, v["mix_pre"], dst=k.B)
        spill(k, "h_spilled", k.h_spill, k.A[:, :, :])
        rwkv_project(k)
        rwkv_vectors(k)
        rwkv_scan(k)
        rwkv_sample_step(k)
        rwkv_finish(k)
        project(k, "latents", k.B, DT, k.io["w_in"][0], COL_Q, QT + KT, k.C)
        rms_norm(k, "q_norm", k.C[:, 0:QT], QT, v["mla_q_norm"])
        rms_norm(k, "kv_norm", k.C[:, QT:QT + KT], KT, v["mla_kv_norm"])
        key_rope(k)
        prompt_attention(k, "mla", True)
        decode_attention(k)
        memory_keys(k, v["mem_norm"])
        prompt_attention(k, "mem", False)
        decode_memory(k)
        merge(k)
        project(k, "mix_out", k.C, DT, k.io["w_out"][0], 0, DT, k.B)
        rms_norm(k, "mix_post", k.B, DT, v["mix_post"], residual=k.A, fetch=k.h_spill)
        ffn(k, "ffn2", v["ffn2_pre"], v["ffn2_post"], k.io["ffn2_gate"][0], k.io["ffn2_up"][0], k.io["ffn2_down"][0])
        store_y(k, k.A)



_OUTS = [("y_prompt", (1, SEQ, D)), ("y_sample", (DEC, 1, D)),
         ("rows_prompt", (1, 1, SEQ, CW)), ("rows_sample", (1, DEC, 1, CW)),
         ("wkv_prompt", (1, 1, RH, RN, RN)), ("wkv_sample", (1, DEC, RH, RN, RN)),
         ("shift_prompt", (1, 1, RPROJ)), ("shift_sample", (1, DEC, RPROJ)),
         ("mem_k_prompt", (1, 1, MEM, MH, P)), ("mem_v_prompt", (1, 1, MEM, MH, P))]


def kernel(**inputs):
    import concourse.bacc as bacc
    from concourse.bass_utils import run_bass_kernel_spmd

    nc = bacc.Bacc("TRN2", target_bir_lowering=False, num_devices=1)
    arrays, dram = {}, {}
    for name, a in {**inputs, **shape_constants()}.items():
        a = np.ascontiguousarray(a)
        arrays[f"in_{name}"] = a
        dram[name] = nc.dram_tensor(f"in_{name}", a.shape, mybir.dt.from_np(a.dtype), kind="ExternalInput").ap()
    outs = {name: nc.dram_tensor(f"out_{name}", shape, F32, kind="ExternalOutput").ap() for name, shape in _OUTS}
    build(nc, dram, outs)
    r = run_bass_kernel_spmd(nc, [arrays], core_ids=[0])
    return tuple(r.results[0][f"out_{name}"] for name, _ in _OUTS)
```

```python
import numpy as np
import concourse.bass as bass
from concourse import mybir
from contextlib import ExitStack

F32 = mybir.dt.float32
ALU = mybir.AluOpType
ACT = mybir.ActivationFunctionType
AX = mybir.AxisListType

P = 128
D = 1024
DT = D // P
SEQ = 1024
DEC = 8
T = SEQ + DEC
NT = 3
TG = T // NT
FFN = 2816
FT = FFN // P
RMS_EPS = 1e-6


class Count:

    def __init__(self, k, name):
        self.sem = k.nc.alloc_semaphore(name=name)
        k.semaphores.append(self.sem)
        self.n = 0

    def up(self, instruction, by=1):
        instruction.then_inc(self.sem, by)
        self.n += by
        return self.n


class Kit:
    pass


def stage(program):
    def whole(k, *args, **kwargs):
        before, k.semaphores = k.semaphores, []
        program(k, *args, **kwargs)
        k.nc.clear_and_free_semaphores(k.semaphores)
        k.nc.all_engine_barrier()
        k.semaphores = before
    return whole


def grp(g):
    return slice(g * TG, (g + 1) * TG)



@stage
def load_x(k):
    nc = k.nc
    n_tiles = SEQ // P
    tiles_landed = [Count(k, f"x_tile_landed{s}") for s in range(2)]
    ident_landed, constants_landed = Count(k, "ident_landed"), Count(k, "constants_landed")
    transposed = Count(k, "x_quads_transposed")
    drained = Count(k, "x_quads_drained")
    stage = k.W
    bank = [k.ps[s][:, :].rearrange("p (f t) -> p f t", f=4) for s in range(4)]

    def src(i):
        return k.io["x_prompt"][0, bass.ds(i * P, P), :]

    with nc.Block() as block:
        @block.scalar
        def _(act):
            for dst, x in k.const_loads:
                constants_landed.up(act.dma_start(dst, x), 16)
            act.wait_ge(constants_landed.sem, constants_landed.n)

        @block.sync
        def _(sp):
            sp.dma_start(k.ident[:, :], k.io["c_ident"]).then_inc(ident_landed.sem, 16)
            for s in range(2):
                sp.dma_start(stage[:, s, 0:D], src(s)).then_inc(tiles_landed[s].sem, 16)
            with sp.Fori(0, (n_tiles - 2) // 2) as pair:
                i = pair * 2
                for s in range(2):
                    sp.wait_ge(transposed.sem, 2 * i + 2 * (s + 1))
                    sp.dma_start(stage[:, s, 0:D], src(i + 2 + s)).then_inc(tiles_landed[s].sem, 16)
            sp.wait_ge(transposed.sem, 2 * (n_tiles - 1))
            sp.dma_start(stage[0:DEC, 0, 0:D], k.io["x_sample"].rearrange("b o d -> (b o) d"))\
                .then_inc(tiles_landed[0].sem, 16)

        @block.tensor
        def _(pe):
            pe.wait_ge(ident_landed.sem, 16)
            with pe.Fori(0, n_tiles // 2) as pair:
                i = pair * 2
                for s in range(2):
                    pe.wait_ge(tiles_landed[s].sem, 8 * i + 16)
                    for q in range(2):
                        pe.wait_ge(drained.sem, 2 * i + 2 * s + q + 1)
                        for f in range(4):
                            ins = nc.tensor.transpose(bank[2 * s + q][:, f, :],
                                                      stage[:, s, (4 * q + f) * P:(4 * q + f + 1) * P],
                                                      k.ident[:, :])
                        ins.then_inc(transposed.sem, 1)
            pe.wait_ge(tiles_landed[0].sem, 16 * (n_tiles // 2 + 1))
            for q in range(2):
                pe.wait_ge(drained.sem, 2 * n_tiles + q + 1)
                for f in range(4):
                    ins = nc.tensor.transpose(bank[q][:, f, 0:DEC],
                                              stage[0:DEC, 0, (4 * q + f) * P:(4 * q + f + 1) * P],
                                              k.ident[0:DEC, 0:DEC])
                ins.then_inc(transposed.sem, 1)

        @block.vector
        def _(dve):
            dve.sem_inc(drained.sem, 4)
            with dve.Fori(0, n_tiles // 2) as pair:
                i = pair * 2
                for s in range(2):
                    for q in range(2):
                        dve.wait_ge(transposed.sem, 2 * i + 2 * s + q + 1)
                        nc.vector.tensor_copy(k.A[:, 4 * q:4 * q + 4, bass.ds((i + s) * P, P)],
                                              bank[2 * s + q]).then_inc(drained.sem, 1)
            for q in range(2):
                dve.wait_ge(transposed.sem, 2 * n_tiles + q + 1)
                nc.vector.tensor_copy(k.A[:, 4 * q:4 * q + 4, SEQ:T], bank[q][:, :, 0:DEC])\
                    .then_inc(drained.sem, 1)


@stage
def store_y(k, src):
    nc = k.nc
    n_tiles = SEQ // P
    transposed = Count(k, "y_quads_transposed")
    drained = Count(k, "y_quads_drained")
    stored = [Count(k, f"y_stored{s}") for s in range(2)]
    stage = k.W
    bank = [k.ps[s][:, :].rearrange("p (f t) -> p f t", f=4) for s in range(4)]
    copied = Count(k, "y_lhs_copied")
    lhs = k.C[:, 0:2, 0:D].rearrange("p s (f t) -> p s f t", f=DT)

    with nc.Block() as block:
        @block.scalar
        def _(act):
            with act.Fori(0, n_tiles // 2) as pair:
                i = pair * 2
                for s in range(2):
                    act.wait_ge(transposed.sem, 2 * i + 2 * s + 2)
                    nc.scalar.activation(lhs[:, s], src[:, :, bass.ds((i + s) * P, P)], ACT.Copy).then_inc(copied.sem, 1)

        @block.tensor
        def _(pe):
            pe.sem_inc(transposed.sem, 4)
            with pe.Fori(0, n_tiles // 2) as pair:
                i = pair * 2
                for s in range(2):
                    pe.wait_ge(copied.sem, i + s + 1)
                    for q in range(2):
                        pe.wait_ge(drained.sem, 2 * i + 2 * s + q + 1)
                        for f in range(4):
                            ins = nc.tensor.transpose(bank[2 * s + q][:, f, :], lhs[:, s, 4 * q + f, :],
                                                      k.ident[:, :])
                        ins.then_inc(transposed.sem, 1)
            for q in range(2):
                pe.wait_ge(drained.sem, 2 * n_tiles + q + 1)
                for f in range(4):
                    ins = nc.tensor.transpose(bank[q][0:DEC, f, :], src[:, 4 * q + f, SEQ:T], k.ident[:, :])
                ins.then_inc(transposed.sem, 1)

        @block.vector
        def _(dve):
            dve.sem_inc(drained.sem, 4)
            with dve.Fori(0, n_tiles // 2) as pair:
                i = pair * 2
                for s in range(2):
                    dve.wait_ge(stored[s].sem, 8 * i + 16)
                    for q in range(2):
                        dve.wait_ge(transposed.sem, 2 * i + 2 * s + q + 1 + 4)
                        nc.vector.tensor_copy(stage[:, s, 512 * q:512 * (q + 1)],
                                              bank[2 * s + q].rearrange("p f t -> p (f t)"))\
                            .then_inc(drained.sem, 1)
            dve.wait_ge(stored[0].sem, 16 * (n_tiles // 2 + 1))
            for q in range(2):
                dve.wait_ge(transposed.sem, 2 * n_tiles + q + 1 + 4)
                nc.vector.tensor_copy(stage[0:DEC, 0, 512 * q:512 * (q + 1)],
                                      bank[q][0:DEC].rearrange("p f t -> p (f t)")).then_inc(drained.sem, 1)

        @block.sync
        def _(sp):
            for s in range(2):
                sp.sem_inc(stored[s].sem, 16)
            with sp.Fori(0, n_tiles // 2) as pair:
                i = pair * 2
                for s in range(2):
                    sp.wait_ge(drained.sem, 2 * i + 2 * (s + 1) + 4)
                    sp.dma_start(k.io["y_prompt"][0, bass.ds((i + s) * P, P), :], stage[:, s, 0:D])\
                        .then_inc(stored[s].sem, 16)
            sp.wait_ge(drained.sem, 2 * n_tiles + 2 + 4)
            sp.dma_start(k.io["y_sample"].rearrange("b o d -> (b o) d"), stage[0:DEC, 0, 0:D])\
                .then_inc(stored[0].sem, 16)
            sp.wait_ge(stored[0].sem, 16 * (n_tiles // 2 + 2))
            sp.wait_ge(stored[1].sem, 16 * (n_tiles // 2 + 1))


class InverseRms:

    def __init__(self, k, name, src, n, cols, half=1.0, second=False):
        self.k, self.src, self.n, self.cols, self.half = k, src, n, cols, half
        self.tiles = [(j, min(P, cols - j * P)) for j in range((cols + P - 1) // P)]
        spare = k.W[:, :, :].rearrange("p a c -> p (a c)")
        self.slots = [(spare[:, 2 * T:3 * T], spare[:, 3 * T:4 * T])] if second else [(k.sq[:, 0, 0:cols], k.sq[:, 1, 0:cols]), (spare[:, 0:cols], spare[:, T:T + cols])]
        self.sums = k.ps[6 if second else 7][:, 0:n // 2 * 16].rearrange("p (i j) -> p j i", j=16)
        self.full = cols // P
        self.at = 3 * 512 if second else 0
        self.factor = k.psum_flat[:, self.at:self.at + cols]
        self.col = k.rms_col[:, (T // P + 1) * int(second):]
        self.act_s = Steps(k, name + "_squares", [("sq", f) for f in range(n)] + ["root"])
        self.dve_s = Steps(k, name + "_pairs", [("pair", i) for i in range(n // 2)] + ["sum", "inverse"])
        self.pe_s = Steps(k, name + "_sums", list(range(n // 2)) + ["spread"])
        self.chain = Count(k, name + "_inverse_chain")

    def columns(self, op):
        ins = op(self.col[:, 0:self.full], self.sums[:, 0:self.full, :])
        if self.cols % P:
            m = self.cols % P
            ins = op(self.col[0:m, self.full:self.full + 1], self.sums[0:m, self.full:self.full + 1, :])
        return ins

    def on_act(self, act):
        self.squares(act)
        self.root(act)

    def squares(self, act):
        for f in range(self.n):
            if f % 2 == 0 and f >= 4:
                self.pe_s.wait(act, f // 2 - 2)
            self.act_s.done(self.k.nc.scalar.activation(self.slots[f // 2 % 2][f % 2], self.src[:, f, 0:self.cols],
                                                        ACT.Square), ("sq", f))

    def root(self, act):
        self.dve_s.wait(act, "sum")
        self.act_s.done(self.columns(lambda out, x: self.k.nc.scalar.activation(
            out, out, ACT.Sqrt, scale=1.0 / (self.n * P), bias=self.k.eps_col[0:out.shape[0], 0:1])), "root")

    def on_dve(self, dve):
        self.pairs(dve)
        self.inverse(dve)
        self.pe_s.wait(dve, "spread")

    def pairs(self, dve):
        for i in range(self.n // 2):
            a, b = self.slots[i % 2]
            self.act_s.wait(dve, ("sq", 2 * i + 1))
            self.dve_s.done(self.k.nc.vector.tensor_tensor(a, a, b, ALU.add), ("pair", i))

    def inverse(self, dve):
        self.pe_s.wait(dve, self.n // 2 - 1)
        self.dve_s.done(self.columns(lambda out, x: self.k.nc.vector.tensor_reduce(out, x, AX.X, ALU.add)), "sum")
        self.act_s.wait(dve, "root")
        ins = self.columns(lambda out, x: self.k.nc.vector.reciprocal(out, out))
        if self.half != 1.0:
            self.chain.up(ins)
            dve.wait_ge(self.chain.sem, self.chain.n)
            ins = self.columns(lambda out, x: self.k.nc.vector.tensor_scalar(out, out, self.half, None, ALU.mult))
        self.dve_s.done(ins, "inverse")

    def on_pe(self, pe):
        self.add_up(pe)
        self.spread(pe)

    def add_up(self, pe):
        for i in range(self.n // 2):
            self.dve_s.wait(pe, ("pair", i))
            for j, m in self.tiles:
                ins = self.k.nc.tensor.matmul(self.sums[0:m, j, i:i + 1], self.slots[i % 2][0][:, j * P:j * P + m],
                                              self.k.ones[:, 0:1], start=True, stop=True)
            self.pe_s.done(ins, i)

    def spread(self, pe):
        self.dve_s.wait(pe, "inverse")
        for j, m in self.tiles:
            ins = self.k.nc.tensor.matmul(self.factor[:, j * P:j * P + m],
                                          self.col[0:m, j:j + 1].to_broadcast([m, P]), self.k.ident[0:m, 0:m],
                                          start=True, stop=True)
        self.pe_s.done(ins, "spread")


@stage
def rms_norm(k, name, src, n, gain, dst=None, residual=None, half=1.0, cols=T, to_src=False, fetch=None):
    nc = k.nc
    inverse = InverseRms(k, name, src, n, cols, half)
    scaled = Count(k, name + "_scaled")
    fetched = Count(k, name + "_residual_landed")
    by_pool = [2, 4, 6] if residual is not None else []
    out = src if dst is None else dst
    to = src if to_src else residual

    with nc.Block() as block:
        if fetch is not None:
            @block.sync
            def _(sp):
                sp.dma_start(residual[:, :, :], fetch).then_inc(fetched.sem, 16)

        @block.scalar
        def _(act):
            inverse.on_act(act)

        @block.tensor
        def _(pe):
            inverse.on_pe(pe)

        def add(eng, f):
            return eng.tensor_tensor(to[:, f, :], out[:, f, :], residual[:, f, :], ALU.add)

        @block.gpsimd
        def _(pool):
            for f in by_pool:
                if fetch is not None:
                    pool.wait_ge(fetched.sem, 16)
                pool.wait_ge(scaled.sem, f + 1)
                add(nc.gpsimd, f)

        @block.vector
        def _(dve):
            inverse.on_dve(dve)
            for f in range(n):
                nc.vector.scalar_tensor_tensor(out=out[:, f, 0:cols], in0=src[:, f, 0:cols],
                                               scalar=gain[:, f:f + 1], in1=inverse.factor,
                                               op0=ALU.mult, op1=ALU.mult).then_inc(scaled.sem, 1)
            if residual is not None:
                if fetch is not None:
                    dve.wait_ge(fetched.sem, 16)
                for f in range(n):
                    if f not in by_pool:
                        dve.wait_ge(scaled.sem, f + 1)
                        add(nc.vector, f)


@stage
def latent_norms(k, q_latent, q_gain, kv_latent, kv_gain):
    nc = k.nc
    both = [InverseRms(k, "q_norm", q_latent, QT, T), InverseRms(k, "kv_norm", kv_latent, KT, T, second=True)]
    with nc.Block() as block:
        @block.scalar
        def _(act):
            for x in both:
                x.squares(act)
            for x in both:
                x.root(act)

        @block.tensor
        def _(pe):
            for x in both:
                x.add_up(pe)
            for x in both:
                x.spread(pe)

        @block.vector
        def _(dve):
            for x in both:
                x.pairs(dve)
            for x in both:
                x.inverse(dve)
            for x, gain in zip(both, (q_gain, kv_gain)):
                x.pe_s.wait(dve, "spread")
                for f in range(x.n):
                    nc.vector.scalar_tensor_tensor(out=x.src[:, f, :], in0=x.src[:, f, :], scalar=gain[:, f:f + 1],
                                                   in1=x.factor, op0=ALU.mult, op1=ALU.mult)




class Steps:

    def __init__(self, k, name, steps, primed=False):
        self.sem = k.nc.alloc_semaphore(name=name)
        k.semaphores.append(self.sem)
        self.steps, self.per, self.primed, self.at = list(steps), len(steps), primed, 0

    def prime(self, eng):
        eng.sem_inc(self.sem, self.per)

    def done(self, ins, step):
        assert self.steps[self.at % self.per] == step, (self.steps[self.at % self.per], step)
        self.at += 1
        ins.then_inc(self.sem, 1)

    def wait(self, eng, step, it=0, before=0):
        n = self.steps.index(step) + 1 + self.per * (int(self.primed) - before)
        eng.wait_ge(self.sem, it * self.per + n)


RH, RN = 8, 64
RD = RH * RN
RT = RD // P
RPROJ = 3 * RD + 64 + 64 + 128
RPT = RPROJ // P
CH = 64
NCH = SEQ // CH
LNX_EPS = 64e-5
DECAY = float(np.exp(-0.5))


@stage
def spill(k, name, dst, src):
    landed = Count(k, name)
    with k.nc.Block() as block:
        @block.sync
        def _(sp):
            landed.up(sp.dma_start(dst, src), 16)
            sp.wait_ge(landed.sem, landed.n)


class HeadNorms:

    def __init__(self, k):
        self.k, self.heads = k, 2 * RT
        self.banks = (6, 7, 0)

    def sum(self, j, square, groups=range(NT)):
        for g in groups:
            ins = self.k.nc.tensor.matmul(self.k.ps[self.banks[g]][0:self.heads, 0:TG],
                                          self.k.head_sel[:, j * self.heads:(j + 1) * self.heads], square[:, grp(g)],
                                          start=(j == 0), stop=(j == RT - 1))
        return ins

    def each(self, op):
        for g in range(NT):
            ins = op(self.k.rs[0:self.heads, grp(g)], self.k.ps[self.banks[g]][0:self.heads, 0:TG])
        return ins

    def spread(self, j, bank):
        for lo in range(0, T, 512):
            m = min(512, T - lo)
            ins = self.k.nc.tensor.matmul(self.k.psum_flat[:, 512 * bank + lo:512 * bank + lo + m],
                                          self.k.head_sel_t[:, j * P:(j + 1) * P], self.k.rs[0:self.heads, lo:lo + m],
                                          start=True, stop=True)
        return ins


@stage
def rwkv_vectors(k):
    nc = k.nc
    r, kk_, v = k.C[:, 8:12], k.C[:, 12:16], k.C[:, 16:20]
    s_, a_, kn = k.C[:, 0:4], k.C[:, 4:8], k.A[:, 0:4]
    low, gl = k.C[:, 20], k.C[:, 21]
    w2 = k.W[0:64, 0, 0:RD]
    a2 = k.W[64:128, 0, 0:RD]
    J = range(RT)
    G = range(NT)
    pe_s = Steps(k, "vec_products", [(m, j) for j in J for m in "za"] + ["sums"] + [("spread", j) for j in J])
    norms = HeadNorms(k)
    act_s = Steps(k, "vec_functions", ["tanh", "gate"] + [(m, j) for j in J for m in "sa"] +
                  ["root"] + [(m, j) for j in J for m in ("up", "down", "prev")])
    dve_s = Steps(k, "vec_elementwise", [(m, j) for j in J for m in ("sq",)] + ["inverse"] +
                  [("kn", j) for j in J] + [(m, j) for j in J for m in ("cum", "scaled")])
    pool_s = Steps(k, "vec_scaled", [(m, j) for j in J for m in "ra"])
    chain = Count(k, "vec_chain")
    landed = Count(k, "vec_w_landed")
    resets = k.W[:, 1, 0:SEQ]
    up, down, prev = k.sq[:, 0, 0:SEQ], k.sq[:, 1, 0:SEQ], k.rs[:, 0:SEQ]
    tmp, cum = k.A[:, 4, :], k.A[:, 5, 0:SEQ]
    cumprev = k.A[:, 6, 0:SEQ]

    with nc.Block() as block:
        @block.sync
        def _(sp):
            landed.up(sp.dma_start(w2, k.io["rwkv_w2"][0]), 16)
            landed.up(sp.dma_start(a2, k.io["rwkv_a2"][0]), 16)
            landed.up(sp.dma_start(resets, k.io["c_resets"]), 16)

        @block.gpsimd
        def _(pool):
            for j in J:
                act_s.wait(pool, ("up", j))
                pool_s.done(nc.gpsimd.tensor_tensor(r[:, j, 0:SEQ], r[:, j, 0:SEQ], up, ALU.mult), ("r", j))
                act_s.wait(pool, ("down", j))
                pool_s.done(nc.gpsimd.tensor_tensor(a_[:, j, 0:SEQ], a_[:, j, 0:SEQ], down, ALU.mult), ("a", j))

        @block.tensor
        def _(pe):
            pe.wait_ge(landed.sem, 48)
            act_s.wait(pe, "tanh")
            for j in J:
                if j >= 1:
                    act_s.wait(pe, ("s", j - 1))
                for g in G:
                    ins = nc.tensor.matmul(k.ps[g][:, 0:TG], w2[:, j * P:(j + 1) * P], low[0:64, grp(g)],
                                           start=True, stop=True)
                pe_s.done(ins, ("z", j))
                if j >= 1:
                    act_s.wait(pe, ("a", j - 1))
                for g in G:
                    ins = nc.tensor.matmul(k.ps[3 + g][:, 0:TG], a2[:, j * P:(j + 1) * P], low[64:128, grp(g)],
                                           start=True, stop=True)
                pe_s.done(ins, ("a", j))
            act_s.wait(pe, ("a", RT - 1))
            for j in J:
                dve_s.wait(pe, ("sq", j))
                ins = norms.sum(j, k.A[:, 4 + j, :])
            pe_s.done(ins, "sums")
            dve_s.wait(pe, "inverse")
            for j in J:
                if j >= 2:
                    dve_s.wait(pe, ("kn", j - 2))
                pe_s.done(norms.spread(j, 3 * (j % 2)), ("spread", j))

        @block.scalar
        def _(act):
            act_s.done(nc.scalar.activation(low[0:64], low[0:64], ACT.Tanh), "tanh")
            act_s.done(nc.scalar.activation(gl, gl, ACT.Sigmoid), "gate")
            for j in J:
                pe_s.wait(act, ("z", j))
                for g in G:
                    ins = nc.scalar.activation(s_[:, j, grp(g)], k.ps[g][:, 0:TG], ACT.Sigmoid,
                                               bias=k.w0[:, j:j + 1])
                act_s.done(ins, ("s", j))
                pe_s.wait(act, ("a", j))
                for g in G:
                    ins = nc.scalar.activation(a_[:, j, grp(g)], k.ps[3 + g][:, 0:TG], ACT.Sigmoid,
                                               bias=k.a0[:, j:j + 1])
                act_s.done(ins, ("a", j))
            pe_s.wait(act, "sums")
            act_s.done(norms.each(lambda c, x: nc.scalar.activation(c, x, ACT.Sqrt)), "root")
            for j in J:
                dve_s.wait(act, ("cum", j))
                if j:
                    pool_s.wait(act, ("a", j - 1))
                act_s.done(nc.scalar.activation(up, cum, ACT.Exp, scale=-DECAY), ("up", j))
                act_s.done(nc.scalar.activation(down, cum, ACT.Exp, scale=DECAY), ("down", j))
                act_s.done(nc.scalar.activation(prev, cumprev, ACT.Exp, scale=-DECAY), ("prev", j))

        @block.vector
        def _(dve):
            def link(ins):
                chain.up(ins)
                dve.wait_ge(chain.sem, chain.n)

            dve.wait_ge(landed.sem, 48)
            for j in J:
                link(nc.vector.tensor_scalar(kn[:, j], kk_[:, j], k.k_k[:, j:j + 1], None, ALU.mult))
                dve_s.done(nc.vector.tensor_tensor(k.A[:, 4 + j], kn[:, j], kn[:, j], ALU.mult), ("sq", j))
            act_s.wait(dve, "root")
            link(norms.each(lambda c, x: nc.vector.tensor_scalar(c, c, 1e-12, None, ALU.max)))
            dve_s.done(norms.each(lambda c, x: nc.vector.reciprocal(c, c)), "inverse")
            for j in J:
                pe_s.wait(dve, ("spread", j))
                norm = k.A[:, 4 + j]
                at = 512 * 3 * (j % 2)
                link(nc.vector.tensor_tensor(kn[:, j], kn[:, j], k.psum_flat[:, at:at + T], ALU.mult))
                link(nc.vector.tensor_scalar(norm, a_[:, j], -1.0, k.k_a[:, j:j + 1], ALU.add, ALU.mult))
                link(nc.vector.scalar_tensor_tensor(out=kk_[:, j], in0=norm, scalar=1.0, in1=kk_[:, j],
                                                    op0=ALU.add, op1=ALU.mult))
                dve_s.done(nc.vector.tensor_tensor(a_[:, j], kn[:, j], a_[:, j], ALU.mult), ("kn", j))
            dve_s.wait(dve, ("kn", RT - 1))
            for j in J:
                if j >= 1:
                    act_s.wait(dve, ("prev", j - 1))
                link(nc.vector.tensor_tensor_scan(cum, resets, s_[:, j, 0:SEQ], 0.0,
                                                  ALU.mult, ALU.add))
                dve_s.done(nc.vector.tensor_tensor(cumprev, cum, s_[:, j, 0:SEQ], ALU.subtract), ("cum", j))
                act_s.wait(dve, ("up", j))
                link(nc.vector.tensor_copy(k.chunk_decay[:, :, j],
                                           up.rearrange("p (c t) -> p c t", t=CH)[:, :, CH - 1]))
                act_s.wait(dve, ("down", j))
                link(nc.vector.tensor_tensor(kk_[:, j, 0:SEQ], kk_[:, j, 0:SEQ], down, ALU.mult))
                act_s.wait(dve, ("prev", j))
                dve_s.done(nc.vector.scalar_tensor_tensor(out=kn[:, j, 0:SEQ], in0=kn[:, j, 0:SEQ], scalar=-1.0,
                                                          in1=prev, op0=ALU.mult, op1=ALU.mult), ("scaled", j))


@stage
def rwkv_scan(k):
    nc = k.nc
    nhead = [(h, q) for h in range(RT) for q in range(2)]
    R2 = range(2)
    LV = [2, 4, 8, 16, 32]
    W0, W1 = k.W[:, 0], k.W[:, 1]
    base = [W0, W1]
    def view(s, at, c):
        return base[s][:, at:at + RT * c].rearrange("p (h c) -> p h c", h=RT)
    AR = [view(s, 0, 128) for s in R2]
    Bt = [view(s, 512, 64) for s in R2]
    Kt = [view(s, 768, 64) for s in R2]
    Vt = [view(s, 1024, 64) for s in R2]
    G1 = [view(s, 1280, 128) for s in R2]
    G2 = [view(s, 1792, 128) for s in R2]
    X = k.rw
    def wide(s, i, c=64):
        return X[:, s, i * 256:i * 256 + RT * c].rearrange("p (h c) -> p h c", h=RT)
    Vm = [view(s, 2304, 64) for s in R2]
    Bm = [view(s, 2560, 64) for s in R2]
    Km = [wide(s, 0) for s in R2]
    NT_ = [wide(s, 1) for s in R2]
    Tm = [wide(s, 2) for s in R2]
    TT = [wide(s, 3) for s in R2]
    Ym = [wide(s, 4) for s in R2]
    Wm = [wide(s, 5) for s in R2]
    Um = [wide(s, 6) for s in R2]
    ST = [k.ST, k.st_rows]
    bank = [[k.ps[4 * s + b][:, :] for b in range(4)] for s in R2]

    def half(b, lo, c):
        return b[:, lo:lo + RT * c].rearrange("p (h c) -> p h c", h=RT)

    pe_s = Steps(k, "scan_products",
                 [(m, s) for s in R2 for m in ("gram", "turned")] +
                 [(m, s, l) for l in LV for m in ("Y", "Z") for s in R2][:-1] +
                 [("W", 0), ("Z", 1, LV[-1]), ("U", 0), ("S", 0), ("W", 1), ("U", 1), ("O", 0), ("S", 1), ("O", 1)],
                 primed=True)
    act_s = Steps(k, "scan_copies",
                  [("turned", s) for s in R2] + [("Y", s, l) for l in LV for s in R2] +
                  [(m, s) for s in R2 for m in "WU"] + [("O", s) for s in R2], primed=True)
    dve_s = Steps(k, "scan_masks_and_sums",
                  [("gram", s) for s in R2] + [("first", s) for s in R2] +
                  [("T", s, l) for l in LV for s in R2] + [("state", s) for s in R2], primed=True)
    pool_s = Steps(k, "scan_operands", [("load", s) for s in R2] + [("level", s, l) for l in LV for s in R2])
    load_c = Count(k, "scan_loads")
    zeroed = Count(k, "scan_zeroed")
    chain = Count(k, "scan_state_chain")
    settled_at = Count(k, "scan_products_may_start")

    with nc.Block() as block:
        @block.gpsimd
        def _(pool):
            nc.gpsimd.memset(ST[0][:, :, :], 0.0).then_inc(zeroed.sem, 1)
            with pool.Fori(0, NCH // 2) as it:
                for s in R2:
                    pe_s.wait(pool, ("O", s), it, before=1)
                    dve_s.wait(pool, ("state", s), it, before=1)
                    at = bass.ds((it * 2 + s) * CH, CH)
                    for src, dst in ((k.A[:, 0:4, at], AR[s][:, :, 0:64]), (k.C[:, 8:12, at], AR[s][:, :, 64:128]),
                                     (k.C[:, 4:8, at], Bt[s]), (k.C[:, 12:16, at], Kt[s]),
                                     (k.C[:, 16:20, at], Vt[s])):
                        nc.gpsimd.tensor_copy(dst, src).then_inc(load_c.sem, 1)
                    pool.wait_ge(load_c.sem, it * 10 + 5 * s + 5)
                    pool_s.done(nc.gpsimd.tensor_copy(k.decay_now[:, s:s + 1, :],
                                                      k.chunk_decay[:, bass.ds(it * 2 + s, 1), :]), ("load", s))
                for l in LV:
                    for s in R2:
                        dve_s.wait(pool, ("gram", s), it)
                        if l > 2:
                            pe_s.wait(pool, ("Y", s, l // 2), it)
                        pool_s.done(nc.gpsimd.tensor_tensor(NT_[s], G1[s][:, :, 0:64], k.level_mask[l], ALU.mult),
                                    ("level", s, l))

        @block.tensor
        def _(pe):
            pe_s.prime(pe)
            pe.wait_ge(zeroed.sem, 1)

            def settled():
                pe.sem_inc(settled_at.sem, 1)

            def mm(out, lhsT, rhs, start=True, stop=True, q=0):
                return nc.tensor.matmul(out, lhsT, rhs, start=start, stop=stop)

            def lane(t, h, q, lo=0, c=64):
                return t[64 * q:64 * q + 64, h, lo:lo + c]

            with pe.Fori(0, NCH // 2) as it:
                def carried_in(s):
                    if s == 1:
                        dve_s.wait(pe, ("state", 0), it)
                    else:
                        dve_s.wait(pe, ("state", 1), it, before=1)
                    act_s.wait(pe, ("turned", s), it)
                    settled()
                    for h, q in nhead:
                        out = lane(half(bank[s][0], 0, 64), h, q)
                        mm(out, lane(AR[s], h, q), lane(ST[s], h, q), stop=False)
                        ins = mm(out, lane(G2[s], h, q), lane(Vm[s], h, q), start=False)
                    pe_s.done(ins, ("W", s))

                def solved(s):
                    act_s.wait(pe, ("W", s), it)
                    dve_s.wait(pe, ("T", s, LV[-1]), it)
                    settled()
                    for h, q in nhead:
                        ins = mm(lane(half(bank[s][1], 0, 64), h, q), lane(TT[s], h, q), lane(Wm[s], h, q))
                    pe_s.done(ins, ("U", s))

                def state(s):
                    act_s.wait(pe, ("U", s), it)
                    settled()
                    for h, q in nhead:
                        out = lane(half(bank[s][3], 0, 64), h, q)
                        mm(out, lane(Bm[s], h, q), lane(Um[s], h, q), stop=False)
                        ins = mm(out, lane(Km[s], h, q), lane(Vm[s], h, q), start=False)
                    pe_s.done(ins, ("S", s))

                def rest(s):
                    solved(s)
                    state(s)

                def output(s, pairs):
                    for h in pairs:
                        for q in range(2):
                            o = lane(half(bank[s][2], 0, 64), h, q)
                            mm(o, lane(ST[s], h, q), lane(AR[s], h, q, 64), stop=False)
                            mm(o, lane(Um[s], h, q), lane(G1[s], h, q, 64), start=False, stop=False)
                            ins = mm(o, lane(Vm[s], h, q), lane(G2[s], h, q, 64), start=False)
                    return ins

                for s in R2:
                    b = bank[s]
                    pool_s.wait(pe, ("load", s), it)
                    act_s.wait(pe, ("O", s), it, before=1)
                    dve_s.wait(pe, ("state", s), it, before=1)
                    settled()
                    for h, q in nhead:
                        mm(lane(half(b[0], 0, 128), h, q, 0, 128), lane(Bt[s], h, q), lane(AR[s], h, q, 0, 128))
                    for h, q in nhead:
                        mm(lane(half(b[1], 0, 128), h, q, 0, 128), lane(Kt[s], h, q), lane(AR[s], h, q, 0, 128))
                    for h, q in nhead:
                        ins = mm(lane(half(b[2], 0, 64), h, q), lane(AR[s], h, q), lane(Bt[s], h, q))
                    pe_s.done(ins, ("gram", s))
                    for src, dst in ((Vt[s], half(b[3], 0, 64)), (Bt[s], half(b[3], 256, 64)), (Kt[s], half(b[2], 256, 64))):
                        if src is Kt[s]:
                            dve_s.wait(pe, ("gram", s), it)
                            settled()
                        for h, q in nhead:
                            ins = mm(lane(dst, h, q), lane(src, h, q), k.ident[64 * q:64 * q + 64, 64 * q:64 * q + 64])
                    pe_s.done(ins, ("turned", s))
                for l in LV:
                    for s in R2:
                        b = bank[s]
                        pool_s.wait(pe, ("level", s, l), it)
                        if l == 2:
                            dve_s.wait(pe, ("first", s), it)
                        else:
                            dve_s.wait(pe, ("T", s, l // 2), it)
                        settled()
                        for h, q in nhead:
                            ins = mm(lane(half(b[0], 0, 64), h, q), lane(NT_[s], h, q), lane(Tm[s], h, q))
                        pe_s.done(ins, ("Y", s, l))
                    for s in R2:
                        b = bank[s]
                        act_s.wait(pe, ("Y", s, l), it)
                        settled()
                        if l < LV[-1]:
                            for h, q in nhead:
                                mm(lane(half(b[1], 0, 64), h, q), lane(TT[s], h, q), lane(Ym[s], h, q))
                        for h, q in nhead:
                            ins = mm(lane(half(b[1], 256, 64), h, q), lane(Ym[s], h, q), lane(TT[s], h, q))
                        pe_s.done(ins, ("Z", s, l))
                        if (s, l) == (0, LV[-1]):
                            carried_in(0)
                rest(0)
                output(0, range(0, 2))
                carried_in(1)
                output(0, range(2, 3))
                solved(1)
                pe_s.done(output(0, range(3, 4)), ("O", 0))
                state(1)
                pe_s.done(output(1, range(4)), ("O", 1))

        @block.scalar
        def _(act):
            act_s.prime(act)
            with act.Fori(0, NCH // 2) as it:
                for s in R2:
                    b = bank[s]
                    pe_s.wait(act, ("turned", s), it)
                    nc.scalar.activation(Vm[s], half(b[3], 0, 64), ACT.Copy)
                    nc.scalar.activation(Bm[s], half(b[3], 256, 64), ACT.Copy)
                    act_s.done(nc.scalar.activation(Km[s], half(b[2], 256, 64), ACT.Copy), ("turned", s))
                for l in LV:
                    for s in R2:
                        pe_s.wait(act, ("Y", s, l), it)
                        act_s.done(nc.scalar.activation(Ym[s], half(bank[s][0], 0, 64), ACT.Copy), ("Y", s, l))
                for s in R2:
                    b = bank[s]
                    pe_s.wait(act, ("W", s), it)
                    act_s.done(nc.scalar.activation(Wm[s], half(b[0], 0, 64), ACT.Copy), ("W", s))
                    pe_s.wait(act, ("U", s), it)
                    act_s.done(nc.scalar.activation(Um[s], half(b[1], 0, 64), ACT.Copy), ("U", s))
                for s in R2:
                    b = bank[s]
                    pe_s.wait(act, ("O", s), it)
                    act_s.done(nc.scalar.activation(k.C[:, 0:4, bass.ds((it * 2 + s) * CH, CH)],
                                                    half(b[2], 0, 64), ACT.Copy), ("O", s))

        @block.vector
        def _(dve):
            dve_s.prime(dve)
            with dve.Fori(0, NCH // 2) as it:
                for s in R2:
                    b = bank[s]
                    pe_s.wait(dve, ("gram", s), it)
                    pool_s.wait(dve, ("load", s), it)
                    nc.vector.tensor_tensor(G1[s], half(b[0], 0, 128), k.gram_mask, ALU.mult)
                    nc.vector.tensor_tensor(G2[s], half(b[1], 0, 128), k.gram_mask, ALU.mult)
                    dve_s.done(nc.vector.tensor_tensor(Tm[s], half(b[2], 0, 64), k.first_mask, ALU.mult),
                               ("gram", s))
                for s in R2:
                    dve_s.wait(dve, ("gram", s), it)
                    nc.vector.tensor_tensor(TT[s], G1[s][:, :, 0:64], k.first_mask_t, ALU.mult).then_inc(chain.sem, 1)
                    dve.wait_ge(chain.sem, it * 6 + 2 * s + 1)
                    nc.vector.tensor_tensor(Tm[s], Tm[s], k.ident4, ALU.add).then_inc(chain.sem, 1)
                    dve.wait_ge(chain.sem, it * 6 + 2 * s + 2)
                    dve_s.done(nc.vector.tensor_tensor(TT[s], TT[s], k.ident4, ALU.add), ("first", s))
                for l in LV:
                    for s in R2:
                        pe_s.wait(dve, ("Z", s, l), it)
                        if l == 2:
                            dve_s.wait(dve, ("first", s), it)
                        else:
                            dve_s.wait(dve, ("T", s, l // 2), it)
                        if l < LV[-1]:
                            nc.vector.tensor_tensor(Tm[s], Tm[s], half(bank[s][1], 0, 64), ALU.add)
                        dve_s.done(nc.vector.tensor_tensor(TT[s], TT[s], half(bank[s][1], 256, 64), ALU.add),
                                   ("T", s, l))
                for s in R2:
                    pe_s.wait(dve, ("S", s), it)
                    nc.vector.tensor_tensor(ST[1 - s][:, :, :], ST[s][:, :, :], half(bank[s][3], 0, 64), ALU.add)\
                        .then_inc(chain.sem, 1)
                    dve.wait_ge(chain.sem, it * 6 + s + 5)
                    dve_s.done(nc.vector.tensor_tensor(ST[1 - s][:, :, :], ST[1 - s][:, :, :],
                                                       k.decay_now[:, s, :].unsqueeze(2).to_broadcast([P, RT, RN]),
                                                       ALU.mult), ("state", s))
                    dve_s.wait(dve, ("state", s), it)


@stage
def rwkv_sample_step(k):
    nc = k.nc
    names = "rwkvab"
    srcs = [k.C[:, 8:12], k.C[:, 0:4], k.C[:, 12:16], k.C[:, 16:20], k.A[:, 0:4], k.C[:, 4:8]]
    W = k.W[:, :, :].rearrange("p s c -> p (s c)")
    S = W[:, 0:2048].rearrange("p (i j) -> p i j", j=RN)
    tmp = W[:, 2048:4096].rearrange("p (i j) -> p i j", j=RN)
    rows = k.rwflat[0:DEC, 0:6 * RD].rearrange("p (m c) -> p m c", m=6)
    vec = W[:, 4096:4096 + 6 * 64].rearrange("p (m c) -> p m c", m=6)
    sa = W[:, 4480:4512]
    o = W[:, 4512:4544]
    vrow = W[:, 4544:4576]
    orow = k.rwflat[0:DEC, 0:RD]
    state_landed = Count(k, "state_landed")
    turned = Count(k, "vectors_turned")
    copied = Count(k, "vectors_copied")
    put = Count(k, "vectors_put")
    got = Count(k, "vectors_got")
    decayed = Count(k, "decay_ready")
    chain = Count(k, "step_chain")
    stepped = Count(k, "step_done")
    stored = Count(k, "step_stored")
    o_put = Count(k, "o_put")
    o_got = Count(k, "o_got")
    o_turned = Count(k, "o_turned")
    st_turned = Count(k, "prompt_state_turned")
    st_copied = Count(k, "prompt_state_copied")
    rows2 = k.t_scratch.rearrange("m b c -> b m c")
    state = k.io["state_rwkv"][0].rearrange("b h (x i) j -> (b h x) i j", x=2)
    state_out = k.io["wkv_sample"][0].rearrange("b h (x i) j -> (b h x) i j", x=2)

    with nc.Block() as block:
        @block.sync
        def _(sp):
            sp.dma_start(S, state).then_inc(state_landed.sem, 16)
            sp.wait_ge(copied.sem, 6)
            sp.dma_start(rows2, rows).then_inc(put.sem, 16)
            sp.wait_ge(put.sem, 16)
            for m in range(6):
                src = k.t_scratch[m].rearrange("b (h c) -> (b h) c", c=RN).unsqueeze(1).to_broadcast([64, 2, RN])
                sp.dma_start(vec[:, m], src).then_inc(got.sem, 16)
            sp.dma_start(vrow, k.t_scratch[3].rearrange("b (x c) -> (b x) c", c=32)).then_inc(got.sem, 16)
            sp.wait_ge(st_copied.sem, 1)
            for q in range(2):
                sp.dma_start(k.io["wkv_prompt"][0, 0].rearrange("(h q) i j -> q i h j", q=2)[q],
                             k.st_rows[64 * q:64 * q + 64]).then_inc(stored.sem, 16)
            sp.wait_ge(stepped.sem, 1)
            sp.dma_start(state_out, S).then_inc(stored.sem, 16)
            sp.wait_ge(stepped.sem, 2)
            sp.dma_start(k.o_scratch.rearrange("b (x c) -> (b x) c", c=32), o).then_inc(o_put.sem, 16)
            sp.wait_ge(o_put.sem, 16)
            sp.dma_start(orow, k.o_scratch).then_inc(o_got.sem, 16)
            sp.wait_ge(stored.sem, 48)

        @block.tensor
        def _(pe):
            for m in range(6):
                if m == 1:
                    pe.wait_ge(decayed.sem, 1)
                for j in range(RT):
                    ins = nc.tensor.transpose(k.ps[m][0:DEC, j * P:(j + 1) * P], srcs[m][:, j, SEQ:T], k.ident[:, :])
                ins.then_inc(turned.sem, 1)
            for h in range(RT):
                for q in range(2):
                    l = slice(64 * q, 64 * q + 64)
                    ins = nc.tensor.matmul(k.ps[6][l, h * RN:(h + 1) * RN], k.ST[l, h, :], k.ident[l, l],
                                           start=True, stop=True)
            ins.then_inc(st_turned.sem, 1)
            pe.wait_ge(o_got.sem, 16)
            for j in range(RT):
                ins = nc.tensor.transpose(k.ps[7][:, j * DEC:(j + 1) * DEC], orow[:, j * P:(j + 1) * P],
                                          k.ident[0:DEC, 0:DEC])
            ins.then_inc(o_turned.sem, 1)

        @block.scalar
        def _(act):
            nc.scalar.activation(srcs[1][:, :, SEQ:T], srcs[1][:, :, SEQ:T], ACT.Exp, scale=-DECAY)\
                .then_inc(decayed.sem, 1)
            for m in range(6):
                act.wait_ge(turned.sem, m + 1)
                nc.scalar.activation(rows[:, m], k.ps[m][0:DEC, :], ACT.Copy).then_inc(copied.sem, 1)
            act.wait_ge(st_turned.sem, 1)
            nc.scalar.activation(k.st_rows[:, :, :], k.ps[6][:, 0:RT * RN].rearrange("p (h c) -> p h c", h=RT),
                                 ACT.Copy).then_inc(st_copied.sem, 1)
            act.wait_ge(o_turned.sem, 1)
            nc.scalar.activation(k.C[:, 0:4, SEQ:T], k.ps[7][:, 0:RT * DEC].rearrange("p (j b) -> p j b", b=DEC),
                                 ACT.Copy)

        @block.vector
        def _(dve):
            def link(ins):
                chain.up(ins)
                dve.wait_ge(chain.sem, chain.n)

            def over_rows(m):
                return vec[:, m].unsqueeze(1).to_broadcast([P, 32, RN])

            def over_cols(x):
                return x.unsqueeze(2).to_broadcast([P, 32, RN])

            dve.wait_ge(state_landed.sem, 16)
            dve.wait_ge(got.sem, 7 * 16)
            link(nc.vector.tensor_tensor(tmp, S, over_rows(4), ALU.mult))
            link(nc.vector.tensor_reduce(sa, tmp, AX.X, ALU.add))
            link(nc.vector.tensor_tensor(S, S, over_rows(1), ALU.mult))
            link(nc.vector.tensor_tensor(tmp, over_cols(sa), over_rows(5), ALU.mult))
            link(nc.vector.tensor_tensor(S, S, tmp, ALU.subtract))
            link(nc.vector.tensor_tensor(tmp, over_cols(vrow), over_rows(2), ALU.mult))
            nc.vector.tensor_tensor(S, S, tmp, ALU.add).then_inc(stepped.sem, 1)
            dve.wait_ge(stepped.sem, 1)
            link(nc.vector.tensor_tensor(tmp, S, over_rows(0), ALU.mult))
            nc.vector.tensor_reduce(o, tmp, AX.X, ALU.add).then_inc(stepped.sem, 1)


@stage
def rwkv_finish(k):
    nc = k.nc
    r, kk_, v, gl = k.C[:, 8:12], k.C[:, 12:16], k.C[:, 16:20], k.C[:, 21]
    o, out = k.C[:, 0:4], k.A[:, 4:8]
    J, G = range(RT), range(NT)
    pe_s = Steps(k, "fin_sums", [x for j in range(RT + 1) for x in
                 ([("mean", j), ("bonus", j)] if j < RT else []) + ([("var", j - 1)] if j else [])] +
                 ["sums"] + [(m, j) for j in J for m in ("spread", "g")])
    act_s = Steps(k, "fin_functions", [("sq", j) for j in J] + ["root"] + [("g", j) for j in J])
    dve_s = Steps(k, "fin_elementwise", [x for j in J for x in [("rk", j), ("centred", j), ("bonus", j)]] + ["inverse"] +
                  [("norm", j) for j in J])
    chain = Count(k, "fin_chain")
    landed = Count(k, "g2_landed")
    g2 = k.W[:, 0, 0:RD]
    bonus, square, gate = k.A[:, 0:4], k.C[:, 4:8], k.C[:, 4:8]
    norms = HeadNorms(k)
    with nc.Block() as block:
        @block.sync
        def _(sp):
            sp.dma_start(g2, k.io["rwkv_g2"][0]).then_inc(landed.sem, 16)

        @block.tensor
        def _(pe):
            pe.wait_ge(landed.sem, 16)
            for j in range(RT + 1):
                if j < RT:
                    if j:
                        dve_s.wait(pe, ("centred", j - 1))
                    for g in G:
                        ins = nc.tensor.matmul(k.ps[g][:, 0:TG], k.headones[:, :], o[:, j, grp(g)], start=True, stop=True)
                    pe_s.done(ins, ("mean", j))
                    dve_s.wait(pe, ("rk", j))
                    if j:
                        dve_s.wait(pe, ("bonus", j - 1))
                    for g in G:
                        ins = nc.tensor.matmul(k.ps[3 + g][:, 0:TG], k.headones[:, :], bonus[:, j, grp(g)],
                                               start=True, stop=True)
                    pe_s.done(ins, ("bonus", j))
                if j:
                    act_s.wait(pe, ("sq", j - 1))
                    pe_s.done(norms.sum(j - 1, square[:, j - 1], (0, 1)), ("var", j - 1))
            for j in J:
                ins = norms.sum(j, square[:, j], (2,))
            pe_s.done(ins, "sums")
            dve_s.wait(pe, "inverse")
            for j in J:
                if j:
                    dve_s.wait(pe, ("norm", j - 1))
                pe_s.done(norms.spread(j, 0), ("spread", j))
                if j:
                    act_s.wait(pe, ("g", j - 1))
                for g in G:
                    ins = nc.tensor.matmul(k.ps[3 + g][:, 0:TG], g2[:, j * P:(j + 1) * P], gl[:, grp(g)], start=True, stop=True)
                pe_s.done(ins, ("g", j))

        @block.scalar
        def _(act):
            for j in J:
                dve_s.wait(act, ("centred", j))
                act_s.done(nc.scalar.activation(square[:, j], o[:, j], ACT.Square), ("sq", j))
            pe_s.wait(act, "sums")
            act_s.done(norms.each(lambda c, x: nc.scalar.activation(c, x, ACT.Sqrt, scale=1.0 / RN,
                                                                    bias=k.lnx_eps[0:2 * RT, 0:1])), "root")
            for j in J:
                pe_s.wait(act, ("g", j))
                for g in G:
                    ins = nc.scalar.activation(gate[:, j, grp(g)], k.ps[3 + g][:, 0:TG], ACT.Copy)
                act_s.done(ins, ("g", j))

        @block.vector
        def _(dve):
            def link(ins):
                chain.up(ins)
                dve.wait_ge(chain.sem, chain.n)
            for j in J:
                dve_s.done(nc.vector.scalar_tensor_tensor(out=bonus[:, j], in0=r[:, j], scalar=k.r_k[:, j:j + 1],
                                                          in1=kk_[:, j], op0=ALU.mult, op1=ALU.mult), ("rk", j))
                pe_s.wait(dve, ("mean", j))
                for g in G:
                    ins = nc.vector.scalar_tensor_tensor(out=o[:, j, grp(g)], in0=k.ps[g][:, 0:TG], scalar=-1.0 / RN,
                                                         in1=o[:, j, grp(g)], op0=ALU.mult, op1=ALU.add)
                dve_s.done(ins, ("centred", j))
                pe_s.wait(dve, ("bonus", j))
                for g in G:
                    ins = nc.vector.tensor_tensor(out[:, j, grp(g)], k.ps[3 + g][:, 0:TG], v[:, j, grp(g)], ALU.mult)
                dve_s.done(ins, ("bonus", j))
            act_s.wait(dve, "root")
            dve_s.done(norms.each(lambda c, x: nc.vector.reciprocal(c, c)), "inverse")
            dve_s.wait(dve, "inverse")
            for j in J:
                pe_s.wait(dve, ("spread", j))
                dve_s.done(nc.vector.scalar_tensor_tensor(out=o[:, j], in0=o[:, j], scalar=k.lnx_g[:, j:j + 1],
                                                          in1=k.psum_flat[:, 0:T], op0=ALU.mult, op1=ALU.mult),
                           ("norm", j))
                dve_s.wait(dve, ("norm", j))
                link(nc.vector.scalar_tensor_tensor(out=out[:, j], in0=o[:, j], scalar=k.lnx_b[:, j:j + 1],
                                                    in1=out[:, j], op0=ALU.add, op1=ALU.add))
                act_s.wait(dve, ("g", j))
                nc.vector.tensor_tensor(out[:, j], out[:, j], gate[:, j], ALU.mult)


R32 = mybir.dt.float32r


@stage
def rms_split(k, name, gain, spill_to):
    nc = k.nc
    inverse = InverseRms(k, name, k.A, DT, T)
    high = Count(k, name + "_high")
    scaled = Count(k, name + "_scaled")
    spilled = Count(k, name + "_spilled")
    by_pool = [1, 3, 5]
    with nc.Block() as block:
        @block.sync
        def _(sp):
            sp.dma_start(spill_to, k.A[:, :, :]).then_inc(spilled.sem, 16)

        @block.tensor
        def _(pe):
            inverse.on_pe(pe)

        @block.scalar
        def _(act):
            inverse.on_act(act)
            for f in range(DT):
                act.wait_ge(scaled.sem, f + 1)
                nc.scalar.activation(k.XR[:, 0, f, :], k.A[:, f, :], ACT.Copy).then_inc(high.sem, 1)

        def low_part(eng, on, f):
            eng.wait_ge(high.sem, f + 1)
            on.tensor_tensor(k.XR[:, 1, f, :], k.A[:, f, :], k.XR[:, 0, f, :].bitcast(F32), ALU.subtract)

        @block.gpsimd
        def _(pool):
            for f in by_pool:
                low_part(pool, nc.gpsimd, f)

        @block.vector
        def _(dve):
            inverse.on_dve(dve)
            dve.wait_ge(spilled.sem, 16)
            for f in range(DT + 1):
                if f < DT:
                    nc.vector.scalar_tensor_tensor(out=k.A[:, f, :], in0=k.A[:, f, :], scalar=gain[:, f:f + 1],
                                                   in1=inverse.factor, op0=ALU.mult, op1=ALU.mult)\
                        .then_inc(scaled.sem, 1)
                if f > 0 and f - 1 not in by_pool:
                    low_part(dve, nc.vector, f - 1)


@stage
def ffn_core(k, name, w_gate, w_up, w_down):
    nc = k.nc
    N = FT // 2
    G = range(NT)
    U = ("gu0", "gu1", "down")
    raw = {u: k.wraw[:, i, :] for i, u in enumerate(U)}
    wr = {u: k.wR[:, i] for i, u in enumerate(U)}
    gu_src = [t.rearrange("(f p) n -> p f n", p=P) for t in (w_gate, w_up)]
    dn_src = w_down.rearrange("(f p) n -> p f n", p=P)
    gu_steps = [("gu", t, g) for t in range(2) for g in G]
    dn_steps = [("dn", g, j) for g in G for j in range(DT)]
    landed = {u: Count(k, f"{name}_{u}_landed") for u in U}
    pe_s = Steps(k, name + "_products", gu_steps + dn_steps, primed=True)
    work = [("w", "gu1"), (0, 0), ("w", "down"), (0, 1), (0, 2), (1, 0), ("w", "gu0"), (1, 1), (1, 2)]

    def steps_of(kinds):
        return [s for m in work for s in ([m] if m[0] == "w" else [(x,) + m for x in kinds])]

    act_s = Steps(k, name + "_functions", steps_of(("sig", "hi")), primed=True)
    dve_s = Steps(k, name + "_sums", steps_of(("silu", "h", "lo")) + dn_steps, primed=True)
    first = Count(k, name + "_first_weights_high")
    first_split = Count(k, name + "_first_weights_split")
    cleared = Count(k, name + "_cleared")
    sig = [k.t6[:, i, :] for i in range(3)]
    h = [k.t6[:, 3 + i, :] for i in range(3)]
    last_gu = {"gu0": ("gu", 0, NT - 1), "gu1": ("gu", 1, NT - 1), "down": ("dn", NT - 1, DT - 1)}

    def load(sp, u, i):
        if u == "down":
            sp.dma_start(raw[u].rearrange("p (f c) -> p f c", f=2), dn_src[:, bass.ds(i * 2, 2), :])\
                .then_inc(landed[u].sem, 16)
            return
        t = int(u[2])
        for m in range(2):
            sp.dma_start(raw[u][:, m * D:(m + 1) * D].rearrange("p (f c) -> p f c", f=DT),
                         gu_src[m][:, :, bass.ds((i * 2 + t) * P, P)]).then_inc(landed[u].sem, 16)

    with nc.Block() as block:
        @block.gpsimd
        def _(pool):
            nc.gpsimd.memset(k.A[:, :, :], 0.0).then_inc(cleared.sem, 1)

        @block.sync
        def _(sp):
            for u in U:
                load(sp, u, 0)
            sp.wait_ge(first_split.sem, 1)
            load(sp, "gu0", 1)

            def refill(u, it, i):
                dve_s.wait(sp, ("w", u), it)
                sp.sem_inc(k.settled.sem, 1)
                load(sp, u, i)

            with sp.Fori(0, N - 2) as it:
                refill("gu1", it, it + 1)
                refill("down", it, it + 1)
                refill("gu0", it, it + 2)
            refill("gu1", N - 2, N - 1)
            refill("down", N - 2, N - 1)

        @block.tensor
        def _(pe):
            pe_s.prime(pe)

            def three(out, wgt, cols, x, g, first, last):
                for n, (a, b) in enumerate(((0, 0), (0, 1), (1, 0))):
                    ins = nc.tensor.matmul(out, wgt[:, a, cols], x(b)[:, grp(g)],
                                           start=first and n == 0, stop=last and n == 2)
                return ins

            pe.wait_ge(first_split.sem, 1)
            with pe.Fori(0, N) as it:
                for t in range(2):
                    u = f"gu{t}"
                    dve_s.wait(pe, ("w", u), it, before=1 - t)
                    for g in G:
                        n = NT * t + g
                        if n >= 2:
                            dve_s.wait(pe, ("h",) + gu_steps[n - 2][1:], it)
                        else:
                            dve_s.wait(pe, ("h",) + gu_steps[2 * NT - 2 + n][1:], it, before=1)
                        for m in range(2):
                            for f in range(DT):
                                ins = three(k.ps[2 * (n % 2) + m][:, 0:TG], wr[u],
                                            slice(m * D + f * P, m * D + (f + 1) * P),
                                            lambda b, f=f: k.XR[:, b, f, :], g, f == 0, f == DT - 1)
                        pe_s.done(ins, ("gu", t, g))
                dve_s.wait(pe, ("w", "down"), it)
                for g in G:
                    dve_s.wait(pe, ("lo", 1, g), it)
                    for j in range(DT):
                        n = g * DT + j
                        if n >= 4:
                            dve_s.wait(pe, dn_steps[n - 4], it)
                        else:
                            dve_s.wait(pe, dn_steps[len(dn_steps) - 4 + n], it, before=1)
                        for t in range(2):
                            ins = three(k.ps[4 + n % 4][:, 0:TG], wr["down"], slice(t * D + j * P, t * D + (j + 1) * P),
                                        lambda b, t=t: k.hidR[:, b, t, :], g, t == 0, t == 1)
                        pe_s.done(ins, ("dn", g, j))

        def whole(eng, once):
            with eng.Fori(0, N - 1) as it:
                once(it, False)
            once(N - 1, True)

        @block.scalar
        def _(act):
            act.wait_ge(landed["gu0"].sem, 32)
            nc.scalar.activation(wr["gu0"][:, 0, :], raw["gu0"], ACT.Copy).then_inc(first.sem, 1)
            act_s.prime(act)

            def once(it, last):
                for m in work:
                    if m[0] == "w":
                        u = m[1]
                        if u == "gu0":
                            if not last:
                                act.wait_ge(landed[u].sem, (it + 2) * 32)
                            pe_s.wait(act, last_gu[u], it)
                        else:
                            act.wait_ge(landed[u].sem, (it + 1) * (16 if u == "down" else 32))
                            pe_s.wait(act, last_gu[u], it, before=1)
                        n = 1 if last and u == "gu0" else 2 * D
                        act_s.done(nc.scalar.activation(wr[u][:, 0, 0:n], raw[u][:, 0:n], ACT.Copy), m)
                        continue
                    t, g = m
                    n = NT * t + g
                    pe_s.wait(act, ("gu", t, g), it)
                    dve_s.wait(act, ("h", 1 - t, g), it, before=1 - t)
                    act_s.done(nc.scalar.activation(sig[g], k.ps[2 * (n % 2)][:, 0:TG], ACT.Sigmoid), ("sig", t, g))
                    dve_s.wait(act, ("h", t, g), it)
                    if t == 0 and g == 0:
                        pe_s.wait(act, last_gu["down"], it, before=1)
                    act_s.done(nc.scalar.activation(k.hidR[:, 0, t, grp(g)], h[g], ACT.Copy), ("hi", t, g))

            whole(act, once)

        @block.vector
        def _(dve):
            dve.wait_ge(first.sem, 1)
            nc.vector.tensor_tensor(wr["gu0"][:, 1, :], raw["gu0"], wr["gu0"][:, 0, :].bitcast(F32), ALU.subtract)\
                .then_inc(first_split.sem, 1)
            dve_s.prime(dve)
            dve.wait_ge(cleared.sem, 1)

            def once(it, last):
                for m in work:
                    if m[0] == "w":
                        u = m[1]
                        act_s.wait(dve, m, it)
                        n = 1 if last and u == "gu0" else 2 * D
                        dve_s.done(nc.vector.tensor_tensor(wr[u][:, 1, 0:n], raw[u][:, 0:n], wr[u][:, 0, 0:n].bitcast(F32),
                                                           ALU.subtract), m)
                        continue
                    t, g = m
                    n = NT * t + g
                    act_s.wait(dve, ("sig", t, g), it)
                    dve_s.done(nc.vector.tensor_tensor(sig[g], sig[g], k.ps[2 * (n % 2)][:, 0:TG], ALU.mult),
                               ("silu", t, g))
                    dve_s.wait(dve, ("silu", t, g), it)
                    dve_s.done(nc.vector.tensor_tensor(h[g], sig[g], k.ps[2 * (n % 2) + 1][:, 0:TG], ALU.mult),
                               ("h", t, g))
                    act_s.wait(dve, ("hi", t, g), it)
                    dve_s.done(nc.vector.tensor_tensor(k.hidR[:, 1, t, grp(g)], h[g],
                                                       k.hidR[:, 0, t, grp(g)].bitcast(F32), ALU.subtract),
                               ("lo", t, g))
                for n, (_, g, j) in enumerate(dn_steps):
                    pe_s.wait(dve, ("dn", g, j), it)
                    if n == 0:
                        dve_s.wait(dve, dn_steps[-1], it, before=1)
                    dve_s.done(nc.vector.tensor_tensor(k.A[:, j, grp(g)], k.A[:, j, grp(g)], k.ps[4 + n % 4][:, 0:TG],
                                                       ALU.add), ("dn", g, j))

            whole(dve, once)


def ffn(k, name, pre, post, w_gate, w_up, w_down):
    rms_split(k, name + "_pre", pre, k.h_spill)
    ffn_core(k, name, w_gate, w_up, w_down)
    rms_norm(k, name + "_post", k.A, DT, post, residual=k.B, half=0.5, to_src=True, fetch=k.h_spill)


class SplitWeights:

    def __init__(self, k, name, src, n):
        self.k, self.src, self.n = k, src, n
        self.landed = [Count(k, f"{name}_w_landed{s}") for s in range(2)]
        self.high_made = [Count(k, f"{name}_w_high{s}") for s in range(2)]
        self.low_made = [Count(k, f"{name}_w_low{s}") for s in range(2)]
        self.raw = [k.praw[:, s, :] for s in range(2)]
        self.parts = [k.pR[:, s] for s in range(2)]

    def load(self, sp, s, i):
        sp.dma_start(self.raw[s].rearrange("p (f c) -> p f c", f=DT), self.src(i)).then_inc(self.landed[s].sem, 16)

    def loads(self, sp):
        self.load(sp, 0, 0)
        self.load(sp, 1, 1)
        if self.n > 2:
            with sp.Fori(0, self.n // 2 - 1) as it:
                for s in range(2):
                    sp.wait_ge(self.low_made[s].sem, it + 1)
                    sp.sem_inc(self.k.settled.sem, 1)
                    self.load(sp, s, it * 2 + 2 + s)

    def high(self, act, s, m):
        act.wait_ge(self.landed[s].sem, m * 16 + 16)
        self.k.nc.scalar.activation(self.parts[s][:, 0, :], self.raw[s], ACT.Copy).then_inc(self.high_made[s].sem, 1)

    def low(self, dve, s, m):
        dve.wait_ge(self.high_made[s].sem, m + 1)
        self.k.nc.vector.tensor_tensor(self.parts[s][:, 1, :], self.raw[s], self.parts[s][:, 0, :].bitcast(F32),
                                       ALU.subtract).then_inc(self.low_made[s].sem, 1)

    def ready(self, pe, s, m):
        pe.wait_ge(self.low_made[s].sem, m + 1)

    def passes(self, eng, once):
        if self.n > 2:
            with eng.Fori(0, self.n // 2 - 1) as it:
                once(it, False)
        once(self.n // 2 - 1, True)


def three(k, out, parts, cols, f, g, first, last):
    for n, (a, b) in enumerate(((0, 0), (0, 1), (1, 0))):
        ins = k.nc.tensor.matmul(out, parts[:, a, cols], k.XR[:, b, f, grp(g)],
                                 start=first and n == 0, stop=last and n == 2)
    return ins


@stage
def project_split(k, name, w_dram, col0, n, out, fetch=None):
    nc = k.nc
    src = w_dram.rearrange("(f p) n -> p f n", p=P)
    w = SplitWeights(k, name, lambda i: src[:, :, bass.ds(col0 + i * P, P)], n)
    multiplied = Steps(k, name + "_multiplied", [(s, g) for s in range(2) for g in range(NT)], primed=True)
    stored = Steps(k, name + "_stored", [(s, g) for s in range(2) for g in range(NT)], primed=True)
    fetched = Count(k, name + "_low_part_landed")
    with nc.Block() as block:
        @block.sync
        def _(sp):
            w.loads(sp)

        if fetch is not None:
            @block.gpsimd
            def _(pool):
                pool.dma_start(k.XR[:, 1], fetch).then_inc(fetched.sem, 16)

        @block.tensor
        def _(pe):
            multiplied.prime(pe)
            if fetch is not None:
                pe.wait_ge(fetched.sem, 16)
            with pe.Fori(0, n // 2) as it:
                for s in range(2):
                    w.ready(pe, s, it)
                    for g in range(NT):
                        stored.wait(pe, (s, g), it, before=1)
                        for f in range(DT):
                            ins = three(k, k.ps[NT * s + g][:, 0:TG], w.parts[s], slice(f * P, (f + 1) * P), f, g,
                                        f == 0, f == DT - 1)
                        multiplied.done(ins, (s, g))

        @block.scalar
        def _(act):
            stored.prime(act)
            w.high(act, 0, 0)

            def once(it, last):
                for s in range(2):
                    if s == 0:
                        multiplied.wait(act, (1, NT - 1), it, before=1)
                        w.high(act, 1, it)
                    elif not last:
                        multiplied.wait(act, (0, NT - 1), it)
                        w.high(act, 0, it + 1)
                    for g in range(NT):
                        multiplied.wait(act, (s, g), it)
                        stored.done(nc.scalar.activation(out[:, bass.ds(it * 2 + s, 1), grp(g)],
                                                         k.ps[NT * s + g][:, 0:TG].rearrange("p (a t) -> p a t", a=1),
                                                         ACT.Copy), (s, g))
            w.passes(act, once)

        @block.vector
        def _(dve):
            w.low(dve, 0, 0)

            def once(it, last):
                w.low(dve, 1, it)
                if not last:
                    w.low(dve, 0, it + 1)
            w.passes(dve, once)


@stage
def rwkv_project(k):
    nc = k.nc
    n = RPT
    src = k.io["w_in"][0].rearrange("(f p) n -> p f n", p=P)
    w = SplitWeights(k, "rwkv_p", lambda i: src[:, :, bass.ds(i * P, P)], n)
    shift_landed = Count(k, "rwkv_shift_landed")
    spilled = Count(k, "u_low_spilled")
    shift_ready = Count(k, "rwkv_shift_ready")
    multiplied = Steps(k, "rwkv_p_multiplied", [(s, g) for s in range(2) for g in range(NT)], primed=True)
    copied = Steps(k, "rwkv_p_copied", [(s, g) for s in range(2) for g in range(NT)], primed=True)
    mixed = Steps(k, "rwkv_p_mixed", range(2), primed=True)
    chain = Count(k, "rwkv_mix_chain")
    rows_ready = Count(k, "shift_rows_ready")
    rows_copied = Count(k, "shift_rows_copied")
    rows_stored = Count(k, "shift_rows_stored")
    before_ready = Count(k, "shift_columns_ready")
    rows = k.C[0:DEC + 1, 16:18, :].rearrange("p a t -> p (a t)")[:, 0:RPROJ]
    rows_out = k.A[0:DEC + 1, 0:2, :].rearrange("p a t -> p (a t)")[:, 0:RPROJ]
    before = k.sq[:, 1, 0:RPT * DEC].rearrange("p (j b) -> p j b", b=DEC)
    last_p = k.sq[:, 1, 256:256 + RPT * (DEC + 1)].rearrange("p (j b) -> p j b", b=DEC + 1)
    flat = [k.A[:, 2 + 2 * s:4 + 2 * s, :].rearrange("p a t -> p (a t)")[:, 0:T + 1] for s in range(2)]
    diff = k.rs

    with nc.Block() as block:
        @block.sync
        def _(sp):
            sp.dma_start(rows[0:DEC, :], k.io["state_shift"][0]).then_inc(shift_landed.sem, 16)
            w.loads(sp)
            sp.dma_start(k.u_low, k.XR[:, 1].bitcast(F32)).then_inc(spilled.sem, 16)
            sp.wait_ge(spilled.sem, 16)
            sp.wait_ge(rows_copied.sem, 4)
            sp.dma_start(k.io["shift_prompt"][0], rows_out[0:1, :]).then_inc(rows_stored.sem, 16)
            sp.dma_start(k.io["shift_sample"][0], rows_out[1:DEC + 1, :]).then_inc(rows_stored.sem, 16)
            sp.wait_ge(rows_stored.sem, 32)

        @block.tensor
        def _(pe):
            pe.wait_ge(shift_landed.sem, 16)
            for j in range(n):
                ins = nc.tensor.transpose(k.ps[7][:, j * DEC:(j + 1) * DEC], rows[0:DEC, j * P:(j + 1) * P],
                                          k.ident[0:DEC, 0:DEC])
            ins.then_inc(shift_ready.sem, 1)
            multiplied.prime(pe)
            with pe.Fori(0, n // 2) as it:
                for s in range(2):
                    w.ready(pe, s, it)
                    for g in range(NT):
                        copied.wait(pe, (s, g), it, before=1)
                        for f in range(DT):
                            ins = three(k, k.ps[NT * s + g][:, 0:TG], w.parts[s], slice(f * P, (f + 1) * P), f, g,
                                        f == 0, f == DT - 1)
                        multiplied.done(ins, (s, g))
            mixed.wait(pe, 1, n // 2 - 1)
            copied.wait(pe, (1, NT - 1), n // 2 - 1)
            for q in range(4):
                for j in range(4 * q, min(4 * q + 4, n)):
                    ins = nc.tensor.transpose(k.ps[q][0:DEC + 1, (j % 4) * P:(j % 4 + 1) * P], last_p[:, j, :],
                                              k.ident[:, :])
                ins.then_inc(rows_ready.sem, 1)

        @block.scalar
        def _(act):
            copied.prime(act)
            w.high(act, 0, 0)

            def once(it, last):
                for s in range(2):
                    if s == 0:
                        multiplied.wait(act, (1, NT - 1), it, before=1)
                        w.high(act, 1, it)
                    elif not last:
                        multiplied.wait(act, (0, NT - 1), it)
                        w.high(act, 0, it + 1)
                    mixed.wait(act, s, it, before=1)
                    for g in range(NT):
                        multiplied.wait(act, (s, g), it)
                        copied.done(nc.scalar.activation(flat[s][:, 1 + g * TG:1 + (g + 1) * TG],
                                                         k.ps[NT * s + g][:, 0:TG], ACT.Copy), (s, g))
            w.passes(act, once)
            for q in range(4):
                act.wait_ge(rows_ready.sem, q + 1)
                wide = min(4 * P, RPROJ - 4 * q * P)
                nc.scalar.activation(rows_out[:, 4 * q * P:4 * q * P + wide], k.ps[q][0:DEC + 1, 0:wide], ACT.Copy)\
                    .then_inc(rows_copied.sem, 1)

        @block.vector
        def _(dve):
            w.low(dve, 0, 0)
            for s in range(2):
                nc.vector.memset(flat[s][:, 0:1], 0.0).then_inc(before_ready.sem, 1)
            dve.wait_ge(shift_ready.sem, 1)
            nc.vector.tensor_copy(before, k.ps[7][:, 0:n * DEC].rearrange("p (j b) -> p j b", b=DEC))\
                .then_inc(before_ready.sem, 1)
            dve.wait_ge(before_ready.sem, 3)
            mixed.prime(dve)

            def once(it, last):
                for s in range(2):
                    if s == 0:
                        w.low(dve, 1, it)
                    elif not last:
                        w.low(dve, 0, it + 1)
                    j = it * 2 + s
                    copied.wait(dve, (s, NT - 1), it)
                    mixed.wait(dve, 1 - s, it, before=1 - s)
                    nc.vector.tensor_tensor(diff[:, 0:SEQ], flat[s][:, 0:SEQ], flat[s][:, 1:SEQ + 1], ALU.subtract)\
                        .then_inc(chain.sem, 1)
                    nc.vector.tensor_tensor(diff[:, SEQ:T].rearrange("p (a b) -> p a b", a=1),
                                            before[:, bass.ds(j, 1), :],
                                            flat[s][:, SEQ + 1:T + 1].rearrange("p (a b) -> p a b", a=1), ALU.subtract)\
                        .then_inc(chain.sem, 1)
                    nc.vector.tensor_copy(k.mu_now[:, 0:1], k.mu[:, bass.ds(j, 1)]).then_inc(chain.sem, 1)
                    nc.vector.tensor_copy(last_p[:, bass.ds(j, 1), :],
                                          flat[s][:, SEQ:T + 1].rearrange("p (a b) -> p a b", a=1)).then_inc(chain.sem, 1)
                    dve.wait_ge(chain.sem, it * 8 + 4 * s + 4)
                    mixed.done(nc.vector.scalar_tensor_tensor(
                        out=k.C[:, bass.ds(j + 8, 1), :], in0=diff[:, :].rearrange("p (a t) -> p a t", a=1),
                        scalar=k.mu_now[:, 0:1], in1=flat[s][:, 1:T + 1].rearrange("p (a t) -> p a t", a=1),
                        op0=ALU.mult, op1=ALU.add), s)
            w.passes(dve, once)


@stage
def split_tiles(k, name, src):
    nc = k.nc
    high = Count(k, name + "_high")
    with nc.Block() as block:
        @block.scalar
        def _(act):
            for f in range(DT):
                nc.scalar.activation(k.XR[:, 0, f, :], src[:, f, :], ACT.Copy).then_inc(high.sem, 1)

        @block.vector
        def _(dve):
            for f in range(DT):
                dve.wait_ge(high.sem, f + 1)
                nc.vector.tensor_tensor(k.XR[:, 1, f, :], src[:, f, :], k.XR[:, 0, f, :].bitcast(F32), ALU.subtract)


MH_, RT_ = 8, 4
NOPE, ROPE, VH = 64, 32, 64
QH = NOPE + ROPE
QL, KVL = 768, 256
QT, KT = QL // P, KVL // P
CW = KVL + ROPE
MLA_SCALE = QH ** -0.5
PAST, PAGE = 2048, 128
NPAGE = PAST // PAGE
MEM, MH = 256, 4
MTOK = MEM // P
MEM_SCALE = P ** -0.5
COL_Q = RPROJ
COL_PE = COL_Q + QL + KVL
COL_MEM = COL_PE + ROPE
COL_GATE = COL_MEM + MH * P
NEG = -1e30
NQ = SEQ // P


@stage
def key_rope(k):
    nc = k.nc
    pe_rows = slice(NOPE, QH)
    cos, sin = k.C[pe_rows, 17, :], k.C[pe_rows, 18, :]
    key, tmp = k.C[pe_rows, 16, :], k.C[pe_rows, 19, :]
    w = k.praw[:, 0, 0:DT * QH]
    parts = k.pR[:, 0]
    G = range(NT)
    landed = Count(k, "pe_w_landed")
    pe_s = Steps(k, "pe_products", ["key", "swap"] + [("rows", i) for i in range(NQ + 1)])
    act_s = Steps(k, "pe_copies", ["w", "key"] + [("rows", i) for i in range(NQ + 1)])
    dve_s = Steps(k, "pe_rotated", ["w", "cos", "sin", "key"])
    stored = [Count(k, f"rows_stored{s}") for s in range(2)]
    stage = [k.praw[:, 1, CW * s:CW * (s + 1)] for s in range(2)]
    with nc.Block() as block:
        @block.sync
        def _(sp):
            src = k.io["w_in"][0].rearrange("(f p) n -> p f n", p=P)[:, :, COL_PE - NOPE:COL_PE + ROPE]
            sp.dma_start(w.rearrange("p (f c) -> p f c", f=DT), src).then_inc(landed.sem, 16)
            sp.dma_start(cos, k.io["c_cos"]).then_inc(landed.sem, 16)
            sp.dma_start(sin, k.io["c_sin"]).then_inc(landed.sem, 16)
            sp.dma_start(k.perm[pe_rows, :], k.io["c_perm"]).then_inc(landed.sem, 16)
            for i in range(NQ):
                act_s.wait(sp, ("rows", i))
                sp.dma_start(k.io["rows_prompt"][0, 0, i * P:(i + 1) * P, :], stage[i % 2]).then_inc(stored[i % 2].sem, 16)
            act_s.wait(sp, ("rows", NQ))
            sp.dma_start(k.io["rows_sample"][0].rearrange("b o c -> (b o) c"), stage[NQ % 2][0:DEC])\
                .then_inc(stored[NQ % 2].sem, 16)
            for s in range(2):
                sp.wait_ge(stored[s].sem, 16 * len(range(s, NQ + 1, 2)))

        @block.tensor
        def _(pe):
            pe.wait_ge(landed.sem, 64)
            dve_s.wait(pe, "w")
            for g in G:
                for f in range(DT):
                    ins = three(k, k.ps[g][0:QH, 0:TG], parts, slice(f * QH, (f + 1) * QH), f, g, f == 0, f == DT - 1)
            pe_s.done(ins, "key")
            act_s.wait(pe, "key")
            for g in G:
                ins = nc.tensor.matmul(k.ps[3 + g][pe_rows, 0:TG], k.perm[pe_rows, :], key[:, grp(g)],
                                       start=True, stop=True)
            pe_s.done(ins, "swap")
            dve_s.wait(pe, "key")
            for i in range(NQ + 1):
                n = P if i < NQ else DEC
                cols = slice(i * P, i * P + n)
                b = k.ps[6 + i % 2]
                if i >= 2:
                    act_s.wait(pe, ("rows", i - 2))
                for f in range(KT):
                    nc.tensor.transpose(b[0:n, f * P:(f + 1) * P], k.C[:, 14 + f, cols], k.ident[:, :])
                pe_s.done(nc.tensor.transpose(b[0:n, KVL:CW], k.C[pe_rows, 16, cols], k.ident[pe_rows, pe_rows]),
                          ("rows", i))

        @block.scalar
        def _(act):
            act.wait_ge(landed.sem, 64)
            act_s.done(nc.scalar.activation(parts[:, 0, 0:DT * QH], w, ACT.Copy), "w")
            pe_s.wait(act, "key")
            for g in G:
                ins = nc.scalar.activation(key[:, grp(g)], k.ps[g][pe_rows, 0:TG], ACT.Copy)
            act_s.done(ins, "key")
            for i in range(NQ + 1):
                n = P if i < NQ else DEC
                pe_s.wait(act, ("rows", i))
                if i >= 2:
                    act.wait_ge(stored[i % 2].sem, 16 * (i // 2))
                act_s.done(nc.scalar.activation(stage[i % 2][0:n], k.ps[6 + i % 2][0:n, 0:CW], ACT.Copy), ("rows", i))

        @block.vector
        def _(dve):
            dve.wait_ge(landed.sem, 64)
            act_s.wait(dve, "w")
            dve_s.done(nc.vector.tensor_tensor(parts[:, 1, 0:DT * QH], w, parts[:, 0, 0:DT * QH].bitcast(F32),
                                               ALU.subtract), "w")
            pe_s.wait(dve, "swap")
            for g in G:
                ins = nc.vector.tensor_tensor(tmp[:, grp(g)], k.ps[3 + g][pe_rows, 0:TG], sin[:, grp(g)], ALU.mult)
            dve_s.done(ins, "cos")
            act_s.wait(dve, "key")
            dve_s.done(nc.vector.tensor_tensor(key, key, cos, ALU.mult), "sin")
            dve_s.wait(dve, "sin")
            dve_s.done(nc.vector.tensor_tensor(key, key, tmp, ALU.add), "key")
            dve_s.wait(dve, "key")
            for tile in (21, 0):
                nc.vector.tensor_copy(k.C[pe_rows, tile, :], key)


@stage
def prompt_attention(k, name, mla):
    nc = k.nc
    heads = MH_ if mla else MH
    depth = QH if mla else P
    nq = NQ
    S2, G = range(2), range(NT)
    kq = QT if mla else DT
    xq = k.C[:, 8:8 + QT]
    scale = MLA_SCALE if mla else MEM_SCALE
    wide = VH if mla else P
    q_buf = [k.C[:, (19 if mla else 13) + s, :] for s in S2]
    k_buf = [k.C[:, (21, 0)[s], :] if mla else k.C[:, 15, s * MEM:(s + 1) * MEM] for s in S2]
    v_buf = [(k.C[:, 1, s * 512:(s + 1) * 512].rearrange("p (t c) -> p t c", t=NQ) if mla else
              k.C[:, 16, s * 256:(s + 1) * 256].rearrange("p (t c) -> p t c", t=MTOK)) for s in S2]
    prob = [k.C[:, (2 if mla else 17) + s, 0:SEQ] for s in S2]
    probT = [k.C[:, (4 if mla else 19) + s, 0:SEQ] for s in S2]
    wq = [k.W[:, s, 0:kq * depth].rearrange("p (f c) -> p f c", f=kq) if mla else k.praw[:, s, :] for s in S2]
    wq_parts = [k.pR[:, s] for s in S2]
    wk = [k.W[:, s, 1024:1024 + KT * NOPE].rearrange("p (f c) -> p f c", f=KT) for s in S2]
    wv = [k.W[:, s, 1280:1280 + KT * VH].rearrange("p (f c) -> p f c", f=KT) for s in S2]
    nw = 3 if mla else 1
    keys = [(i + 1) * P if mla else MEM for i in range(nq)]
    blocks = [n // P for n in keys]
    pe_rows = slice(NOPE, QH)
    cos, sin = k.C[pe_rows, 17, :], k.C[pe_rows, 18, :]

    landed = [Count(k, f"{name}_w_landed{s}") for s in S2]
    head_steps = [("q", g) for g in G] + ([("k", g) for g in G] + ["v"] if mla else [])
    order = []
    for i in range(nq + 2):
        order += [("S", i)] * (i < nq) + [("T", i - 1)] * (1 <= i <= nq) + [("O", i - 2)] * (i >= 2)
    pe_s = Steps(k, name + "_products",
                 [(s, x) for s in S2 for x in (head_steps[:-1] + ["swap", "v"] if mla else head_steps) + order],
                 primed=True)
    act_s = Steps(k, name + "_functions",
                  [(s, x) for s in S2 for x in head_steps + [y for y in order for y in
                   ([("exp", y[1])] if y[0] == "S" else [("T", y[1])] if y[0] == "T" else [("O", y[1])])]],
                  primed=True)
    dve_s = Steps(k, name + "_softmax",
                  [(s, x) for s in S2 for x in ["q"] + [(m, i) for i in range(nq) for m in ("max", "prob")]],
                  primed=True)
    pool_s = Steps(k, name + "_operands", [(x, s) for s in S2 for x in ("high", "low", "kv")]) if not mla else None
    chain = Count(k, name + "_chain")
    links = [0]
    per_chain = 2 * ((1 if mla else 0) + 2 * nq)

    with nc.Block() as block:
        @block.sync
        def _(sp):
            with sp.Fori(0, heads // 2) as it:
                for s in S2:
                    h = it * 2 + s
                    pe_s.wait(sp, (s, "v" if mla else ("q", NT - 1)), it, before=1)
                    if mla:
                        sp.dma_start(wq[s], k.io["mla_w_qb"][0].rearrange("(f p) n -> p f n", p=P)[:, :, bass.ds(h * QH, QH)])\
                            .then_inc(landed[s].sem, 16)
                        sp.dma_start(wk[s], k.io["mla_w_uk"][0].rearrange("(f p) h n -> p f (h n)", p=P)
                                     [:, :, bass.ds(h * NOPE, NOPE)]).then_inc(landed[s].sem, 16)
                        sp.dma_start(wv[s], k.io["mla_w_uv"][0].rearrange("(f p) h n -> p f (h n)", p=P)
                                     [:, :, bass.ds(h * VH, VH)]).then_inc(landed[s].sem, 16)
                    else:
                        sp.dma_start(wq[s].rearrange("p (f c) -> p f c", f=DT),
                                     k.io["w_in"][0].rearrange("(f p) n -> p f n", p=P)
                                     [:, :, bass.ds(COL_MEM + h * P, P)]).then_inc(landed[s].sem, 16)

        if not mla:
            @block.gpsimd
            def _(pool):
                with pool.Fori(0, heads // 2) as it:
                    for s in S2:
                        pe_s.wait(pool, (s, ("q", NT - 1)), it, before=1)
                        pool.wait_ge(landed[s].sem, it * 16 + 16)
                        pool.sem_inc(k.settled.sem, 1)
                        pool_s.done(nc.gpsimd.tensor_copy(wq_parts[s][:, 0, :], wq[s]), ("high", s))
                        pool_s.wait(pool, ("high", s), it)
                        pool_s.done(nc.gpsimd.tensor_tensor(wq_parts[s][:, 1, :], wq[s],
                                                            wq_parts[s][:, 0, :].bitcast(F32), ALU.subtract),
                                    ("low", s))
                        pe_s.wait(pool, (s, ("O", nq - 1)), it, before=1)
                        pool.sem_inc(k.settled.sem, 1)
                        nc.gpsimd.tensor_copy(k_buf[s].rearrange("p (a t) -> p a t", a=1),
                                              k.memT[:, bass.ds(it * 2 + s, 1), :])
                        pool_s.done(nc.gpsimd.tensor_copy(v_buf[s], k.memV[:, :, bass.ds((it * 2 + s) * P, P)]),
                                    ("kv", s))

        @block.tensor
        def _(pe):
            def settled():
                pe.sem_inc(k.settled.sem, 1)

            pe_s.prime(pe)
            with pe.Fori(0, heads // 2) as it:
                for s in S2:
                    if mla:
                        pe.wait_ge(landed[s].sem, it * (16 * nw) + 16 * nw)
                    else:
                        pool_s.wait(pe, ("low", s), it)
                    if s == 0:
                        act_s.wait(pe, (1, ("O", nq - 1)), it, before=1)
                    else:
                        act_s.wait(pe, (0, ("O", nq - 1)), it)
                    for g in G:
                        for f in range(kq):
                            if mla:
                                ins = nc.tensor.matmul(k.ps[g][0:depth, 0:TG], wq[s][:, f], xq[:, f, grp(g)],
                                                       start=(f == 0), stop=(f == kq - 1))
                            else:
                                ins = three(k, k.ps[g][:, 0:TG], wq_parts[s], slice(f * P, (f + 1) * P), f, g,
                                            f == 0, f == kq - 1)
                        pe_s.done(ins, (s, ("q", g)))
                    if mla:
                        for g in G:
                            for f in range(KT):
                                ins = nc.tensor.matmul(k.ps[3 + g][0:NOPE, 0:TG], wk[s][:, f], k.C[:, 14 + f, grp(g)],
                                                       start=(f == 0), stop=(f == KT - 1))
                            pe_s.done(ins, (s, ("k", g)))
                        act_s.wait(pe, (s, ("q", NT - 1)), it)
                        settled()
                        for g in G:
                            ins = nc.tensor.matmul(k.ps[g][pe_rows, 0:TG], k.perm[pe_rows, :],
                                                   q_buf[s][pe_rows, grp(g)], start=True, stop=True)
                        pe_s.done(ins, (s, "swap"))
                        for t in range(NQ):
                            for f in range(KT):
                                ins = nc.tensor.matmul(k.ps[7][:, t * VH:(t + 1) * VH],
                                                       k.C[:, 14 + f, t * P:(t + 1) * P], wv[s][:, f],
                                                       start=(f == 0), stop=(f == KT - 1))
                        pe_s.done(ins, (s, "v"))
                    else:
                        pool_s.wait(pe, ("kv", s), it)
                    for m, i in order:
                        if m == "S":
                            if i == 0:
                                dve_s.wait(pe, (s, "q"), it)
                                if mla:
                                    act_s.wait(pe, (s, "v"), it)
                            if i >= 2:
                                act_s.wait(pe, (s, ("exp", i - 2)), it)
                            for b in range((keys[i] + 511) // 512):
                                n = min(512, keys[i] - 512 * b)
                                last = mla and b == (keys[i] - 1) // 512
                                out = k.ps[2 * (i % 2) + b]
                                ins = nc.tensor.matmul(out[:, 0:n], q_buf[s][0:depth, i * P:(i + 1) * P],
                                                       k_buf[s][0:depth, 512 * b:512 * b + n],
                                                       start=True, stop=not last)
                                if last:
                                    ins = nc.tensor.matmul(out[:, n - P:n], k.ident[:, :], k.causal[:, :],
                                                           start=False, stop=True)
                        elif m == "T":
                            dve_s.wait(pe, (s, ("prob", i)), it)
                            if i >= 1:
                                act_s.wait(pe, (s, ("T", i - 1)), it)
                            for b in range(blocks[i]):
                                ins = nc.tensor.transpose(k.ps[4 + b // 4][:, (b % 4) * P:(b % 4 + 1) * P],
                                                          prob[i % 2][:, b * P:(b + 1) * P], k.ident[:, :])
                        else:
                            act_s.wait(pe, (s, ("T", i)), it)
                            if i >= 2:
                                act_s.wait(pe, (s, ("O", i - 2)), it)
                            lo = VH * s if mla else 0
                            settled()
                            for b in range(blocks[i]):
                                ins = nc.tensor.matmul(k.ps[6 + i % 2][lo:lo + wide, 0:P], v_buf[s][:, b, :],
                                                       probT[i % 2][:, b * P:(b + 1) * P],
                                                       start=(b == 0), stop=(b == blocks[i] - 1))
                        pe_s.done(ins, (s, (m, i)))

        @block.scalar
        def _(act):
            act_s.prime(act)
            with act.Fori(0, heads // 2) as it:
                for s in S2:
                    for g in G:
                        pe_s.wait(act, (s, ("q", g)), it)
                        act_s.done(nc.scalar.activation(q_buf[s][0:depth, grp(g)], k.ps[g][0:depth, 0:TG], ACT.Copy),
                                   (s, ("q", g)))
                    if mla:
                        for g in G:
                            pe_s.wait(act, (s, ("k", g)), it)
                            act_s.done(nc.scalar.activation(k_buf[s][0:NOPE, grp(g)], k.ps[3 + g][0:NOPE, 0:TG],
                                                            ACT.Copy), (s, ("k", g)))
                        pe_s.wait(act, (s, "v"), it)
                        act_s.done(nc.scalar.activation(v_buf[s], k.ps[7][:, :].rearrange("p (t c) -> p t c", t=NQ),
                                                        ACT.Copy), (s, "v"))
                    for m, i in order:
                        if m == "S":
                            dve_s.wait(act, (s, ("max", i)), it)
                            act_s.done(nc.scalar.activation(prob[i % 2][:, 0:keys[i]], k.psw[i % 2][:, 0:keys[i]],
                                                            ACT.Exp, scale=scale, bias=k.nmax[:, i % 2:i % 2 + 1],
                                                            accum_out=k.rsum[:, i % 2:i % 2 + 1]), (s, ("exp", i)))
                        elif m == "T":
                            pe_s.wait(act, (s, ("T", i)), it)
                            act_s.done(nc.scalar.activation(probT[i % 2][:, 0:keys[i]], k.psw[2][:, 0:keys[i]],
                                                            ACT.Copy), (s, ("T", i)))
                        else:
                            pe_s.wait(act, (s, ("O", i)), it)
                            lo = VH * s if mla else 0
                            at = bass.ds(it, 1) if mla else bass.ds(it * 2 + s, 1)
                            out = (k.A[:, 0:4] if mla else k.C[:, 8:12])[lo:lo + wide, at, i * P:(i + 1) * P]
                            act_s.done(nc.scalar.activation(out, k.ps[6 + i % 2][lo:lo + wide, 0:P]
                                                            .rearrange("p (a t) -> p a t", a=1), ACT.Copy),
                                       (s, ("O", i)))

        @block.vector
        def _(dve):
            dve_s.prime(dve)
            with dve.Fori(0, heads // 2) as it:
                links[0] = 0

                def link(ins):
                    links[0] += 1
                    ins.then_inc(chain.sem, 1)
                    dve.wait_ge(chain.sem, it * per_chain + links[0])

                for s in S2:
                    q_s = (k.q_dec if mla else k.qm_dec)[0:depth, bass.ds(it * 2 + s, 1), :]
                    q_cols = q_buf[s][0:depth, SEQ:T].rearrange("p (a t) -> p a t", a=1)
                    if mla:
                        pe_s.wait(dve, (s, "swap"), it)
                        act_s.wait(dve, (s, ("q", NT - 1)), it)
                        for g in G:
                            nc.vector.tensor_tensor(k.sq[pe_rows, 0, grp(g)], k.ps[g][pe_rows, 0:TG], sin[:, grp(g)],
                                                    ALU.mult)
                        link(nc.vector.tensor_tensor(k.sq[pe_rows, 1, :], q_buf[s][pe_rows, :], cos, ALU.mult))
                        dve_s.done(nc.vector.tensor_tensor(q_buf[s][pe_rows, :], k.sq[pe_rows, 0, :],
                                                           k.sq[pe_rows, 1, :], ALU.add), (s, "q"))
                        dve_s.wait(dve, (s, "q"), it)
                        nc.vector.tensor_copy(q_s, q_cols)
                    else:
                        act_s.wait(dve, (s, ("q", NT - 1)), it)
                        dve_s.done(nc.vector.tensor_copy(q_s, q_cols), (s, "q"))
                    for i in range(nq):
                        nmax, rsum = k.nmax[:, i % 2:i % 2 + 1], k.rsum[:, i % 2:i % 2 + 1]
                        pe_s.wait(dve, (s, ("S", i)), it)
                        link(nc.vector.tensor_reduce(nmax, k.psw[i % 2][:, 0:keys[i]], AX.X, ALU.max))
                        dve_s.done(nc.vector.tensor_scalar(nmax, nmax, -scale, None, ALU.mult), (s, ("max", i)))
                        act_s.wait(dve, (s, ("exp", i)), it)
                        link(nc.vector.reciprocal(rsum, rsum))
                        dve_s.done(nc.vector.tensor_scalar(prob[i % 2][:, 0:keys[i]], prob[i % 2][:, 0:keys[i]],
                                                           rsum, None, ALU.mult), (s, ("prob", i)))
            assert 2 * links[0] == per_chain * 2


@stage
def decode_attention(k):
    nc = k.nc
    NS = 4
    ng = NPAGE // 4
    wuk = k.C[:, 0, 0:KT * 512].rearrange("p (f c) -> p f c", f=KT)
    wuv = k.C[:, 1, 0:KT * 512].rearrange("p (f c) -> p f c", f=KT)
    cache = k.Bc
    wukT = k.W[0:NOPE, 0, 0:MH_ * KVL].rearrange("p (h c) -> p h c", h=MH_)
    cT = [[k.W[:, 1 - z, 512 * f:512 * (f + 1)] for f in range(KT + 1)] for z in range(2)]
    turned = [k.ps[0:3], k.ps[3:6]]
    nT = k.W[:, 1, 1536:1540]
    misc = k.W[:, 1, 1600:2816]
    qlat = misc[:, 0:KT * 64].rearrange("p (f b h) -> p f b h", f=KT, b=DEC)
    qpe = misc[0:ROPE, 128:192].rearrange("p (h b) -> p h b", b=DEC)
    q_now = misc[:, 192:192 + 24].rearrange("p (f h) -> p f h", f=3)
    NK = PAST + 1
    sc = k.sq[0:MH_, :, :].rearrange("p a t -> p (a t)")[:, 0:NK]
    tops, ntop, total, rs = misc[0:MH_, 400:405], misc[0:MH_, 408:409], misc[0:MH_, 412:413], misc[0:MH_, 416:417]
    scT = misc[:, 256:256 + 136].rearrange("p (g h) -> p g h", h=MH_)
    ctx_rows = k.spare_w[0:MH_, 5632:5632 + DEC * KVL].rearrange("p (b c) -> p b c", b=DEC)
    ctx = misc[:, 448:448 + 128].rearrange("p (f h b) -> p f h b", f=KT, h=MH_)
    scores = k.ps[6][0:MH_, :]
    own_turned, own_score = k.ps[7][:, 0:4], k.ps[7][0:MH_, 4:5]
    weights_turned, context = k.ps[7][:, 8:144], k.ps[7][0:MH_, 256:512]

    order, act_order, dve_order = [], [], []
    for s in range(NS + 1):
        def of(slot, *steps):
            return [(slot, x) for x in steps] if 0 <= slot < NS else []
        order += of(s, ("T", 0)) + of(s - 1, "pT") + of(s, ("T", 1)) + of(s - 1, "ctx")
        order += of(s, ("S", 0), ("T", 2), ("S", 1), "nT", ("T", 3), ("S", 2), "nS", ("S", 3))
        act_order += of(s - 1, "exp") + of(s, ("T", 0)) + of(s - 1, "pT")
        act_order += of(s, ("T", 1), ("c", 0), ("T", 2), ("c", 1), "nT", ("T", 3), ("c", 2), ("c", 3))
        dve_order += of(s, "q", ("T", 0), ("T", 1)) + of(s - 1, "ctx")
        dve_order += of(s, ("m", 0), ("T", 2), ("m", 1), ("T", 3), ("m", 2), "own", ("m", 3), "top")

    setup = Count(k, "dec_setup_landed")
    set_pe = Steps(k, "dec_setup_products", [("wukT", j) for j in range(4)] + ["qlat"])
    set_act = Steps(k, "dec_setup_copies", [("wukT", j) for j in range(4)] + ["qlat"])
    qpe_moved = Count(k, "dec_qpe_moved")
    landed = [Count(k, f"dec_cache_landed{s}") for s in range(NS)]
    landed_sw = [Count(k, f"dec_cache_landed_sw{s}") for s in range(NS)]
    pe_s = Steps(k, "dec_products", order, primed=True)
    act_s = Steps(k, "dec_copies", act_order, primed=True)
    dve_s = Steps(k, "dec_softmax", dve_order, primed=True)
    chain = Count(k, "dec_chain")
    per_chain = 2 * NS
    pages_may_land = Count(k, "dec_pages_may_land")
    out_pe = Count(k, "dec_out_multiplied")
    ctx_turned, ctx_copied = Count(k, "dec_ctx_turned"), Count(k, "dec_ctx_copied")
    links = [0]
    n_phys = k.io["cache_mla"].shape[1]

    def wait_before(steps, eng, s, x, it):
        if s:
            steps.wait(eng, (s - 1, x), it)
        else:
            steps.wait(eng, (NS - 1, x), it, before=1)

    def pages(eng, it, s, part):
        b = it * NS + s
        pe_s.wait(eng, (s, "ctx"), it, before=1)
        eng.sem_inc(pages_may_land.sem, 1)
        with eng.Fori(0, NPAGE // 4) as pair:
            at = []
            for i in range(2):
                page = pair * 4 + (2 * i + part)
                at.append(eng.value_load(k.pages[0:1, bass.ds(b * NPAGE + page, 1)], min_val=0, max_val=n_phys - 1))
            for i in range(2):
                eng.dma_start(cache[:, s, bass.ds(pair * 4 + (2 * i + part), 1), :],
                              k.io["cache_mla"][0, bass.ds(at[i], 1)].rearrange("a p c -> p a c"))\
                    .then_inc((landed_sw if part else landed)[s].sem, 16)

    with nc.Block() as block:
        @block.sync
        def _(sp):
            sp.dma_start(wuk, k.io["mla_w_uk"][0].rearrange("(f p) h n -> p f (h n)", p=P)).then_inc(setup.sem, 16)
            sp.dma_start(wuv, k.io["mla_w_uv"][0].rearrange("(f p) h n -> p f (h n)", p=P)).then_inc(setup.sem, 16)
            sp.dma_start(qpe, k.q_dec[NOPE:QH, :, :]).then_inc(qpe_moved.sem, 16)
            with sp.Fori(0, DEC // NS) as it:
                for s in range(NS):
                    pages(sp, it, s, 0)
                    sp.dma_start(cache[0:1, s, NPAGE, :], k.io["rows_sample"][0, bass.ds(it * NS + s, 1), 0, :])\
                        .then_inc(landed[s].sem, 16)

        @block.gpsimd
        def _(pool):
            with pool.Fori(0, DEC // NS) as it:
                for s in range(NS):
                    pages(pool, it, s, 1)

        @block.tensor
        def _(pe):
            def settled():
                pe.sem_inc(k.settled.sem, 1)

            pe.wait_ge(setup.sem, 32)
            for j in range(4):
                for i in range(4):
                    h, f = (4 * j + i) // KT, (4 * j + i) % KT
                    ins = nc.tensor.transpose(k.ps[j][0:NOPE, i * P:(i + 1) * P], wuk[:, f, h * NOPE:(h + 1) * NOPE],
                                              k.ident[:, :])
                set_pe.done(ins, ("wukT", j))
            set_act.wait(pe, ("wukT", 3))
            for f in range(KT):
                for h in range(MH_):
                    ins = nc.tensor.matmul(k.ps[4][:, (f * MH_ + h) * DEC:(f * MH_ + h + 1) * DEC],
                                           wukT[:, h, f * P:(f + 1) * P], k.q_dec[0:NOPE, h, :], start=True, stop=True)
            set_pe.done(ins, "qlat")
            pe_s.prime(pe)
            set_act.wait(pe, "qlat")
            with pe.Fori(0, DEC // NS) as it:
                for s, x in order:
                    if x == ("T", 0):
                        pe.wait_ge(landed[s].sem, (it + 1) * (16 * (NPAGE // 2 + 1)))
                        pe.wait_ge(landed_sw[s].sem, (it + 1) * (8 * NPAGE))
                    if x[0] == "T":
                        g = x[1]
                        for done in (act_s, dve_s):
                            if g >= 2:
                                done.wait(pe, (s, ("T", g - 2)), it)
                            else:
                                wait_before(done, pe, s, ("T", g + 2), it)
                        for f in range(KT + 1):
                            n = P if f < KT else ROPE
                            for i in range(4):
                                ins = nc.tensor.transpose(turned[g % 2][f][0:n, i * P:(i + 1) * P],
                                                          cache[:, s, 4 * g + i, f * P:f * P + n], k.ident[:, :])
                    elif x[0] == "S":
                        g = x[1]
                        act_s.wait(pe, (s, ("T", g)), it)
                        dve_s.wait(pe, (s, ("T", g)), it)
                        if g:
                            act_s.wait(pe, (s, ("c", g - 1)), it)
                        else:
                            wait_before(act_s, pe, s, ("c", ng - 1), it)
                        settled()
                        for f in range(KT + 1):
                            n = P if f < KT else ROPE
                            ins = nc.tensor.matmul(scores, q_now[0:n, f, :], cT[g % 2][f][0:n, :],
                                                   start=(f == 0), stop=(f == KT))
                    elif x == "nT":
                        wait_before(dve_s, pe, s, "ctx", it)
                        settled()
                        for f in range(KT + 1):
                            n = P if f < KT else ROPE
                            ins = nc.tensor.transpose(own_turned[0:n, f:f + 1], cache[0:1, s, NPAGE, f * P:f * P + n],
                                                      k.ident[0:1, 0:1])
                    elif x == "nS":
                        act_s.wait(pe, (s, "nT"), it)
                        settled()
                        for f in range(KT + 1):
                            n = P if f < KT else ROPE
                            ins = nc.tensor.matmul(own_score, q_now[0:n, f, :], nT[0:n, f:f + 1],
                                                   start=(f == 0), stop=(f == KT))
                    elif x == "pT":
                        act_s.wait(pe, (s, "exp"), it)
                        settled()
                        for g in range(NPAGE):
                            nc.tensor.transpose(weights_turned[:, g * MH_:(g + 1) * MH_], sc[:, g * P:(g + 1) * P],
                                                k.ident[0:MH_, 0:MH_])
                        ins = nc.tensor.transpose(weights_turned[0:1, NPAGE * MH_:(NPAGE + 1) * MH_], sc[:, PAST:NK],
                                                  k.ident[0:MH_, 0:MH_])
                    else:
                        act_s.wait(pe, (s, "pT"), it)
                        settled()
                        for g in range(NPAGE):
                            nc.tensor.matmul(context, scT[:, g, :], cache[:, s, g, 0:KVL], start=(g == 0), stop=False)
                        ins = nc.tensor.matmul(context, scT[0:1, NPAGE, :], cache[0:1, s, NPAGE, 0:KVL],
                                               start=False, stop=True)
                    pe_s.done(ins, (s, x))
            dve_s.wait(pe, (NS - 1, "ctx"), DEC // NS - 1)
            for b in range(DEC):
                for f in range(KT):
                    at = (f * DEC + b) * MH_
                    ins = nc.tensor.transpose(k.ps[1][:, at:at + MH_], ctx_rows[:, b, f * P:(f + 1) * P],
                                              k.ident[0:MH_, 0:MH_])
            ins.then_inc(ctx_turned.sem, 1)
            pe.wait_ge(ctx_copied.sem, 1)
            for h in range(MH_):
                lo = (h % 2) * VH
                for f in range(KT):
                    ins = nc.tensor.matmul(k.ps[0][lo:lo + VH, (h // 2) * DEC:(h // 2 + 1) * DEC],
                                           wuv[:, f, h * VH:(h + 1) * VH], ctx[:, f, h, :],
                                           start=(f == 0), stop=(f == KT - 1))
            ins.then_inc(out_pe.sem, 1)

        def wait_turned(eng, s, g, it):
            pe_s.wait(eng, (s, ("T", g)), it)
            if g >= 2:
                pe_s.wait(eng, (s, ("S", g - 2)), it)
            else:
                wait_before(pe_s, eng, s, ("S", g + 2), it)

        @block.scalar
        def _(act):
            for j in range(4):
                set_pe.wait(act, ("wukT", j))
                dst = k.W[0:NOPE, 0, 512 * j:512 * (j + 1)]
                set_act.done(nc.scalar.activation(dst, k.ps[j][0:NOPE, :], ACT.Copy), ("wukT", j))
            set_pe.wait(act, "qlat")
            for f in range(KT):
                ins = nc.scalar.activation(qlat[:, f].rearrange("p b h -> p h b"),
                                           k.ps[4][:, f * 64:(f + 1) * 64].rearrange("p (h b) -> p h b", h=MH_), ACT.Copy)
            set_act.done(ins, "qlat")
            act_s.prime(act)
            with act.Fori(0, DEC // NS) as it:
                for s, x in act_order:
                    if x[0] == "T":
                        g = x[1]
                        wait_turned(act, s, g, it)
                        nc.scalar.activation(cT[g % 2][0], turned[g % 2][0][:, :], ACT.Copy)
                        ins = nc.scalar.activation(cT[g % 2][2][0:ROPE], turned[g % 2][2][0:ROPE, :], ACT.Copy)
                    elif x == "nT":
                        pe_s.wait(act, (s, "nT"), it)
                        nc.scalar.activation(nT[:, 0:2], own_turned[:, 0:2], ACT.Copy)
                        ins = nc.scalar.activation(nT[0:ROPE, 2:3], own_turned[0:ROPE, 2:3], ACT.Copy)
                    elif x[0] == "c":
                        g = x[1]
                        pe_s.wait(act, (s, ("S", g)), it)
                        ins = nc.scalar.activation(sc[:, g * 512:(g + 1) * 512], scores, ACT.Copy)
                    elif x == "pT":
                        pe_s.wait(act, (s, "pT"), it)
                        nc.scalar.activation(scT[:, 0:NPAGE, :], weights_turned[:, 0:NPAGE * MH_]
                                             .rearrange("p (g h) -> p g h", h=MH_), ACT.Copy)
                        ins = nc.scalar.activation(scT[0:1, NPAGE, :], weights_turned[0:1, NPAGE * MH_:], ACT.Copy)
                    else:
                        dve_s.wait(act, (s, "top"), it)
                        act_s.wait(act, (s, ("c", ng - 1)), it)
                        ins = nc.scalar.activation(sc, sc, ACT.Exp, scale=MLA_SCALE, bias=ntop, accum_out=total)
                    act_s.done(ins, (s, x))
            act.wait_ge(out_pe.sem, 1)
            nc.scalar.activation(k.A[:, 0:4, SEQ:T], k.ps[0][:, 0:4 * DEC].rearrange("p (j b) -> p j b", b=DEC), ACT.Copy)

        @block.vector
        def _(dve):
            set_act.wait(dve, "qlat")
            dve.wait_ge(qpe_moved.sem, 16)
            dve_s.prime(dve)
            with dve.Fori(0, DEC // NS) as it:
                links[0] = 0

                def link(ins):
                    links[0] += 1
                    ins.then_inc(chain.sem, 1)
                    dve.wait_ge(chain.sem, it * per_chain + links[0])

                for s, x in dve_order:
                    if x == "q":
                        wait_before(pe_s, dve, s, ("S", ng - 1), it)
                        nc.vector.tensor_copy(q_now[:, 0:KT, :].unsqueeze(2), qlat[:, :, bass.ds(it * NS + s, 1), :])
                        ins = nc.vector.tensor_copy(q_now[0:ROPE, KT, :].unsqueeze(2), qpe[:, :, bass.ds(it * NS + s, 1)])
                    elif x[0] == "T":
                        g = x[1]
                        wait_turned(dve, s, g, it)
                        ins = nc.vector.tensor_copy(cT[g % 2][1], turned[g % 2][1][:, :])
                    elif x[0] == "m":
                        g = x[1]
                        act_s.wait(dve, (s, ("c", g)), it)
                        ins = nc.vector.tensor_reduce(tops[:, g:g + 1], sc[:, g * 512:(g + 1) * 512], AX.X, ALU.max)
                    elif x == "own":
                        pe_s.wait(dve, (s, "nS"), it)
                        nc.vector.tensor_copy(tops[:, ng:ng + 1], own_score)
                        ins = nc.vector.tensor_copy(sc[:, PAST:NK], own_score)
                    elif x == "top":
                        dve_s.wait(dve, (s, ("m", ng - 1)), it)
                        link(nc.vector.tensor_reduce(ntop, tops, AX.X, ALU.max))
                        ins = nc.vector.tensor_scalar(ntop, ntop, -MLA_SCALE, None, ALU.mult)
                    else:
                        pe_s.wait(dve, (s, "ctx"), it)
                        link(nc.vector.reciprocal(rs, total))
                        ins = nc.vector.tensor_scalar(ctx_rows[:, bass.ds(it * NS + s, 1), :],
                                                      context.rearrange("p (a c) -> p a c", a=1), rs, None, ALU.mult)
                    dve_s.done(ins, (s, x))
            assert links[0] == per_chain
            dve.wait_ge(ctx_turned.sem, 1)
            nc.vector.tensor_copy(ctx, k.ps[1][:, 0:KT * DEC * MH_].rearrange("p (f b h) -> p f h b", f=KT, b=DEC))\
                .then_inc(ctx_copied.sem, 1)


@stage
def memory_keys(k, gain):
    nc = k.nc
    mT = k.C[:, 8:10, :].rearrange("p a t -> p (a t)")[:, 0:DT * MEM].rearrange("p (f t) -> p f t", f=DT)
    w = [k.C[:, 13 + 4 * m:17 + 4 * m, :].rearrange("p a t -> p (a t)")[:, 0:4096].rearrange("p (f c) -> p f c", f=DT)
         for m in range(2)]
    raw = [k.W[:, t, 0:D] for t in range(MTOK)]
    rows = [k.C[:, 10, 0:MTOK * 512].rearrange("p (t c) -> p t c", t=MTOK), k.memV]
    landed = Count(k, "mem_landed")
    wlanded = Count(k, "mem_w_landed")
    low_landed = Count(k, "mem_u_low_landed")
    pe_s = Steps(k, "mem_turned", range(4))
    act_s = Steps(k, "mem_copied", range(4))
    with nc.Block() as block:
        @block.sync
        def _(sp):
            for t in range(MTOK):
                sp.dma_start(raw[t], k.io["mem_prompt"][0, t * P:(t + 1) * P, :]).then_inc(landed.sem, 16)
            for m, src in enumerate((k.io["mem_w_k"], k.io["mem_w_v"])):
                sp.dma_start(w[m], src[0].rearrange("(f p) n -> p f n", p=P)).then_inc(wlanded.sem, 16)
        @block.gpsimd
        def _(pool):
            pool.dma_start(k.XR[:, 1], k.u_low).then_inc(low_landed.sem, 16)

        @block.tensor
        def _(pe):
            pe.wait_ge(landed.sem, 32)
            for x in range(4):
                t, q = divmod(x, 2)
                for f in range(4):
                    ins = nc.tensor.transpose(k.ps[x][:, f * P:(f + 1) * P], raw[t][:, (4 * q + f) * P:(4 * q + f + 1) * P],
                                              k.ident[:, :])
                pe_s.done(ins, x)

        @block.scalar
        def _(act):
            for x in range(4):
                t, q = divmod(x, 2)
                pe_s.wait(act, x)
                act_s.done(nc.scalar.activation(mT[:, 4 * q:4 * q + 4, t * P:(t + 1) * P],
                                                k.ps[x][:, :].rearrange("p (f t) -> p f t", f=4), ACT.Copy), x)
    rms_norm(k, "mem_norm", mT, DT, gain, cols=MEM)
    pe_s = Steps(k, "mem_multiplied", [(m, t) for m in range(2) for t in range(MTOK)] + ["kT0", "kT1"])
    act_s = Steps(k, "mem_rows", [(m, t) for m in range(2) for t in range(MTOK)] + ["kT0", "kT1"])
    stored = Count(k, "mem_stored")
    with nc.Block() as block:
        @block.tensor
        def _(pe):
            pe.wait_ge(wlanded.sem, 32)
            for m in range(2):
                for t in range(MTOK):
                    for f in range(DT):
                        ins = nc.tensor.matmul(k.ps[2 * m + t][:, :], mT[:, f, t * P:(t + 1) * P], w[m][:, f, :],
                                               start=(f == 0), stop=(f == DT - 1))
                    pe_s.done(ins, (m, t))
            act_s.wait(pe, (0, MTOK - 1))
            for t in range(MTOK):
                for h in range(MH):
                    ins = nc.tensor.transpose(k.ps[4 + t][:, h * P:(h + 1) * P], rows[0][:, t, h * P:(h + 1) * P],
                                              k.ident[:, :])
                pe_s.done(ins, f"kT{t}")

        @block.scalar
        def _(act):
            for m in range(2):
                for t in range(MTOK):
                    pe_s.wait(act, (m, t))
                    act_s.done(nc.scalar.activation(rows[m][:, t, :], k.ps[2 * m + t][:, :], ACT.Copy), (m, t))
            for t in range(MTOK):
                pe_s.wait(act, f"kT{t}")
                act_s.done(nc.scalar.activation(k.memT[:, :, t * P:(t + 1) * P],
                                                k.ps[4 + t][:, :].rearrange("p (h t) -> p h t", h=MH), ACT.Copy), f"kT{t}")

        @block.sync
        def _(sp):
            for m, out in enumerate((k.io["mem_k_prompt"], k.io["mem_v_prompt"])):
                for t in range(MTOK):
                    act_s.wait(sp, (m, t))
                    sp.dma_start(out[0, 0, t * P:(t + 1) * P].rearrange("p h c -> p (h c)"), rows[m][:, t, :])\
                        .then_inc(stored.sem, 16)
            sp.wait_ge(stored.sem, 64)

        @block.gpsimd
        def _(pool):
            pool.wait_ge(low_landed.sem, 16)


@stage
def decode_memory(k):
    nc = k.nc
    B8 = range(DEC)
    qrow = k.W[0:DEC, 0, 0:512]
    NS = 4
    keys = [k.spare_w[:, 3072 + D * i:3072 + D * (i + 1)].rearrange("p (t c) -> p t c", t=MTOK) for i in range(NS)]
    vals = [k.C[:, i, 0:D].rearrange("p (t c) -> p t c", t=MTOK) for i in (12, 13, 14, 15, 16, 18, 19, 20)]
    prod = k.C[:, 17, 0:1024].rearrange("p (t c) -> p t c", t=MTOK)
    sc = k.W[:, 1, 0:64].rearrange("p (b t h) -> p b t h", b=DEC, t=MTOK)
    mx, m1, dg = k.W[:, 1, 64:96], k.W[0:32, 1, 96:97], k.W[0:32, 1, 100:132]
    rs = k.W[:, 1, 132:164]
    pe_s = Steps(k, "dm_products", ["q"] + [("laid", b) for b in B8] + ["mT", "mB", "sum"] + [("o", b) for b in B8])
    act_s = Steps(k, "dm_copies", ["q", "exp"])
    dve_s = Steps(k, "dm_softmax", [("s", b) for b in B8] + ["mx", "diag", "sub", "rs", "out"])
    klanded = [Count(k, f"dm_keys_landed{s}") for s in range(NS)]
    vlanded = [Count(k, f"dm_values_landed{s}") for s in B8]
    chain = Count(k, "dm_chain")

    def rows(src, b):
        return src[0, b].rearrange("(t p) h c -> p t (h c)", p=P)

    with nc.Block() as block:
        @block.sync
        def _(sp):
            for b in range(NS):
                sp.dma_start(keys[b], rows(k.io["cache_mem_k"], b)).then_inc(klanded[b].sem, 16)
            for b in range(NS):
                for v in (2 * b, 2 * b + 1):
                    sp.dma_start(vals[v], rows(k.io["cache_mem_v"], v)).then_inc(vlanded[v].sem, 16)
                dve_s.wait(sp, ("s", b))
                sp.dma_start(keys[b], rows(k.io["cache_mem_k"], b + NS)).then_inc(klanded[b].sem, 16)

        @block.tensor
        def _(pe):
            for h in range(MH):
                ins = nc.tensor.transpose(k.ps[0][0:DEC, h * P:(h + 1) * P], k.qm_dec[:, h, :], k.ident[:, :])
            pe_s.done(ins, "q")
            act_s.wait(pe, "q")
            for b in B8:
                if b >= 2:
                    dve_s.wait(pe, ("s", b - 2))
                pe_s.done(nc.tensor.matmul(k.ps[6 + b % 2][:, :], k.ident[0:DEC, b:b + 1].to_broadcast([DEC, P]), qrow,
                                           start=True, stop=True), ("laid", b))
            dve_s.wait(pe, "mx")
            pe_s.done(nc.tensor.transpose(k.ps[1][0:32, 0:P], mx, k.ident[:, :]), "mT")
            dve_s.wait(pe, "diag")
            pe_s.done(nc.tensor.matmul(k.ps[2][:, 0:32], k.ones[0:32, :], dg, start=True, stop=True), "mB")
            act_s.wait(pe, "exp")
            pe_s.done(nc.tensor.matmul(k.ps[3][:, 0:64], k.ones[:, :], sc.rearrange("p b t h -> p (b t h)"),
                                       start=True, stop=True), "sum")
            for b in B8:
                pe.wait_ge(vlanded[b].sem, 16)
                for h in range(MH):
                    for t in range(MTOK):
                        ins = nc.tensor.matmul(k.ps[4][:, b * MH + h:b * MH + h + 1], vals[b][:, t, h * P:(h + 1) * P],
                                               sc[:, b, t, h:h + 1], start=(t == 0), stop=(t == MTOK - 1))
                pe_s.done(ins, ("o", b))

        @block.scalar
        def _(act):
            pe_s.wait(act, "q")
            act_s.done(nc.scalar.activation(qrow, k.ps[0][0:DEC, :], ACT.Copy), "q")
            dve_s.wait(act, "sub")
            act_s.done(nc.scalar.activation(sc, sc, ACT.Exp, scale=MEM_SCALE), "exp")

        @block.vector
        def _(dve):
            def link(ins):
                chain.up(ins)
                dve.wait_ge(chain.sem, chain.n)

            for b in B8:
                dve.wait_ge(klanded[b % NS].sem, 16 * (b // NS + 1))
                if b:
                    dve_s.wait(dve, ("s", b - 1))
                pe_s.wait(dve, ("laid", b))
                link(nc.vector.tensor_tensor(prod, keys[b % NS], k.ps[6 + b % 2].unsqueeze(1).to_broadcast([P, MTOK, 512]),
                                             ALU.mult))
                dve_s.done(nc.vector.tensor_reduce(sc[:, b], prod.rearrange("p t (h c) -> p t h c", h=MH), AX.X, ALU.add),
                           ("s", b))
            dve_s.wait(dve, ("s", DEC - 1))
            dve_s.done(nc.vector.tensor_tensor(mx.rearrange("p (b h) -> p b h", b=DEC), sc[:, :, 0], sc[:, :, 1], ALU.max),
                       "mx")
            pe_s.wait(dve, "mT")
            link(nc.vector.tensor_reduce(m1, k.ps[1][0:32, 0:P], AX.X, ALU.max))
            dve_s.done(nc.vector.tensor_scalar(dg, k.ident[0:32, 0:32], m1, None, ALU.mult), "diag")
            pe_s.wait(dve, "mB")
            top = k.ps[2][:, 0:32].rearrange("p (b h) -> p b h", b=DEC)
            dve_s.done(nc.vector.tensor_tensor(sc, sc, top.unsqueeze(2).to_broadcast([P, DEC, MTOK, MH]), ALU.subtract),
                       "sub")
            pe_s.wait(dve, "sum")
            sums = k.ps[3][:, 0:64].rearrange("p (b t h) -> p b h t", b=DEC, t=MTOK)
            link(nc.vector.tensor_reduce(rs.rearrange("p (b h) -> p b h", b=DEC), sums, AX.X, ALU.add))
            dve_s.done(nc.vector.reciprocal(rs, rs), "rs")
            dve_s.wait(dve, "rs")
            pe_s.wait(dve, ("o", DEC - 1))
            dve_s.done(nc.vector.tensor_tensor(k.C[:, 8:12, SEQ:T].rearrange("p h b -> p b h"),
                                               k.ps[4][:, 0:32].rearrange("p (b h) -> p b h", b=DEC),
                                               rs.rearrange("p (b h) -> p b h", b=DEC), ALU.mult), "out")


@stage
def merge(k):
    nc = k.nc
    branches = [(k.A[:, 4:8], k.io["rwkv_w_o"][0]), (k.A[:, 0:4], k.io["mla_w_o"][0]), (k.C[:, 8:12], k.io["mem_w_o"][0])]
    NB = len(branches)
    B3, G = range(NB), range(NT)
    raw = [k.C[:, 20, 0:D], k.C[:, 21, 0:D], k.sq[:, 1, 0:D]]
    parts = [k.gateR[:, b] for b in B3]
    w_o = [k.w_o[:, b, :].rearrange("p (f c) -> p f c", f=4) for b in B3]
    gate_landed = [Count(k, f"gate_w_landed{b}") for b in B3]
    out_landed = [Count(k, f"branch_w_landed{b}") for b in B3]
    steps = [(b, g) for b in B3 for g in G]
    work = [m for b in B3 for m in [("w", (b + 1) % NB)] + [(b, g) for g in G]]
    pe_s = Steps(k, "merge_products", steps, primed=True)
    act_s = Steps(k, "merge_functions", work, primed=True)
    dve_s = Steps(k, "merge_sums", [x for m in work for x in ([m] if m[0] == "w" or m[0] == 0 else [("mult",) + m, m])],
                  primed=True)
    first = Count(k, "merge_first_weights_high")
    first_split = Count(k, "merge_first_weights_split")
    gate_w = k.io["w_in"][0].rearrange("(f p) n -> p f n", p=P)

    def load_gate(sp, b, j):
        sp.dma_start(raw[b].rearrange("p (f c) -> p f c", f=DT), gate_w[:, :, bass.ds(COL_GATE + b * D + j * P, P)])\
            .then_inc(gate_landed[b].sem, 16)

    def load_out(sp, b, j):
        sp.dma_start(w_o[b], branches[b][1].rearrange("(f p) n -> p f n", p=P)[:, :, bass.ds(j * P, P)])\
            .then_inc(out_landed[b].sem, 16)

    def whole(eng, once):
        with eng.Fori(0, DT - 1) as j:
            once(j, False)
        once(DT - 1, True)

    with nc.Block() as block:
        @block.sync
        def _(sp):
            for b in B3:
                load_gate(sp, b, 0)
                load_out(sp, b, 0)
            sp.wait_ge(first_split.sem, 1)
            load_gate(sp, 0, 1)

            def refill(j, last):
                for b in B3:
                    if b:
                        dve_s.wait(sp, ("w", b), j)
                        sp.sem_inc(k.settled.sem, 1)
                        load_gate(sp, b, j + 1)
                    pe_s.wait(sp, (b, NT - 1), j)
                    sp.sem_inc(k.settled.sem, 1)
                    load_out(sp, b, j + 1)
                if not last:
                    dve_s.wait(sp, ("w", 0), j)
                    sp.sem_inc(k.settled.sem, 1)
                    load_gate(sp, 0, j + 2)

            with sp.Fori(0, DT - 2) as j:
                refill(j, False)
            refill(DT - 2, True)

        @block.tensor
        def _(pe):
            pe_s.prime(pe)
            pe.wait_ge(first_split.sem, 1)
            with pe.Fori(0, DT) as j:
                for b in B3:
                    dve_s.wait(pe, ("w", b), j, before=1 if b == 0 else 0)
                    pe.wait_ge(out_landed[b].sem, j * 16 + 16)
                    for g in G:
                        if b:
                            dve_s.wait(pe, (b - 1, g) if b == 1 else ("mult", b - 1, g), j)
                        else:
                            dve_s.wait(pe, ("mult", NB - 1, g), j, before=1)
                        for f in range(DT):
                            three(k, k.ps[2 * g][:, 0:TG], parts[b], slice(f * P, (f + 1) * P), f, g,
                                  f == 0, f == DT - 1)
                        for f in range(4):
                            ins = nc.tensor.matmul(k.ps[2 * g + 1][:, 0:TG], w_o[b][:, f], branches[b][0][:, f, grp(g)],
                                                   start=(f == 0), stop=(f == 3))
                        pe_s.done(ins, (b, g))

        @block.scalar
        def _(act):
            act.wait_ge(gate_landed[0].sem, 16)
            nc.scalar.activation(parts[0][:, 0, :], raw[0], ACT.Copy).then_inc(first.sem, 1)
            act_s.prime(act)

            def once(j, last):
                for m in work:
                    if m[0] == "w":
                        b = m[1]
                        if b:
                            act.wait_ge(gate_landed[b].sem, j * 16 + 16)
                            pe_s.wait(act, (b, NT - 1), j, before=1)
                        else:
                            if not last:
                                act.wait_ge(gate_landed[b].sem, j * 16 + 32)
                            pe_s.wait(act, (b, NT - 1), j)
                        n = 1 if last and b == 0 else D
                        act_s.done(nc.scalar.activation(parts[b][:, 0, 0:n], raw[b][:, 0:n], ACT.Copy), m)
                        continue
                    b, g = m
                    pe_s.wait(act, m, j)
                    if b:
                        dve_s.wait(act, (b - 1, g), j)
                    else:
                        dve_s.wait(act, (NB - 1, g), j, before=1)
                    act_s.done(nc.scalar.activation(k.t3[:, g, :], k.ps[2 * g][:, 0:TG], ACT.Sigmoid), m)

            whole(act, once)

        @block.vector
        def _(dve):
            dve.wait_ge(first.sem, 1)
            nc.vector.tensor_tensor(parts[0][:, 1, :], raw[0], parts[0][:, 0, :].bitcast(F32), ALU.subtract)\
                .then_inc(first_split.sem, 1)
            dve_s.prime(dve)

            def once(j, last):
                for m in work:
                    act_s.wait(dve, m, j)
                    if m[0] == "w":
                        b = m[1]
                        n = 1 if last and b == 0 else D
                        dve_s.done(nc.vector.tensor_tensor(parts[b][:, 1, 0:n], raw[b][:, 0:n],
                                                           parts[b][:, 0, 0:n].bitcast(F32), ALU.subtract), m)
                        continue
                    b, g = m
                    out = k.C[:, bass.ds(12 + j, 1), grp(g)]
                    t = k.t3[:, g, :].rearrange("p (a t) -> p a t", a=1)
                    x = k.ps[2 * g + 1][:, 0:TG].rearrange("p (a t) -> p a t", a=1)
                    if b == 0:
                        dve_s.done(nc.vector.tensor_tensor(out, t, x, ALU.mult), m)
                        continue
                    dve_s.done(nc.vector.tensor_tensor(t, t, x, ALU.mult), ("mult",) + m)
                    dve_s.wait(dve, ("mult",) + m, j)
                    dve_s.wait(dve, (b - 1, g), j)
                    dve_s.done(nc.vector.tensor_tensor(out, out, t, ALU.add), m)

            whole(dve, once)


def shape_constants():
    c = np.arange(P)
    s, t = c[:, None] % CH, np.arange(CH)[None, :]
    resets = np.broadcast_to((np.arange(SEQ) % CH != 0), (P, SEQ))
    strict, upto = s < t, s <= t
    masks = [(t % 2 == 0) & (s == t + 1), (s % 2 == 0) & (t == s + 1), s == t]
    masks += [(s // (2 * l) == t // (2 * l)) & (s % (2 * l) < l) & (t % (2 * l) >= l) for l in (2, 4, 8, 16, 32)]
    head_sel = np.concatenate([np.arange(RH)[None, :] == 2 * j + c[:, None] // RN for j in range(RT)], 1)
    head_sel_t = np.concatenate([(np.arange(RH)[:, None] == 2 * j + c[None, :] // RN) for j in range(RT)], 1)
    half = ROPE // 2
    freqs = np.float32(10000.0) ** (-np.arange(half, dtype=np.float32) / np.float32(half))
    pos = np.concatenate([np.arange(SEQ), np.full(DEC, PAST)]).astype(np.float32)
    ang = (freqs[:, None] * pos[None, :]).astype(np.float64)
    i = np.arange(ROPE)
    perm = i[:, None] == (i[None, :] + half) % ROPE
    cos = np.concatenate([np.cos(ang), np.cos(ang)])
    sin = np.concatenate([-np.sin(ang), np.sin(ang)])
    causal = np.where(c[None, :] <= c[:, None], 0.0, NEG)
    out = {"c_cos": cos, "c_sin": sin, "c_perm": perm, "c_causal": causal, "c_ident": np.eye(P), "c_headones": (c[:, None] // RN) == (c[None, :] // RN), "c_resets": resets,
           "c_gram": np.concatenate([strict, upto], 1), "c_head_sel": head_sel, "c_head_sel_t": head_sel_t, "c_masks": np.stack(masks, 1)}
    return {name: np.ascontiguousarray(a, dtype=np.float32) for name, a in out.items()}


VECTORS = [("ffn1_pre", DT), ("ffn1_post", DT), ("mix_pre", DT), ("mix_post", DT), ("ffn2_pre", DT),
           ("ffn2_post", DT), ("rwkv_mu", RPT), ("rwkv_w0", RT), ("rwkv_a0", RT), ("rwkv_k_k", RT), ("rwkv_k_a", RT),
           ("rwkv_r_k", RT), ("rwkv_lnx_g", RT), ("rwkv_lnx_b", RT), ("mla_q_norm", 6), ("mla_kv_norm", 2),
           ("mem_norm", DT)]


def build(nc, dram, outs):
    k = Kit()
    k.nc = nc
    k.semaphores = []
    k.io = {**dram, **outs}
    with ExitStack() as ctx:
        k.ctx = ctx

        def sb(name, shape):
            return ctx.enter_context(nc.sbuf_tensor(name, shape, F32))

        base = (nc.sbuf_base + 31) // 32 * 32
        sb("area", [P, (3 * DT + 4) * T + 18 * D + 8])

        def at(name, shape, first, dtype=F32):
            return nc.alloc_sbuf_tensor_at(name, shape, dtype, offset=base + 4 * first)

        k.A, k.B, k.C = at("A", [P, DT, T], 0), at("B", [P, DT, T], DT * T), at("C", [P, FT, T], 2 * DT * T)
        k.W = at("W", [P, 2, FT * P], (2 * DT + FT) * T)
        k.XR = at("XR", [P, 2, DT, T], DT * T, R32)
        k.hidR = at("hidR", [P, 2, 2, T], 3 * DT * T, R32)
        k.wR = at("wR", [P, 3, 2, 2 * D], (3 * DT + 4) * T, R32)
        k.praw, k.pR = at("praw", [P, 2, D], (2 * DT + FT) * T), at("pR", [P, 2, 2, D], (2 * DT + FT) * T + 2 * D, R32)
        k.gateR = at("gateR", [P, 3, 2, D], (2 * DT + FT) * T, R32)
        k.w_o = at("w_o", [P, 3, 4 * P], (2 * DT + FT) * T + 6 * D)
        k.spare_w = at("spare_w", [P, 15 * RT * P], (2 * DT + FT) * T)
        k.wraw = at("wraw", [P, 3, 2 * D], (3 * DT + 4) * T + 12 * D)
        k.rs, k.sq = sb("rs", [P, T]), sb("sq", [P, 2, T])
        k.t3 = k.sq[:, :, :].rearrange("p a t -> p (a t)")[:, 0:NT * TG].rearrange("p (g t) -> p g t", g=NT)
        k.t6 = k.sq[:, :, :].rearrange("p a t -> p (a t)").rearrange("p (g t) -> p g t", g=2 * NT)
        k.ident, k.ones, k.headones = sb("ident", [P, P]), sb("ones", [P, P]), sb("headones", [P, P])
        k.eps_col, k.lnx_eps, k.mu_now = sb("eps", [P, 1]), sb("lnx_eps", [P, 1]), sb("mu_now", [P, 1])
        k.vec = sb("vec", [P, sum(n for _, n in VECTORS)])
        k.gram = sb("gram", [P, 2 * CH])
        k.masks = sb("masks", [P, 8, CH])
        k.ST, k.st_rows = sb("ST", [P, RT, RN]), sb("st_rows", [P, RT, RN])
        k.chunk_decay, k.decay_now = sb("chunk_decay", [P, NCH, RT]), sb("decay_now", [P, 2, RT])
        k.rwflat = k.A[:, 4:8, :].rearrange("p a t -> p (a t)")
        k.rw = k.rwflat[:, 0:2 * 1792].rearrange("p (s c) -> p s c", s=2)
        k.rowbuf = k.W[:, 1, 1024:1024 + T + 1]
        k.gbuf = k.W[:, 1, 0:T]
        k.gram_mask = k.gram[:, :].unsqueeze(1).to_broadcast([P, RT, 2 * CH])

        def over_pairs(i):
            return k.masks[:, i, :].unsqueeze(1).to_broadcast([P, RT, CH])

        k.first_mask, k.first_mask_t, k.ident4 = over_pairs(0), over_pairs(1), over_pairs(2)
        k.level_mask = {l: over_pairs(3 + i) for i, l in enumerate((2, 4, 8, 16, 32))}
        psum = ctx.enter_context(nc.psum_tensor("banks", [P, 8, 512], F32))
        k.psum_flat = psum[:, :, :].rearrange("p b c -> p (b c)")
        k.head_sel, k.head_sel_t = sb("head_sel", [P, 2 * RT * RT]), sb("head_sel_t", [2 * RT, RT * P])
        k.rms_col = sb("rms_col", [P, 2 * (T // P + 1)])[:, :]
        k.ps = [psum[:, i, :] for i in range(8)]
        k.psw = [psum[:, 2 * i:2 * i + 2, :].rearrange("p b c -> p (b c)") for i in range(4)]
        k.h_spill = nc.dram_tensor("h_spill", [P, DT, T], F32).ap()
        k.t_scratch = nc.dram_tensor("t_scratch", [6, DEC, RD], F32).ap()
        k.o_scratch = nc.dram_tensor("o_scratch", [DEC, RD], F32).ap()

        k.perm, k.causal = sb("perm", [P, ROPE]), sb("causal", [P, P])
        k.nmax, k.rsum = sb("nmax", [P, 2]), sb("rsum", [P, 2])
        k.q_dec, k.qm_dec = sb("q_dec", [P, MH_, DEC]), sb("qm_dec", [P, MH, DEC])
        k.pages = ctx.enter_context(nc.sbuf_tensor("pages", [1, DEC * NPAGE], mybir.dt.int32))
        k.settled = Count(k, "products_may_start")
        k.u_low = nc.dram_tensor("u_low", [P, DT, T], F32).ap()
        k.memT = k.C[:, 12, 0:MH * MEM].rearrange("p (h t) -> p h t", h=MH)
        k.memV = k.C[:, 21, 0:MTOK * 512].rearrange("p (t c) -> p t c", t=MTOK)
        k.Bc = k.C[:, 2:22, :].rearrange("p a t -> p (a t)")[:, 0:4 * (NPAGE + 1) * CW]\
            .rearrange("p (s g c) -> p s g c", s=4, g=NPAGE + 1)
        k.const_loads = [(k.causal[:, :], k.io["c_causal"]), (k.pages[:, :], k.io["page_table"].rearrange("b g -> (b g)").unsqueeze(0)),
                         (k.headones[:, :], k.io["c_headones"]), (k.gram[:, :], k.io["c_gram"]),
                         (k.masks[:, :, :], k.io["c_masks"]), (k.head_sel[:, :], k.io["c_head_sel"]),
                         (k.head_sel_t[:, :], k.io["c_head_sel_t"])]
        at, v = 0, {}
        for name, n in VECTORS:
            v[name] = k.vec[:, at:at + n]
            src = dram[name][0]
            if name == "rwkv_r_k":
                src = src.rearrange("h n -> (h n)")
            k.const_loads.append((v[name], src.rearrange("(f p) -> p f", p=P)))
            at += n
        k.mu, k.w0, k.a0, k.k_k, k.k_a = (v["rwkv_" + x] for x in ("mu", "w0", "a0", "k_k", "k_a"))
        k.r_k, k.lnx_g, k.lnx_b = (v["rwkv_" + x] for x in ("r_k", "lnx_g", "lnx_b"))
        ms = Count(k, "memset")
        with nc.Block() as block:
            @block.gpsimd
            def _(pool):
                nc.gpsimd.memset(k.ones[:, :], 1.0).then_inc(ms.sem, 1)
                nc.gpsimd.memset(k.eps_col[:, :], RMS_EPS).then_inc(ms.sem, 1)
                nc.gpsimd.memset(k.lnx_eps[:, :], LNX_EPS).then_inc(ms.sem, 1)
        with nc.allow_non_contiguous_dma("per-feature vectors go across partitions"):
            load_x(k)
        ffn(k, "ffn1", v["ffn1_pre"], v["ffn1_post"], k.io["ffn1_gate"][0], k.io["ffn1_up"][0], k.io["ffn1_down"][0])
        rms_split(k, "mix_pre", v["mix_pre"], k.h_spill)
        rwkv_project(k)
        rwkv_vectors(k)
        rwkv_scan(k)
        rwkv_sample_step(k)
        rwkv_finish(k)
        project_split(k, "latents", k.io["w_in"][0], COL_Q, QT + KT, k.C[:, 8:16], fetch=k.u_low)
        latent_norms(k, k.C[:, 8:8 + QT], v["mla_q_norm"], k.C[:, 14:14 + KT], v["mla_kv_norm"])
        key_rope(k)
        prompt_attention(k, "mla", True)
        decode_attention(k)
        memory_keys(k, v["mem_norm"])
        prompt_attention(k, "mem", False)
        decode_memory(k)
        merge(k)
        split_tiles(k, "merged", k.C[:, 12:20])
        project_split(k, "mix_out", k.io["w_out"][0], 0, DT, k.A)
        rms_norm(k, "mix_post", k.A, DT, v["mix_post"], residual=k.B, to_src=True, fetch=k.h_spill)
        ffn(k, "ffn2", v["ffn2_pre"], v["ffn2_post"], k.io["ffn2_gate"][0], k.io["ffn2_up"][0], k.io["ffn2_down"][0])
        store_y(k, k.A)



_OUTS = [("y_prompt", (1, SEQ, D)), ("y_sample", (DEC, 1, D)),
         ("rows_prompt", (1, 1, SEQ, CW)), ("rows_sample", (1, DEC, 1, CW)),
         ("wkv_prompt", (1, 1, RH, RN, RN)), ("wkv_sample", (1, DEC, RH, RN, RN)),
         ("shift_prompt", (1, 1, RPROJ)), ("shift_sample", (1, DEC, RPROJ)),
         ("mem_k_prompt", (1, 1, MEM, MH, P)), ("mem_v_prompt", (1, 1, MEM, MH, P))]


def kernel(**inputs):
    import concourse.bacc as bacc
    from concourse.bass_utils import run_bass_kernel_spmd

    nc = bacc.Bacc("TRN2", target_bir_lowering=False, num_devices=1)
    arrays, dram = {}, {}
    for name, a in {**inputs, **shape_constants()}.items():
        a = np.ascontiguousarray(a)
        arrays[f"in_{name}"] = a
        dram[name] = nc.dram_tensor(f"in_{name}", a.shape, mybir.dt.from_np(a.dtype), kind="ExternalInput").ap()
    outs = {name: nc.dram_tensor(f"out_{name}", shape, F32, kind="ExternalOutput").ap() for name, shape in _OUTS}
    build(nc, dram, outs)
    r = run_bass_kernel_spmd(nc, [arrays], core_ids=[0])
    return tuple(r.results[0][f"out_{name}"] for name, _ in _OUTS)
```
